# Optimizing a Trainium2 kernel written in Bass

```python
import math
import jax
import jax.numpy as jnp
from jax import lax
import numpy as np

D_MODEL = 1024
BATCH = 1
SEQ = 1024
DEPTH = 1

HEAD_DIM = 64
BLOCK_Q = 128
NORM_EPS = 1e-6
NEG_INF = -1e30
ATTN_SCALE = HEAD_DIM ** -0.5

SWA_HEADS = 4
SWA_KV_HEADS = 2
SWA_GROUP = SWA_HEADS // SWA_KV_HEADS
SWA_WINDOW = 128
FOX_HEADS = 4
SB_HEADS = 4
DSA_HEADS = 4
IDX_HEADS = 4
IDX_DIM = 64
IDX_SCALE = IDX_DIM ** -0.5
DSA_TOPK_MAX = 256
T5_BUCKETS = 32
T5_MAX_DISTANCE = 128
T5_HEADS = SWA_HEADS + DSA_HEADS
N_BRANCHES = 4
BRANCH_WIDTH = 4 * HEAD_DIM
N_GROUPS = 4
EXPERTS_PER_GROUP = 8
N_EXPERTS = N_GROUPS * EXPERTS_PER_GROUP
EXPERT_FF = 512
TOP_K_IN_GROUP = 2
MOE_BLOCK = 128

IN_SPLITS = (
    SWA_HEADS * HEAD_DIM, SWA_KV_HEADS * HEAD_DIM, SWA_KV_HEADS * HEAD_DIM,
    FOX_HEADS * HEAD_DIM, FOX_HEADS * HEAD_DIM, FOX_HEADS * HEAD_DIM,
    FOX_HEADS,
    SB_HEADS * HEAD_DIM, SB_HEADS * HEAD_DIM, SB_HEADS * HEAD_DIM,
    DSA_HEADS * HEAD_DIM, HEAD_DIM, HEAD_DIM,
    IDX_HEADS * IDX_DIM, IDX_DIM, IDX_HEADS,
    N_BRANCHES * D_MODEL,
)
IN_COLS = sum(IN_SPLITS)

kernel_name = 'hybrid_gated_swa_fox_stickbreak_dsa_hmoe'

def rms_norm(t, g):
    tf = t.astype(jnp.float32)
    tf = tf * lax.rsqrt(jnp.mean(tf * tf, axis=-1, keepdims=True) + NORM_EPS)
    return (tf * g.astype(jnp.float32)).astype(t.dtype)

def t5_bucket(dist):
    n = jnp.maximum(dist, 0)
    max_exact = T5_BUCKETS // 2
    nf = jnp.maximum(n, 1).astype(jnp.float32)
    large = max_exact + (jnp.log(nf / max_exact) / math.log(T5_MAX_DISTANCE / max_exact)
                         * (T5_BUCKETS - max_exact)).astype(jnp.int32)
    large = jnp.minimum(large, T5_BUCKETS - 1)
    return jnp.where(n < max_exact, n, large)

def to_blocks(t):
    b, s = t.shape[:2]
    return jnp.moveaxis(t.reshape((b, s // BLOCK_Q, BLOCK_Q) + t.shape[2:]), 1, 0)

def from_blocks(o):
    nb, b = o.shape[:2]
    return jnp.moveaxis(o, 0, 1).reshape(b, nb * BLOCK_Q, -1)

def sliding_window_attention(q, k, v, sinks, bias_table):
    b, s_len = q.shape[:2]
    nb = s_len // BLOCK_Q
    qb = q.reshape(b, nb, BLOCK_Q, SWA_KV_HEADS, SWA_GROUP, HEAD_DIM)

    def band(t):
        tb = t.reshape(b, nb, BLOCK_Q, SWA_KV_HEADS, HEAD_DIM)
        prev = jnp.concatenate([jnp.zeros_like(tb[:, :1]), tb[:, :-1]], axis=1)
        return jnp.concatenate([prev, tb], axis=2)

    kw, vw = band(k), band(v)
    s = jnp.einsum('bnqkgd,bnskd->bnkgqs', qb, kw).astype(jnp.float32) * ATTN_SCALE
    qi = jnp.arange(BLOCK_Q)[:, None]
    kj = jnp.arange(2 * BLOCK_Q)[None, :]
    dist = BLOCK_Q + qi - kj
    bias = bias_table[t5_bucket(dist)].astype(jnp.float32)
    bias = jnp.transpose(bias, (2, 0, 1)).reshape(SWA_KV_HEADS, SWA_GROUP, BLOCK_Q, 2 * BLOCK_Q)
    kpos = (jnp.arange(nb)[:, None, None] - 1) * BLOCK_Q + kj[None]
    valid = (dist >= 0) & (dist < SWA_WINDOW) & (kpos >= 0)
    s = jnp.where(valid[None, :, None, None], s + bias, NEG_INF)
    sink = sinks.astype(jnp.float32).reshape(1, 1, SWA_KV_HEADS, SWA_GROUP, 1, 1)
    m = jnp.maximum(jnp.max(s, axis=-1, keepdims=True), sink)
    p = jnp.exp(s - m)
    denom = jnp.sum(p, axis=-1, keepdims=True) + jnp.exp(sink - m)
    p = (p / denom).astype(v.dtype)
    o = jnp.einsum('bnkgqs,bnskd->bnqkgd', p, vw)
    return o.reshape(b, s_len, SWA_HEADS * HEAD_DIM)

def forgetting_attention(q, k, v, log_f):
    s_len = q.shape[1]
    c = jnp.cumsum(log_f, axis=1)
    c_keys = jnp.swapaxes(c, 1, 2)
    kpos = jnp.arange(s_len)

    def block(args):
        i, qi, ci = args
        s = jnp.einsum('bqhd,bshd->bhqs', qi, k).astype(jnp.float32) * ATTN_SCALE
        s = s + jnp.swapaxes(ci, 1, 2)[..., None] - c_keys[:, :, None, :]
        qpos = i * BLOCK_Q + jnp.arange(BLOCK_Q)
        s = jnp.where(kpos[None, :] <= qpos[:, None], s, NEG_INF)
        p = jax.nn.softmax(s, axis=-1).astype(v.dtype)
        return jnp.einsum('bhqs,bshd->bqhd', p, v)

    nb = s_len // BLOCK_Q
    out = lax.map(block, (jnp.arange(nb), to_blocks(q), to_blocks(c)))
    return from_blocks(out)

def stick_breaking_attention(q, k, v):
    s_len = q.shape[1]
    kpos = jnp.arange(s_len)

    def block(args):
        i, qi = args
        z = jnp.einsum('bqhd,bshd->bhqs', qi, k).astype(jnp.float32) * ATTN_SCALE
        qpos = i * BLOCK_Q + jnp.arange(BLOCK_Q)
        strict = kpos[None, :] < qpos[:, None]
        log_beta = jax.nn.log_sigmoid(z)
        log_keep = jnp.where(strict, jax.nn.log_sigmoid(-z), 0.0)
        later = lax.cumsum(log_keep, axis=3, reverse=True) - log_keep
        a = jnp.where(strict, jnp.exp(log_beta + later), 0.0).astype(v.dtype)
        return jnp.einsum('bhqs,bshd->bqhd', a, v)

    nb = s_len // BLOCK_Q
    out = lax.map(block, (jnp.arange(nb), to_blocks(q)))
    return from_blocks(out)

def dsa_attention(q, k, v, q_idx, k_idx, w_idx, bias_table):
    s_len = k.shape[1]
    top_k = min(DSA_TOPK_MAX, s_len // 4)
    kpos = jnp.arange(s_len)
    gather = jax.vmap(lambda t, idx: t[idx])

    def block(args):
        i, qi, qii, wi = args
        qpos = i * BLOCK_Q + jnp.arange(BLOCK_Q)
        idx_logits = jnp.einsum('bqhd,bsd->bqhs', qii, k_idx).astype(jnp.float32) * IDX_SCALE
        score = jnp.einsum('bqh,bqhs->bqs', wi.astype(jnp.float32) * IDX_HEADS ** -0.5,
                           jax.nn.relu(idx_logits))
        score = jnp.where(kpos[None, None, :] <= qpos[None, :, None], score, -jnp.inf)
        _, idx = lax.top_k(score, top_k)
        kg = gather(k, idx)
        vg = gather(v, idx)
        s = jnp.einsum('bqhd,bqkd->bhqk', qi, kg).astype(jnp.float32) * ATTN_SCALE
        dist = qpos[None, :, None] - idx
        bias = jnp.moveaxis(bias_table[t5_bucket(dist)], -1, 1).astype(jnp.float32)
        s = jnp.where((dist >= 0)[:, None], s + bias, NEG_INF)
        p = jax.nn.softmax(s, axis=-1).astype(v.dtype)
        return jnp.einsum('bhqk,bqkd->bqhd', p, vg)

    nb = s_len // BLOCK_Q
    out = lax.map(block, (jnp.arange(nb), to_blocks(q), to_blocks(q_idx), to_blocks(w_idx)))
    return from_blocks(out)

def hierarchical_moe(h, w_rg, b_rg, w_re, b_re, w_up, w_down):
    n_tok, d = h.shape
    g_logits = (h @ w_rg).astype(jnp.float32) + b_rg.astype(jnp.float32)
    g_prob = jax.nn.softmax(g_logits, axis=-1)
    grp = jnp.argmax(g_logits, axis=-1).astype(jnp.int32)
    p_grp = jnp.take_along_axis(g_prob, grp[:, None], axis=1)[:, 0]
    e_logits = ((h @ w_re).astype(jnp.float32) + b_re.astype(jnp.float32)).reshape(
        n_tok, N_GROUPS, EXPERTS_PER_GROUP)
    e_in = jnp.take_along_axis(e_logits, grp[:, None, None], axis=1)[:, 0]
    top_p, top_e = lax.top_k(jax.nn.softmax(e_in, axis=-1), TOP_K_IN_GROUP)
    gate = p_grp[:, None] * top_p / jnp.sum(top_p, axis=-1, keepdims=True)
    expert = grp[:, None] * EXPERTS_PER_GROUP + top_e.astype(jnp.int32)

    n_assign = n_tok * TOP_K_IN_GROUP
    flat_e = expert.reshape(-1)
    flat_tok = jnp.repeat(jnp.arange(n_tok, dtype=jnp.int32), TOP_K_IN_GROUP)
    flat_gate = gate.reshape(-1)
    order = jnp.argsort(flat_e)
    se, stok, sgate = flat_e[order], flat_tok[order], flat_gate[order]
    counts = jnp.bincount(flat_e, length=N_EXPERTS).astype(jnp.int32)
    start = jnp.cumsum(counts) - counts
    padded = (counts + MOE_BLOCK - 1) // MOE_BLOCK * MOE_BLOCK
    pend = jnp.cumsum(padded)
    pstart = pend - padded
    pos = pstart[se] + (jnp.arange(n_assign, dtype=jnp.int32) - start[se])
    n_blocks = -(-n_assign // MOE_BLOCK) + N_EXPERTS
    slot_tok = jnp.full((n_blocks * MOE_BLOCK,), n_tok, jnp.int32).at[pos].set(stok)
    blk_expert = jnp.clip(jnp.searchsorted(pend, jnp.arange(n_blocks) * MOE_BLOCK, side='right'),
                          0, N_EXPERTS - 1)
    h_pad = jnp.concatenate([h, jnp.zeros((1, d), h.dtype)], axis=0)
    xb = h_pad[slot_tok].reshape(n_blocks, MOE_BLOCK, d)

    def expert_block(args):
        xi, e = args
        gu = xi @ w_up[e]
        g, u = jnp.split(gu, 2, axis=-1)
        return (jax.nn.silu(g) * u) @ w_down[e]

    yb = lax.map(expert_block, (xb, blk_expert)).reshape(n_blocks * MOE_BLOCK, d)
    contrib = yb[pos] * sgate[:, None].astype(yb.dtype)
    return jnp.zeros((n_tok, d), h.dtype).at[stok].add(contrib)

def setup_inputs(seed: int = 0) -> dict:
    key = jax.random.key(seed)
    ks = jax.random.split(key, 17)
    f32 = jnp.float32
    nrm = lambda k, shp: jax.random.normal(k, shp, f32)
    return {
        'x': nrm(ks[0], (BATCH, SEQ, D_MODEL)),
        'norm_mix_g': 1.0 + 0.02 * nrm(ks[1], (DEPTH, D_MODEL)),
        'w_in': nrm(ks[2], (DEPTH, D_MODEL, IN_COLS)) * D_MODEL ** -0.5,
        'forget_bias': jax.random.uniform(ks[3], (DEPTH, FOX_HEADS), f32, 1.0, 5.0),
        'attn_sinks': 0.5 * nrm(ks[4], (DEPTH, SWA_HEADS)),
        'qk_gain': 1.0 + 0.02 * nrm(ks[5], (DEPTH, 3, 2, HEAD_DIM)),
        'w_branch': nrm(ks[6], (DEPTH, N_BRANCHES, BRANCH_WIDTH, D_MODEL)) * BRANCH_WIDTH ** -0.5,
        'w_out': nrm(ks[7], (DEPTH, D_MODEL, D_MODEL)) * D_MODEL ** -0.5,
        't5_table': 0.5 * nrm(ks[8], (T5_BUCKETS, T5_HEADS)),
        'norm_ffn_g': 1.0 + 0.02 * nrm(ks[9], (DEPTH, D_MODEL)),
        'w_router_group': nrm(ks[10], (DEPTH, D_MODEL, N_GROUPS)) * D_MODEL ** -0.5,
        'b_router_group': 0.01 * nrm(ks[11], (DEPTH, N_GROUPS)),
        'w_router_expert': nrm(ks[12], (DEPTH, D_MODEL, N_EXPERTS)) * D_MODEL ** -0.5,
        'b_router_expert': 0.01 * nrm(ks[13], (DEPTH, N_EXPERTS)),
        'w_expert_up': nrm(ks[14], (DEPTH, N_EXPERTS, D_MODEL, 2 * EXPERT_FF)) * D_MODEL ** -0.5,
        'w_expert_down': nrm(ks[15], (DEPTH, N_EXPERTS, EXPERT_FF, D_MODEL)) * EXPERT_FF ** -0.5,
    }

def reference(x, norm_mix_g, w_in, forget_bias, attn_sinks, qk_gain, w_branch, w_out, t5_table,
              norm_ffn_g, w_router_group, b_router_group, w_router_expert, b_router_expert,
              w_expert_up, w_expert_down):
    b, s = x.shape[:2]
    offsets = np.cumsum(IN_SPLITS)[:-1].tolist()
    for layer in range(DEPTH):
        h = rms_norm(x, norm_mix_g[layer])
        proj = h @ w_in[layer]
        (a_q, a_k, a_v, f_q, f_k, f_v, f_gate, s_q, s_k, s_v,
         d_q, d_k, d_v, i_q, i_k, i_w, gate_cols) = jnp.split(proj, offsets, axis=-1)
        gq = qk_gain[layer]
        heads = lambda t, n: t.reshape(b, s, n, HEAD_DIM)

        o_swa = sliding_window_attention(
            rms_norm(heads(a_q, SWA_HEADS), gq[0, 0]),
            rms_norm(heads(a_k, SWA_KV_HEADS), gq[0, 1]),
            heads(a_v, SWA_KV_HEADS),
            attn_sinks[layer], t5_table[:, :SWA_HEADS])

        log_f = jax.nn.log_sigmoid(f_gate.astype(jnp.float32) + forget_bias[layer].astype(jnp.float32))
        o_fox = forgetting_attention(
            rms_norm(heads(f_q, FOX_HEADS), gq[1, 0]),
            rms_norm(heads(f_k, FOX_HEADS), gq[1, 1]),
            heads(f_v, FOX_HEADS), log_f)

        o_sb = stick_breaking_attention(heads(s_q, SB_HEADS), heads(s_k, SB_HEADS), heads(s_v, SB_HEADS))

        o_dsa = dsa_attention(
            rms_norm(heads(d_q, DSA_HEADS), gq[2, 0]),
            rms_norm(d_k, gq[2, 1]), d_v,
            i_q.reshape(b, s, IDX_HEADS, IDX_DIM), i_k, i_w,
            t5_table[:, SWA_HEADS:])

        g_swa, g_fox, g_sb, g_dsa = jnp.split(jax.nn.sigmoid(gate_cols), N_BRANCHES, axis=-1)
        wb = w_branch[layer]
        merged = (g_swa * (o_swa @ wb[0]) + g_fox * (o_fox @ wb[1])
                  + g_sb * (o_sb @ wb[2]) + g_dsa * (o_dsa @ wb[3]))
        x = x + merged @ w_out[layer]

        h2 = rms_norm(x, norm_ffn_g[layer]).reshape(b * s, D_MODEL)
        y = hierarchical_moe(h2, w_router_group[layer], b_router_group[layer],
                             w_router_expert[layer], b_router_expert[layer],
                             w_expert_up[layer], w_expert_down[layer])
        x = x + y.reshape(b, s, D_MODEL)
    return x


_drawn_inputs = setup_inputs


def setup_inputs(seed=0):
    import zlib

    import numpy as np

    out = dict(_drawn_inputs(seed))
    spreads = {}
    factors = {'attn_sinks': 200.0, 'qk_gain': 4.021, 'b_router_group': 10.437, 'b_router_expert': 3.004}
    for name, (base, spread) in spreads.items():
        noise = np.random.default_rng([zlib.crc32(name.encode()), seed]).standard_normal(out[name].shape)
        drawn = base * np.exp(spread * noise) if base else spread * noise
        out[name] = jnp.asarray(drawn.astype(out[name].dtype))
    for name, factor in factors.items():
        out[name] = (out[name] * factor).astype(out[name].dtype)
    return out
```

```python
from contextlib import ExitStack, contextmanager

import numpy as np

import concourse.bass as bass
from concourse import mybir

ALU = mybir.AluOpType
ACT = mybir.ActivationFunctionType
AX = mybir.AxisListType.X
F32 = mybir.dt.float32
BF16 = mybir.dt.bfloat16
I32 = mybir.dt.int32
U32 = mybir.dt.uint32

P = 128
D = 1024
T = 1024
KC = D // P
NT = T // P
HALF = 512
HD = 64
NH = 4
EPS = 1e-6
NEG = -1e30
SCALE = HD ** -0.5

SWA_Q, SWA_K, FOX_Q, FOX_K, DSA_Q, DSA_K = 0, 2, 3, 5, 7, 9
IDX_Q, IDX_K, SB_Q, SB_K = 10, 12, 13, 15
NORMED = 10
QK_CHUNKS = 17
FG_ROW = IDX_K * P + HD
V_FOX, V_SB, V_SWA, V_DSA, V_IW, V_COLS = 0, 256, 512, 640, 704, 708

TOPK = 256
BAND = 2 * P
T5_LINE = 384
N_BUCKETS = 32
PICKED = -3e38
UNSEEN = -2e38

GROUPS, PER_GROUP, EXPERTS, FF = 4, 8, 32, 512
MAX_BLOCKS = 48
SLOTS = (MAX_BLOCKS + 2) * P
ZERO_BLOCKS = 10


@contextmanager
def semaphores(nc):
    made = []

    def sem(name):
        made.append(nc.alloc_semaphore(name))
        return made[-1]

    yield sem
    nc.clear_and_free_semaphores(made)
    nc.all_engine_barrier()


def near_blocks(i):
    return list(range(max(0, i - 1), i + 1))


def all_blocks(i):
    return list(range(i + 1))


def build(nc, a, out):
    def dram(name, shape, dt=F32):
        return nc.dram_tensor(name, shape, dt, kind="Internal").ap()

    qkT = dram("qkT", (QK_CHUNKS * P, T))
    vtok = dram("vtok", (T, V_COLS))
    gatesT = dram("gatesT", (4 * KC, P, T))
    crow = dram("crow", (2, NH, T))
    t5line = dram("t5line", (2, NH, T5_LINE))
    t5tile = dram("t5tile", (2 * NH, P, BAND))
    otok = dram("otok", (T, D))
    mergedT = dram("mergedT", (KC, P, T))
    x2d = dram("x2d", (T, D))
    h2d = dram("h2d", (T, D))
    slot_tok = dram("slot_tok", (SLOTS, 1), I32)
    ybd = dram("ybd", (SLOTS, D))

    with ExitStack() as top:
        ident = top.enter_context(nc.sbuf_tensor("ident", [P, P], F32))
        lg = top.enter_context(nc.sbuf_tensor("lg", [P, NT, 36], F32))
        with ExitStack() as mem:
            selm = mem.enter_context(nc.sbuf_tensor("selm", [P, sum(range(3, NT + 1)), P], F32))
            sel_at = {i: sum(range(3, i + 1)) for i in range(2, NT)}
            with ExitStack() as early:
                hT = early.enter_context(nc.sbuf_tensor("hT", [P, KC, T], F32))
                iw = early.enter_context(nc.sbuf_tensor("iw", [P, NT, NH], F32))
                norm_input(nc, a, ident, hT)
                project(nc, a, hT, iw, qkT, vtok)
                select_and_gate(nc, a, hT, iw, selm, sel_at, qkT, gatesT, crow, t5line, t5tile, ybd)
            attention(nc, a, ident, selm, sel_at, qkT, vtok, crow, t5tile, otok)
        merge(nc, a, ident, otok, gatesT, mergedT)
        output_and_router(nc, a, ident, lg, mergedT, x2d, h2d)
        pos = [top.enter_context(nc.sbuf_tensor(f"pos{k}", [P, NT], I32)) for k in range(2)]
        gate = [top.enter_context(nc.sbuf_tensor(f"gate{k}", [P, NT], F32)) for k in range(2)]
        eblk = top.enter_context(nc.sbuf_tensor("eblk", [1, MAX_BLOCKS + 2], I32))
        pairs = top.enter_context(nc.sbuf_tensor("pairs", [1, 1], I32))
        route(nc, a, lg, pos, gate, eblk, pairs, slot_tok)
        experts(nc, a, ident, eblk, pairs, slot_tok, h2d, ybd)
        combine(nc, pos, gate, x2d, ybd, out)


def norm_input(nc, a, ident, hT):
    x = a["x"]
    with ExitStack() as c:
        sb = lambda n, s, d=F32: c.enter_context(nc.sbuf_tensor(n, s, d))
        sem = c.enter_context(semaphores(nc))
        xt = [sb(f"ni_x{s}", [P, D]) for s in range(2)]
        xn = [sb(f"ni_xn{s}", [P, D]) for s in range(2)]
        junk = [sb(f"ni_junk{s}", [P, D]) for s in range(2)]
        ss = [sb(f"ni_ss{s}", [P, 1]) for s in range(2)]
        sd = [sb(f"ni_sd{s}", [P, 1]) for s in range(2)]
        rs = [sb(f"ni_rs{s}", [P, 1]) for s in range(2)]
        g = sb("ni_g", [P, KC])
        pt = [c.enter_context(nc.psum_tensor(f"ni_pt{s}", [P, KC, P], F32)) for s in range(2)]
        x_loaded = [sem(f"ni_x_loaded{s}") for s in range(2)]
        g_loaded = sem("ni_g_loaded")
        ident_done = sem("ni_ident_done")
        squared = sem("ni_squared")
        rooted = sem("ni_rooted")
        inverted = sem("ni_inverted")
        scaled = sem("ni_scaled")
        turned = sem("ni_turned")
        stored = sem("ni_stored")
        block = c.enter_context(nc.Block())

        @block.sync
        def _(sp):
            sp.dma_start(g[:, :], a["norm_mix_g"]).then_inc(g_loaded, 16)
            with sp.Fori(0, NT // 2) as it:
                for s in range(2):
                    sp.wait_ge(scaled, it * 2 + s + 1)
                    sp.dma_start(xt[s][:, :], x[bass.ds(it * 2 + s, 1)].rearrange("a p f -> p (a f)")).then_inc(x_loaded[s], 16)

        @block.gpsimd
        def _(pool):
            pool.memset(ident[:, :], 0.0).then_inc(ident_done, 1)
            pool.wait_ge(ident_done, 1)
            pool.affine_select(out=ident[:, :], in_=ident[:, :], compare_op=ALU.not_equal, fill=1.0, base=0,
                               pattern=[[-1, P]], channel_multiplier=1).then_inc(ident_done, 1)

        @block.scalar
        def _(act):
            with act.Fori(0, NT // 2) as it:
                for s in range(2):
                    act.wait_ge(x_loaded[s], it * 16 + 16)
                    act.activation(junk[s][:, :], xt[s][:, :], ACT.Square, accum_out=ss[s][:, :]).then_inc(squared, 1)
                    act.wait_ge(squared, it * 2 + s + 1)
                    act.activation(sd[s][:, :], ss[s][:, :], ACT.Sqrt, scale=1.0 / D, bias=EPS).then_inc(rooted, 1)

        @block.vector
        def _(dve):
            dve.sem_inc(scaled, 2)
            dve.sem_inc(stored, 2)
            dve.wait_ge(g_loaded, 16)
            with dve.Fori(0, NT // 2) as it:
                for s in range(2):
                    dve.wait_ge(rooted, it * 2 + s + 1)
                    dve.reciprocal(rs[s][:, :], sd[s][:, :]).then_inc(inverted, 1)
                    dve.wait_ge(inverted, it * 2 + s + 1)
                    dve.wait_ge(turned, it * 2 + s + 1)
                    dve.tensor_scalar(xn[s][:, :], xt[s][:, :], rs[s][:, 0:1], None, ALU.mult).then_inc(scaled, 1)
                for s in range(2):
                    dve.wait_ge(turned, it * 2 + s + 1 + 2)
                    dve.tensor_tensor(hT[:, :, bass.ds((it * 2 + s) * P, P)], pt[s][:, :, :],
                                      g[:, :].unsqueeze(2).to_broadcast([P, KC, P]), ALU.mult).then_inc(stored, 1)

        @block.tensor
        def _(pe):
            pe.sem_inc(turned, 2)
            pe.wait_ge(ident_done, 2)
            with pe.Fori(0, NT // 2) as it:
                for s in range(2):
                    pe.wait_ge(scaled, it * 2 + s + 1 + 2)
                    pe.wait_ge(stored, it * 2 + s + 1)
                    for k in range(KC):
                        last = pe.transpose(pt[s][:, k, :], xn[s][:, k * P:(k + 1) * P], ident[:, :])
                    last.then_inc(turned, 1)


def project(nc, a, hT, iw, qkT, vtok):
    qk_out = qkT.rearrange("(c p) t -> c p t", p=P)
    with ExitStack() as c:
        sb = lambda n, s, d=F32: c.enter_context(nc.sbuf_tensor(n, s, d))
        sem = c.enter_context(semaphores(nc))
        wt = [sb(f"pj_w{s}", [P, KC, P]) for s in range(2)]
        wv = sb("pj_wv", [P, KC, V_COLS])
        gc = sb("pj_gain", [P, QK_CHUNKS])
        heads_mean = sb("pj_heads_mean", [P, P])
        sq = [sb(f"pj_sq{h}", [P, HALF]) for h in range(2)]
        sd = [sb(f"pj_sd{h}", [P, HALF]) for h in range(2)]
        rc = [sb(f"pj_rc{h}", [P, HALF]) for h in range(2)]
        ob = [sb(f"pj_out{s}", [P, T]) for s in range(2)]
        ps = [[c.enter_context(nc.psum_tensor(f"pj_ps{s}{h}", [P, HALF], F32)) for h in range(2)] for s in range(2)]
        nps = [c.enter_context(nc.psum_tensor(f"pj_nps{h}", [P, HALF], F32)) for h in range(2)]
        w_loaded = [sem(f"pj_w_loaded{s}") for s in range(2)]
        v_loaded = sem("pj_v_loaded")
        gain_loaded = sem("pj_gain_loaded")
        gain_done = sem("pj_gain_done")
        mean_done = sem("pj_mean_done")
        multiplied = sem("pj_multiplied")
        squared = sem("pj_squared")
        averaged = sem("pj_averaged")
        rooted = sem("pj_rooted")
        inverted = sem("pj_inverted")
        evacuated = sem("pj_evacuated")
        iw_done = sem("pj_iw_done")
        stored = [sem(f"pj_stored{s}") for s in range(2)]
        block = c.enter_context(nc.Block())

        @block.sync
        def _(sp):
            def load(k, s):
                sp.dma_start(wt[s][:, :, :], a["w_qk"][k].rearrange("a p k n -> p (a k) n")).then_inc(w_loaded[s], 16)

            def store(k, s):
                sp.wait_ge(evacuated, k * 2 + 2 + 4)
                sp.dma_start(qk_out[bass.ds(k, 1)].rearrange("a p t -> p (a t)"), ob[s][:, :]).then_inc(stored[s], 16)

            load(bass.ds(0, 1), 0)
            load(bass.ds(1, 1), 1)
            sp.dma_start(gc[:, :], a["gain_cols"]).then_inc(gain_loaded, 16)
            sp.dma_start(wv[:, :, :], a["w_v"]).then_inc(v_loaded, 16)
            with sp.Fori(0, 7) as it:
                for s in range(2):
                    sp.wait_ge(multiplied, it * 4 + s * 2 + 2)
                    load(bass.ds(it * 2 + s + 2, 1), s)
                    store(it * 2 + s, s)
            sp.wait_ge(multiplied, 14 * 2 + 2)
            load(bass.ds(16, 1), 0)
            for k in (14, 15, 16):
                store(k, k % 2)
            for t in range(NT):
                k = QK_CHUNKS + t
                sp.wait_ge(evacuated, k * 2 + 2 + 4)
                sp.dma_start(vtok[t * P:(t + 1) * P, :], ob[k % 2][:, 0:V_COLS]).then_inc(stored[k % 2], 16)
            sp.wait_ge(stored[0], 16 * 14)
            sp.wait_ge(stored[1], 16 * 13)

        @block.gpsimd
        def _(pool):
            pool.memset(heads_mean[:, :], 0.0).then_inc(mean_done, 1)
            pool.wait_ge(mean_done, 1)
            for q in range(2):
                pool.memset(heads_mean[q * HD:(q + 1) * HD, q * HD:(q + 1) * HD], 1.0 / HD).then_inc(mean_done, 1)

        @block.scalar
        def _(act):
            with act.Fori(0, NORMED // 2) as it:
                for s in range(2):
                    for h in range(2):
                        act.wait_ge(multiplied, it * 4 + s * 2 + h + 1)
                        act.wait_ge(averaged, it * 4 + s * 2 + h + 1)
                        act.activation(sq[h][:, :], ps[s][h][:, :], ACT.Square).then_inc(squared, 1)
                    for h in range(2):
                        act.wait_ge(averaged, it * 4 + s * 2 + h + 1 + 2)
                        act.wait_ge(inverted, it * 4 + s * 2 + h + 1)
                        act.activation(sd[h][:, :], nps[h][:, :], ACT.Sqrt, bias=EPS).then_inc(rooted, 1)

        @block.vector
        def _(dve):
            dve.sem_inc(evacuated, 4)
            dve.sem_inc(inverted, 2)
            dve.sem_inc(stored[0], 16)
            dve.sem_inc(stored[1], 16)
            dve.wait_ge(gain_loaded, 16)
            for n, q in enumerate((SWA_Q, FOX_Q, DSA_Q)):
                dve.tensor_scalar(gc[:, q:q + 2], gc[:, q:q + 2], SCALE, None, ALU.mult).then_inc(gain_done, 1)
            dve.wait_ge(gain_done, 3)
            with dve.Fori(0, NORMED // 2) as it:
                for s in range(2):
                    for h in range(2):
                        dve.wait_ge(rooted, it * 4 + s * 2 + h + 1 + 2)
                        dve.reciprocal(rc[h][:, :], sd[h][:, :]).then_inc(inverted, 1)
                        dve.wait_ge(inverted, it * 4 + s * 2 + h + 1 + 2)
                        if h == 0:
                            dve.wait_ge(stored[s], it * 16 + 16)
                        dve.scalar_tensor_tensor(ob[s][:, h * HALF:(h + 1) * HALF], ps[s][h][:, :],
                                                 gc[:, bass.ds(it * 2 + s, 1)], rc[h][:, :],
                                                 ALU.mult, ALU.mult).then_inc(evacuated, 1)

            def plain(k, s, waited):
                for h in range(2):
                    dve.wait_ge(multiplied, k * 2 + h + 1)
                    if h == 0:
                        dve.wait_ge(stored[s], waited)
                    dve.tensor_scalar(ob[s][:, h * HALF:(h + 1) * HALF], ps[s][h][:, :], gc[:, bass.ds(k, 1)], None,
                                      ALU.mult).then_inc(evacuated, 1)

            with dve.Fori(NORMED // 2, 8) as it:
                for s in range(2):
                    plain(it * 2 + s, s, it * 16 + 16)
            plain(16, 0, 8 * 16 + 16)
            for t in range(NT):
                k = QK_CHUNKS + t
                s = k % 2
                dve.wait_ge(multiplied, k * 2 + 1)
                dve.wait_ge(stored[s], 16 * (k // 2) + 16)
                if t >= 2:
                    dve.wait_ge(iw_done, t - 1)
                dve.tensor_copy(ob[s][:, 0:HALF], ps[s][0][:, :]).then_inc(evacuated, 1)
                dve.wait_ge(multiplied, k * 2 + 2)
                dve.tensor_copy(ob[s][:, HALF:V_COLS], ps[s][1][:, 0:V_COLS - HALF]).then_inc(evacuated, 1)
                dve.wait_ge(evacuated, k * 2 + 2 + 4)
                dve.tensor_scalar(iw[:, t, :], ob[s][:, V_IW:V_COLS], NH ** -0.5, None, ALU.mult).then_inc(iw_done, 1)

        @block.tensor
        def _(pe):
            pe.sem_inc(averaged, 2)
            pe.sem_inc(rooted, 2)
            pe.wait_ge(mean_done, 3)

            def chunk(k, s, loaded):
                pe.wait_ge(w_loaded[s], loaded)
                for h in range(2):
                    pe.wait_ge(evacuated, k * 2 + h + 1)
                    for q in range(KC):
                        last = pe.matmul(ps[s][h][:, :], wt[s][:, q, :], hT[:, q, h * HALF:(h + 1) * HALF],
                                         start=(q == 0), stop=(q == KC - 1))
                    last.then_inc(multiplied, 1)

            with pe.Fori(0, NORMED // 2) as it:
                for s in range(2):
                    chunk(it * 2 + s, s, it * 16 + 16)
                    for h in range(2):
                        pe.wait_ge(squared, it * 4 + s * 2 + h + 1)
                        pe.wait_ge(rooted, it * 4 + s * 2 + h + 1)
                        pe.matmul(nps[h][:, :], heads_mean[:, :], sq[h][:, :], start=True, stop=True).then_inc(averaged, 1)
            with pe.Fori(NORMED // 2, 8) as it:
                for s in range(2):
                    chunk(it * 2 + s, s, it * 16 + 16)
            chunk(16, 0, 8 * 16 + 16)
            pe.wait_ge(v_loaded, 16)
            for t in range(NT):
                k = QK_CHUNKS + t
                for h, (f, n) in enumerate(((0, HALF), (HALF, V_COLS - HALF))):
                    pe.wait_ge(evacuated, k * 2 + h + 1)
                    for q in range(KC):
                        last = pe.matmul(ps[k % 2][h][:, 0:n], hT[:, q, t * P:(t + 1) * P], wv[:, q, f:f + n],
                                         start=(q == 0), stop=(q == KC - 1))
                    last.then_inc(multiplied, 1)


def select_and_gate(nc, a, hT, iw, selm, sel_at, qkT, gatesT, crow, t5line, t5tile, ybd):
    with ExitStack() as c:
        sb = lambda n, s, d=F32: c.enter_context(nc.sbuf_tensor(n, s, d))
        sem = c.enter_context(semaphores(nc))
        iq = sb("sg_iq", [P, 2, T])
        ik = sb("sg_ik", [P, T])
        fg = sb("sg_fg", [NH, T])
        fa = sb("sg_fa", [NH, T])
        fb = sb("sg_fb", [NH, T])
        fbias = sb("sg_fbias", [NH, 1])
        onehot = sb("sg_onehot", [N_BUCKETS + 1, 2, T5_LINE])
        table = sb("sg_table", [N_BUCKETS + 1, 2 * NH])
        lines = sb("sg_lines", [NH, 2, T5_LINE])
        flip = sb("sg_flip", [P, P])
        reversed_ = sb("sg_reversed", [P, 2 * NH, BAND])
        t5 = sb("sg_t5", [P, 2 * NH, BAND])
        later = sb("sg_later", [P, P])
        r = [sb(f"sg_r{s}", [P, T]) for s in range(2)]
        top8 = sb("sg_top8", [P, 8])
        zeros = sb("sg_zeros", [P, D])
        wt = [sb(f"sg_w{s}", [P, KC, P]) for s in range(2)]
        go = [sb(f"sg_go{s}", [P, T]) for s in range(2)]
        si = [c.enter_context(nc.psum_tensor(f"sg_si{s}", [P, T], F32)) for s in range(2)]
        gp = [[c.enter_context(nc.psum_tensor(f"sg_gp{s}{h}", [P, HALF], F32)) for h in range(2)] for s in range(2)]
        zeros_made = sem("sg_zeros_made")
        zeros_stored = sem("sg_zeros_stored")
        small_loaded = sem("sg_small_loaded")
        idx_loaded = sem("sg_idx_loaded")
        table_set = sem("sg_table_set")
        lines_made = sem("sg_lines_made")
        lines_out = sem("sg_lines_out")
        lines_stored = sem("sg_lines_stored")
        reversed_loaded = sem("sg_reversed_loaded")
        tiles_flipped = sem("sg_tiles_flipped")
        tiles_made = sem("sg_tiles_made")
        tiles_stored = sem("sg_tiles_stored")
        f_act = sem("sg_f_act")
        f_dve = sem("sg_f_dve")
        c_stored = sem("sg_c_stored")
        later_done = sem("sg_later_done")
        scored = sem("sg_scored")
        rectified = sem("sg_rectified")
        added = sem("sg_added")
        picked = sem("sg_picked")
        wait_carrier = sem("sg_wait_carrier")
        w_loaded = [sem(f"sg_w_loaded{s}") for s in range(2)]
        gated = sem("sg_gated")
        sigmoided = sem("sg_sigmoided")
        g_stored = [sem(f"sg_g_stored{s}") for s in range(2)]
        units = [(i, h) for i in range(2, NT) for h in range(NH)]
        block = c.enter_context(nc.Block())

        @block.sync
        def _(sp):
            qk = qkT.rearrange("(c p) t -> p c t", p=P)
            sp.dma_start(iq[:, :, :], qk[:, IDX_Q:IDX_Q + 2, :]).then_inc(idx_loaded, 16)
            for half in range(2):
                sp.dma_start(ik[half * HD:(half + 1) * HD, :], qkT[IDX_K * P:IDX_K * P + HD, :]).then_inc(idx_loaded, 16)
            sp.dma_start(fg[:, :], qkT[FG_ROW:FG_ROW + NH, :]).then_inc(small_loaded, 16)
            sp.dma_start(fbias[:, :], a["forget_bias"]).then_inc(small_loaded, 16)
            sp.dma_start(onehot[:, :, :], a["t5_onehot"]).then_inc(small_loaded, 16)
            sp.dma_start(table[0:N_BUCKETS, :], a["t5_table"]).then_inc(small_loaded, 16)

            def load(k, s):
                sp.dma_start(wt[s][:, :, :], a["w_gate"][k].rearrange("a p k n -> p (a k) n")).then_inc(w_loaded[s], 16)

            def store(k, s):
                sp.wait_ge(sigmoided, k * 2 + 2 + 4)
                sp.dma_start(gatesT[bass.ds(k, 1)].rearrange("a p t -> p (a t)"), go[s][:, :]).then_inc(g_stored[s], 16)

            load(bass.ds(0, 1), 0)
            load(bass.ds(1, 1), 1)
            n = 4 * KC
            with sp.Fori(0, n // 2 - 1) as it:
                for s in range(2):
                    sp.wait_ge(gated, it * 4 + s * 2 + 2)
                    load(bass.ds(it * 2 + s + 2, 1), s)
                    store(it * 2 + s, s)
            for s in range(2):
                store(n - 2 + s, s)
                sp.wait_ge(g_stored[s], 16 + 16 * n // 2)

        @block.gpsimd
        def _(pool):
            pool.memset(later[:, :], 0.0).then_inc(later_done, 1)
            pool.memset(flip[:, :], 0.0).then_inc(later_done, 1)
            pool.wait_ge(later_done, 2)
            pool.affine_select(out=flip[:, :], in_=flip[:, :], compare_op=ALU.not_equal, fill=1.0, base=1 - P,
                               pattern=[[1, P]], channel_multiplier=1).then_inc(later_done, 1)
            pool.affine_select(out=later[:, :], in_=later[:, :], compare_op=ALU.is_ge, fill=UNSEEN, base=0,
                               pattern=[[-1, P]], channel_multiplier=1).then_inc(later_done, 1)
            pool.memset(zeros[:, :], 0.0).then_inc(zeros_made, 1)
            pool.wait_ge(zeros_made, 1)
            for b in range(0, SLOTS // P, ZERO_BLOCKS):
                pool.dma_start(ybd.rearrange("(b p) d -> p b d", p=P)[:, b:b + ZERO_BLOCKS, :],
                               zeros[:, :].unsqueeze(1).to_broadcast([P, ZERO_BLOCKS, D])).then_inc(zeros_stored, 16)
            pool.wait_ge(lines_out, 2)
            pool.dma_start(t5line.rearrange("v h n -> h v n"), lines[:, :, :]).then_inc(lines_stored, 16)
            pool.wait_ge(lines_stored, 16)
            for v in range(2):
                for h in range(NH):
                    src = bass.AP(t5line.tensor, (v * NH + h) * T5_LINE, [[1, P], [1, BAND]])
                    pool.dma_start(reversed_[:, v * NH + h, :], src).then_inc(reversed_loaded, 16)
            pool.wait_ge(tiles_made, 4)
            pool.dma_start(t5tile.rearrange("h p k -> p h k"), t5[:, :, :]).then_inc(tiles_stored, 16)
            pool.wait_ge(f_dve, 4)
            pool.dma_start(crow[0], fg[:, :]).then_inc(c_stored, 16)
            pool.dma_start(crow[1], fa[:, :]).then_inc(c_stored, 16)
            pool.wait_ge(c_stored, 32)
            pool.wait_ge(tiles_stored, 16)
            pool.wait_ge(zeros_stored, 16 * (SLOTS // P // ZERO_BLOCKS))

        @block.scalar
        def _(act):
            act.wait_ge(small_loaded, 64)
            act.activation(fa[:, :], fg[:, :], ACT.Abs, bias=fbias[:, 0:1]).then_inc(f_act, 1)
            act.wait_ge(f_act, 1)
            act.activation(fa[:, :], fa[:, :], ACT.Exp, scale=-1.0).then_inc(f_act, 1)
            act.wait_ge(f_act, 2)
            act.activation(fa[:, :], fa[:, :], ACT.Ln, bias=1.0).then_inc(f_act, 1)
            for u, (i, h) in enumerate(units):
                W = (i + 1) * P
                act.wait_ge(scored, u + 1)
                if u >= 2:
                    act.wait_ge(added, u - 1)
                act.activation(r[u % 2][:, 0:W], si[u % 2][:, 0:W], ACT.Relu).then_inc(rectified, 1)
            with act.Fori(0, 2 * KC) as it:
                for s in range(2):
                    for h in range(2):
                        act.wait_ge(gated, it * 4 + s * 2 + h + 1)
                        if h == 0:
                            act.wait_ge(g_stored[s], it * 16 + 16)
                        act.activation(go[s][:, h * HALF:(h + 1) * HALF], gp[s][h][:, :], ACT.Sigmoid).then_inc(sigmoided, 1)

        @block.vector
        def _(dve):
            dve.memset(table[N_BUCKETS:N_BUCKETS + 1, :], NEG).then_inc(table_set, 1)
            dve.sem_inc(g_stored[0], 16)
            dve.sem_inc(g_stored[1], 16)
            dve.sem_inc(sigmoided, 4)
            dve.wait_ge(small_loaded, 64)
            dve.tensor_scalar(fb[:, :], fg[:, :], fbias[:, 0:1], 0.0, ALU.add, ALU.min).then_inc(f_dve, 1)
            dve.wait_ge(f_act, 3)
            dve.wait_ge(f_dve, 1)
            dve.tensor_tensor(fb[:, :], fb[:, :], fa[:, :], ALU.subtract).then_inc(f_dve, 1)
            dve.wait_ge(f_dve, 2)
            dve.tensor_tensor_scan(fg[:, :], fb[:, :], fb[:, :], 0.0, ALU.add, ALU.min).then_inc(f_dve, 1)
            dve.wait_ge(f_dve, 3)
            dve.tensor_scalar(fa[:, :], fg[:, :], -1.0, None, ALU.mult).then_inc(f_dve, 1)
            for v in range(2):
                dve.wait_ge(lines_made, v + 1)
                dve.tensor_copy(lines[:, v, :], gp[0][v][0:NH, 0:T5_LINE]).then_inc(lines_out, 1)
            dve.wait_ge(later_done, 4)
            for u, (i, h) in enumerate(units):
                W = (i + 1) * P
                acc = selm[:, sel_at[i]:sel_at[i] + i + 1, :].rearrange("p b k -> p (b k)")
                dve.wait_ge(rectified, u + 1)
                if h == 0:
                    dve.tensor_scalar(acc, r[u % 2][:, 0:W], iw[:, i, h:h + 1], None, ALU.mult).then_inc(added, 1)
                else:
                    dve.wait_ge(added, u)
                    dve.scalar_tensor_tensor(acc, r[u % 2][:, 0:W], iw[:, i, h:h + 1], acc, ALU.mult,
                                             ALU.add).then_inc(added, 1)
            for j in range(4):
                dve.wait_ge(tiles_flipped, j + 1)
                dve.tensor_copy(t5[:, 2 * j:2 * j + 2, :].rearrange("p h k -> p (h k)"),
                                gp[j // 2][j % 2][:, :]).then_inc(tiles_made, 1)
            n = 0
            for i in range(2, NT):
                b0 = sel_at[i]
                acc = selm[:, b0:b0 + i + 1, :].rearrange("p b k -> p (b k)")
                dve.wait_ge(added, len(units))
                dve.tensor_tensor(selm[:, b0 + i, :], selm[:, b0 + i, :], later[:, :], ALU.add).then_inc(picked, 1)
                n += 1
                dve.wait_ge(picked, n)
                with dve.Fori(0, TOPK // 8) as rnd:
                    dve.max(top8[:, :], acc).then_inc(picked, 1)
                    dve.wait_ge(picked, rnd * 2 + n + 1)
                    dve.sem_inc(wait_carrier, 1)
                    dve.match_replace(acc, top8[:, :], acc, PICKED).then_inc(picked, 1)
                    dve.wait_ge(picked, rnd * 2 + n + 2)
                    dve.sem_inc(wait_carrier, 1)
                n += 2 * (TOPK // 8)
                dve.tensor_scalar(acc, acc, (PICKED + UNSEEN) / 2, NEG, ALU.is_gt, ALU.mult).then_inc(picked, 1)
                n += 1
                dve.wait_ge(picked, n)

        @block.tensor
        def _(pe):
            pe.wait_ge(small_loaded, 64)
            pe.wait_ge(table_set, 1)
            for v in range(2):
                pe.matmul(gp[0][v][0:NH, 0:T5_LINE], table[:, v * NH:(v + 1) * NH], onehot[:, v, :],
                          start=True, stop=True).then_inc(lines_made, 1)
            pe.wait_ge(idx_loaded, 48)
            for u, (i, h) in enumerate(units):
                if u >= 2:
                    pe.wait_ge(rectified, u - 1)
                rows = slice(HD * (h % 2), HD * (h % 2) + HD)
                for f in range(0, (i + 1) * P, HALF):
                    n = min(HALF, (i + 1) * P - f)
                    last = pe.matmul(si[u % 2][:, f:f + n], iq[rows, h // 2, i * P:(i + 1) * P], ik[rows, f:f + n],
                                     start=True, stop=True)
                last.then_inc(scored, 1)
            pe.wait_ge(later_done, 4)
            pe.wait_ge(reversed_loaded, 16 * 2 * NH)
            for j in range(4):
                pe.matmul(gp[j // 2][j % 2][:, :], flip[:, :], reversed_[:, 2 * j:2 * j + 2, :].rearrange("p h k -> p (h k)"),
                          start=True, stop=True).then_inc(tiles_flipped, 1)
            pe.wait_ge(tiles_made, 4)
            with pe.Fori(0, 2 * KC) as it:
                for s in range(2):
                    pe.wait_ge(w_loaded[s], it * 16 + 16)
                    for h in range(2):
                        pe.wait_ge(sigmoided, it * 4 + s * 2 + h + 1)
                        for q in range(KC):
                            last = pe.matmul(gp[s][h][:, :], wt[s][:, q, :], hT[:, q, h * HALF:(h + 1) * HALF],
                                             start=(q == 0), stop=(q == KC - 1))
                        last.then_inc(gated, 1)


class Chain:

    def __init__(self, sem, per_iteration):
        self.sem, self.per, self.n = sem, per_iteration, 0

    def did(self, instruction):
        instruction.then_inc(self.sem, 1)
        self.n += 1

    def wait(self, engine, it):
        engine.wait_ge(self.sem, it * self.per + self.n)


def attention(nc, a, ident, selm, sel_at, qkT, vtok, crow, t5tile, otok):
    with ExitStack() as c:
        sb = lambda n, s, d=F32: c.enter_context(nc.sbuf_tensor(n, s, d))
        sem = c.enter_context(semaphores(nc))
        m = dict(
            q=[sb(f"at_q{s}", [HD + 2, T]) for s in range(2)],
            k=[sb(f"at_k{s}", [HD + 2, T]) for s in range(2)],
            v=[sb(f"at_v{s}", [P, NT, HD]) for s in range(2)],
            t5=[sb(f"at_t5{s}", [P, BAND]) for s in range(2)],
            hc=[sb(f"at_hc{s}", [P, 1]) for s in range(2)],
            hcn=[sb(f"at_hcn{s}", [P, 1]) for s in range(2)],
            x=[sb(f"at_x{s}", [P, T]) for s in range(2)],
            t=[sb(f"at_t{s}", [P, T]) for s in range(2)],
            sp=sb("at_sp", [P, T]),
            pT=[sb(f"at_pT{s}", [P, NT, P]) for s in range(2)],
            o=[sb(f"at_o{s}", [P, NT, HD]) for s in range(2)],
            negmax=[sb(f"at_negmax{s}", [P, 1]) for s in range(4)],
            rawmax=[sb(f"at_rawmax{s}", [P, 1]) for s in range(2)],
            den=[sb(f"at_den{s}", [P, 1]) for s in range(4)],
            sinkp=[sb(f"at_sinkp{s}", [P, 1]) for s in range(4)],
            rden=[sb(f"at_rden{s}", [P, 1]) for s in range(2)],
            identb=sb("at_identb", [P, P], BF16),
            causal=sb("at_causal", [P, P], BF16),
            strict=sb("at_strict", [P, P], BF16),
            s_ps=[c.enter_context(nc.psum_tensor(f"at_sps{s}", [P, T], F32)) for s in range(2)],
            t_ps=[c.enter_context(nc.psum_tensor(f"at_tps{s}", [P, 4, P], F32)) for s in range(2)],
            o_ps=[c.enter_context(nc.psum_tensor(f"at_ops{s}", [P, HALF], F32)) for s in range(2)],
        )
        masks_done = sem("at_masks_done")
        with nc.Block() as block:
            @block.gpsimd
            def _(pool):
                pool.memset(m["identb"][:, :], 0.0).then_inc(masks_done, 1)
                pool.memset(m["causal"][:, :], 0.0).then_inc(masks_done, 1)
                pool.memset(m["strict"][:, :], 0.0).then_inc(masks_done, 1)
                pool.wait_ge(masks_done, 3)
                pool.affine_select(out=m["identb"][:, :], in_=m["identb"][:, :], compare_op=ALU.not_equal, fill=1.0,
                                   base=0, pattern=[[-1, P]], channel_multiplier=1).then_inc(masks_done, 1)
                pool.affine_select(out=m["causal"][:, :], in_=m["causal"][:, :], compare_op=ALU.is_ge, fill=NEG,
                                   base=0, pattern=[[-1, P]], channel_multiplier=1).then_inc(masks_done, 1)
                pool.affine_select(out=m["strict"][:, :], in_=m["strict"][:, :], compare_op=ALU.is_gt, fill=NEG,
                                   base=0, pattern=[[-1, P]], channel_multiplier=1).then_inc(masks_done, 1)
                pool.wait_ge(masks_done, 6)

        for kind in ("fox", "sb", "dsa", "swa"):
            mixer(nc, a, kind, m, ident, selm, sel_at, qkT, vtok, crow, t5tile, otok)


def mixer(nc, a, kind, m, ident, selm, sel_at, qkT, vtok, crow, t5tile, otok):
    units = [(i, s) for i in range(NT) for s in range(2)]
    N = len(units)
    keys = near_blocks if kind == "swa" else all_blocks
    groups, first_group = [], []
    for u, (i, s) in enumerate(units):
        first_group.append(len(groups))
        ks = keys(i)
        groups += [(u, g, min(4, len(ks) - g)) for g in range(0, len(ks), 4)]
    first_group.append(len(groups))
    NG = len(groups)
    act_turns = kind in ("dsa", "swa")
    q_row = {"fox": FOX_Q, "sb": SB_Q, "dsa": DSA_Q, "swa": SWA_Q}[kind] * P
    k_row = {"fox": FOX_K, "sb": SB_K, "dsa": DSA_K, "swa": SWA_K}[kind] * P
    v_col = {"fox": V_FOX, "sb": V_SB, "dsa": V_DSA, "swa": V_SWA}[kind]
    branch = {"swa": 0, "fox": 1, "sb": 2, "dsa": 3}[kind]
    kv_of = lambda h: {"dsa": 0, "swa": h // 2}.get(kind, h)
    rows = HD + 2 if kind == "fox" else HD
    n_loads = {"fox": 6, "sb": 2, "dsa": 4, "swa": 4}[kind]
    x, t = m["x"], m["t"]

    with ExitStack() as c:
        new = c.enter_context(semaphores(nc))
        sem = lambda n: new(f"{kind}_{n}")
        qk_loaded = [sem(f"qk_loaded{s}") for s in range(2)]
        v_loaded = [sem(f"v_loaded{s}") for s in range(2)]
        logits = sem("logits")
        soft = sem("soft")
        shaped = sem("shaped")
        weighed = sem("weighed")
        turned = sem("turned")
        copied = sem("copied")
        summed = sem("summed")
        finished = sem("finished")
        stored = [sem(f"stored{s}") for s in range(2)]
        dve_chain = sem("dve_chain")
        act_chain = sem("act_chain")
        block = c.enter_context(nc.Block())

        def group_end(u):
            return first_group[u + 1]

        def copy_turned(engine, it, u):
            for g in range(first_group[u], first_group[u + 1]):
                _, b, n = groups[g]
                engine.wait_ge(turned, it * NG + g + 1 + lead)
                if b == 0:
                    engine.wait_ge(summed, it * N + u + 1)
                src, dst = m["t_ps"][g % 2][:, 0:n, :], m["pT"][u % 2][:, b:b + n, :]
                if act_turns:
                    ins = engine.activation(dst, src, ACT.Copy)
                else:
                    ins = engine.tensor_copy(dst, src)
                ins.then_inc(copied, 1)

        lead = NG - first_group[N - 2]

        def free_weights(engine, it, u):
            if u >= 2:
                engine.wait_ge(turned, it * NG + first_group[u - 1] + lead)
            else:
                engine.wait_ge(turned, it * NG + (0 if u == 1 else first_group[N - 1] - NG) + lead)

        @block.sync
        def _(sp):
            def load(h, s):
                hh = kv_of(h)
                sp.dma_start(m["q"][s][0:HD, :], qkT[q_row + h * HD:q_row + (h + 1) * HD, :]).then_inc(qk_loaded[s], 16)
                sp.dma_start(m["k"][s][0:HD, :], qkT[k_row + hh * HD:k_row + (hh + 1) * HD, :]).then_inc(qk_loaded[s], 16)
                if kind == "fox":
                    sp.dma_start(m["q"][s][HD:HD + 1, :], crow[0, h:h + 1, :]).then_inc(qk_loaded[s], 16)
                    sp.dma_start(m["q"][s][HD + 1:HD + 2, :], a["ones"]).then_inc(qk_loaded[s], 16)
                    sp.dma_start(m["k"][s][HD:HD + 1, :], a["ones"]).then_inc(qk_loaded[s], 16)
                    sp.dma_start(m["k"][s][HD + 1:HD + 2, :], crow[1, h:h + 1, :]).then_inc(qk_loaded[s], 16)
                if kind in ("dsa", "swa"):
                    sp.dma_start(m["t5"][s][:, :], t5tile[(NH if kind == "dsa" else 0) + h]).then_inc(qk_loaded[s], 16)
                    col = a["t5_table"][N_BUCKETS - 1:N_BUCKETS, NH + h:NH + h + 1] if kind == "dsa" else a["attn_sinks"][0:1, h:h + 1]
                    sp.dma_start(m["hc"][s][:, :], col.to_broadcast([P, 1])).then_inc(qk_loaded[s], 16)
                sp.dma_start(m["v"][s][:, :, :], vtok[:, v_col + hh * HD:v_col + (hh + 1) * HD].rearrange(
                    "(b p) d -> p b d", p=P)).then_inc(v_loaded[s], 16)

            for s in range(2):
                load(s, s)
            for it in range(2):
                for s in range(2):
                    h = it * 2 + s
                    sp.wait_ge(finished, it * N + N - 1 + s + 2)
                    sp.dma_start(otok[:, branch * 256 + h * HD:branch * 256 + (h + 1) * HD].rearrange(
                        "(b p) d -> p b d", p=P), m["o"][s][:, :, :]).then_inc(stored[s], 16)
                    if it == 0:
                        load(h + 2, s)
            for s in range(2):
                sp.wait_ge(stored[s], 16 + 32)

        @block.scalar
        def _(act):
            if kind == "sb":
                chain = Chain(act_chain, 2 * N)
            if kind == "swa":
                chain = Chain(act_chain, N)

            def soften(it, u):
                W = (units[u][0] + 1) * P
                z, y = m["s_ps"][u % 2], t[u % 2]
                act.wait_ge(logits, it * N + u + 1)
                act.wait_ge(shaped, it * N + u + 1)
                chain.did(act.activation(y[:, 0:W], z[:, 0:W], ACT.Abs))
                chain.wait(act, it)
                chain.did(act.activation(y[:, 0:W], y[:, 0:W], ACT.Exp, scale=-1.0))
                chain.wait(act, it)
                act.activation(y[:, 0:W], y[:, 0:W], ACT.Ln, bias=1.0).then_inc(soft, 1)

            def weigh(it, u):
                W = len(keys(units[u][0])) * P
                act.wait_ge(shaped, it * N + u + 1 + 2)
                if kind == "sb":
                    act.activation(x[u % 2][:, 0:W], x[u % 2][:, 0:W], ACT.Exp).then_inc(weighed, 1)
                    return
                nm = m["negmax"][u % 4][:, 0:1]
                if kind == "swa":
                    chain.did(act.activation(m["sinkp"][u % 4][:, :], m["hc"][units[u][1]][:, :], ACT.Exp, bias=nm))
                if kind == "fox":
                    free_weights(act, it, u)
                src = m["s_ps"][u % 2] if kind == "fox" else x[u % 2]
                act.activation(x[u % 2][:, 0:W], src[:, 0:W], ACT.Exp, bias=nm,
                               accum_out=m["den"][u % 4][:, :]).then_inc(weighed, 1)

            with act.Fori(0, 2) as it:
                if kind in ("sb", "swa"):
                    chain.n = 0
                for u in range(N + 2):
                    if kind == "sb" and u < N:
                        soften(it, u)
                    if 1 <= u <= N:
                        weigh(it, u - 1)
                    if act_turns and u >= 2:
                        copy_turned(act, it, u - 2)

        @block.vector
        def _(dve):
            dve.sem_inc(shaped, 2)
            dve.sem_inc(finished, 2)
            dve.sem_inc(stored[0], 16)
            dve.sem_inc(stored[1], 16)
            if not act_turns:
                dve.sem_inc(copied, 2)

            def ops_of(u):
                i = units[u][0]
                return {"fox": 1, "sb": 3, "swa": 4,
                        "dsa": 2 if i < 2 else 4}[kind] - (1 if kind == "sb" else 0)

            per = sum(ops_of(u) for u in range(N)) + (2 if kind == "swa" else 0)
            chain = Chain(dve_chain, per)

            def shape(it, u):
                i, s = units[u]
                W = len(keys(i)) * P
                S, X = m["s_ps"][u % 2], x[u % 2]
                T5 = m["t5"][s]
                dve.wait_ge(logits, it * N + u + 1)
                if kind == "fox":
                    dve.tensor_reduce(m["negmax"][u % 4][:, :], S[:, 0:W], AX, ALU.max, negate=True).then_inc(shaped, 1)
                    return
                free_weights(dve, it, u)
                if kind == "sb":
                    dve.wait_ge(soft, it * N + u + 1)
                    chain.did(dve.scalar_tensor_tensor(m["sp"][:, 0:W], S[:, 0:W], 0.0, t[u % 2][:, 0:W],
                                                       ALU.max, ALU.add))
                    chain.wait(dve, it)
                    sp = m["sp"][:, 0:W][:, ::-1]
                    chain.did(dve.tensor_tensor_scan(X[:, 0:W][:, ::-1],
                                                     sp, sp, 0.0,
                                                     ALU.add, ALU.max))
                    chain.wait(dve, it)
                    dve.tensor_tensor(X[:, 0:W], S[:, 0:W], X[:, 0:W], ALU.subtract).then_inc(shaped, 1)
                    return
                n0 = 0 if i == 0 else W - BAND
                band = T5[:, P:] if i == 0 else T5[:, :]
                if kind == "dsa" and i >= 2:
                    sel = selm[:, sel_at[i]:sel_at[i] + i + 1, :].rearrange("p b k -> p (b k)")
                    chain.did(dve.scalar_tensor_tensor(X[:, 0:n0], S[:, 0:n0], m["hc"][s][:, 0:1], sel[:, 0:n0],
                                                       ALU.add, ALU.add))
                chain.did(dve.tensor_tensor(X[:, n0:W], S[:, n0:W], band, ALU.add))
                if kind == "dsa" and i >= 2:
                    chain.wait(dve, it)
                    chain.did(dve.tensor_tensor(X[:, n0:W], X[:, n0:W], sel[:, n0:W], ALU.add))
                chain.wait(dve, it)
                if kind == "dsa":
                    dve.tensor_reduce(m["negmax"][u % 4][:, :], X[:, 0:W], AX, ALU.max, negate=True).then_inc(shaped, 1)
                else:
                    chain.did(dve.tensor_reduce(m["rawmax"][u % 2][:, :], X[:, 0:W], AX, ALU.max, negate=True))
                    chain.wait(dve, it)
                    dve.tensor_tensor(m["negmax"][u % 4][:, :], m["rawmax"][u % 2][:, :], m["hcn"][s][:, :],
                                      ALU.min).then_inc(shaped, 1)

            def finish(it, u):
                i, s = units[u]
                O = m["o_ps"][u % 2][:, 0:HD]
                if kind != "sb":
                    dve.wait_ge(weighed, it * N + u + 1 + 2)
                    if kind == "swa":
                        chain.did(dve.tensor_tensor(m["den"][u % 4][:, :], m["den"][u % 4][:, :],
                                                    m["sinkp"][u % 4][:, :], ALU.add))
                        chain.wait(dve, it)
                    chain.did(dve.reciprocal(m["rden"][u % 2][:, :], m["den"][u % 4][:, :]))
                    chain.wait(dve, it)
                dve.wait_ge(summed, it * N + u + 1 + 2)
                if i == 0:
                    dve.wait_ge(stored[s], it * 16 + 16)
                if kind == "sb":
                    dve.tensor_copy(m["o"][s][:, i, :], O).then_inc(finished, 1)
                else:
                    dve.tensor_scalar(m["o"][s][:, i, :], O, m["rden"][u % 2][:, 0:1], None,
                                      ALU.mult).then_inc(finished, 1)

            with dve.Fori(0, 2) as it:
                if kind == "swa":
                    for s in range(2):
                        dve.wait_ge(qk_loaded[s], it * 16 * n_loads + 16 * n_loads)
                        chain.did(dve.tensor_scalar(m["hcn"][s][:, :], m["hc"][s][:, :], -1.0, None, ALU.mult))
                    chain.wait(dve, it)
                if kind == "dsa":
                    for s in range(2):
                        dve.wait_ge(qk_loaded[s], it * 16 * n_loads + 16 * n_loads)
                for u in range(N + 3):
                    if u < N:
                        shape(it, u)
                    if not act_turns and 2 <= u < N + 2:
                        copy_turned(dve, it, u - 2)
                    if u >= 3:
                        finish(it, u - 3)
                assert chain.n == per, (kind, chain.n, per)

        @block.tensor
        def _(pe):
            pe.sem_inc(turned, lead)
            pe.sem_inc(summed, 2)
            if act_turns:
                pe.sem_inc(copied, 2)
            pe.sem_inc(weighed, 2)

            def score(it, u):
                i, s = units[u]
                if i == 0:
                    pe.wait_ge(qk_loaded[s], it * 16 * n_loads + 16 * n_loads)
                pe.wait_ge(weighed if kind == "fox" else shaped, it * N + u + 1)
                k0 = keys(i)[0] * P
                W = len(keys(i)) * P
                q = m["q"][s][0:rows, i * P:(i + 1) * P]
                for f in range(0, W, HALF):
                    n = min(HALF, W - f)
                    masked = kind in ("fox", "sb") and f + n == W
                    if masked:
                        mask = m["causal"] if kind == "fox" else m["strict"]
                        pe.matmul(m["s_ps"][u % 2][:, W - P:W], m["identb"][:, :], mask[:, :],
                                  start=True, stop=False, skip_group_check=True)
                    last = pe.matmul(m["s_ps"][u % 2][:, f:f + n], q, m["k"][s][0:rows, k0 + f:k0 + f + n],
                                     start=not masked, stop=True, skip_group_check=masked)
                last.then_inc(logits, 1)

            def turn(it, u):
                pe.wait_ge(weighed, it * N + u + 1 + 2)
                for g in range(first_group[u], first_group[u + 1]):
                    _, b, n = groups[g]
                    pe.wait_ge(copied, it * NG + g + 1)
                    for j in range(n):
                        last = pe.transpose(m["t_ps"][g % 2][:, j, :], x[u % 2][:, (b + j) * P:(b + j + 1) * P],
                                            ident[:, :])
                    last.then_inc(turned, 1)

            def apply(it, u):
                i, s = units[u]
                if i == 0:
                    pe.wait_ge(v_loaded[s], it * 16 + 16)
                pe.wait_ge(copied, it * NG + group_end(u) + 2)
                pe.wait_ge(finished, it * N + u + 1)
                ks = keys(i)
                for j, kb in enumerate(ks):
                    last = pe.matmul(m["o_ps"][u % 2][:, 0:HD], m["pT"][u % 2][:, j, :], m["v"][s][:, kb, :],
                                     start=(j == 0), stop=(j == len(ks) - 1))
                last.then_inc(summed, 1)

            with pe.Fori(0, 2) as it:
                score(it, 0)
                for u in range(N + 2):
                    if u + 1 < N:
                        score(it, u + 1)
                    if 1 <= u <= N:
                        turn(it, u - 1)
                    if u >= 2:
                        apply(it, u - 2)


def merge(nc, a, ident, otok, gatesT, mergedT):
    with ExitStack() as c:
        sb = lambda n, s, d=F32: c.enter_context(nc.sbuf_tensor(n, s, d))
        sem = c.enter_context(semaphores(nc))
        ot = [sb(f"mg_ot{s}", [P, D]) for s in range(2)]
        oT = sb("mg_oT", [P, KC, T])
        wt = [sb(f"mg_w{s}", [P, 4, 2, P]) for s in range(2)]
        gt = [sb(f"mg_g{s}", [P, 4, T]) for s in range(2)]
        mt = [sb(f"mg_m{s}", [P, T]) for s in range(2)]
        tmp = [sb(f"mg_tmp{s}", [P, HALF]) for s in range(2)]
        pt = [c.enter_context(nc.psum_tensor(f"mg_pt{s}", [P, KC, P], F32)) for s in range(2)]
        ps = [c.enter_context(nc.psum_tensor(f"mg_ps{s}", [P, HALF], F32)) for s in range(4)]
        o_loaded = [sem(f"mg_o_loaded{s}") for s in range(2)]
        turned = sem("mg_turned")
        copied = sem("mg_copied")
        wg_loaded = [sem(f"mg_wg_loaded{s}") for s in range(2)]
        multiplied = sem("mg_multiplied")
        gated = sem("mg_gated")
        added = sem("mg_added")
        stored = [sem(f"mg_stored{s}") for s in range(2)]
        block = c.enter_context(nc.Block())
        oview = otok.rearrange("(t p) d -> t p d", p=P)

        @block.sync
        def _(sp):
            def load(k, s):
                sp.dma_start(wt[s][:, :, :, :], a["w_br"][k].rearrange("a p b k n -> p (a b) k n")).then_inc(wg_loaded[s], 16)
                sp.dma_start(gt[s][:, :, :], gatesT.rearrange("(c b) p t -> c p b t", b=4)[k].rearrange(
                    "a p b t -> p (a b) t")).then_inc(wg_loaded[s], 16)

            def store(k, s):
                sp.wait_ge(added, k * 6 + 6)
                sp.dma_start(mergedT[bass.ds(k, 1)].rearrange("a p t -> p (a t)"), mt[s][:, :]).then_inc(stored[s], 16)

            with sp.Fori(0, NT // 2) as it:
                for s in range(2):
                    sp.wait_ge(turned, it * 2 + s + 1)
                    sp.dma_start(ot[s][:, :], oview[bass.ds(it * 2 + s, 1)].rearrange("a p d -> p (a d)")).then_inc(o_loaded[s], 16)
            load(bass.ds(0, 1), 0)
            load(bass.ds(1, 1), 1)
            with sp.Fori(0, KC // 2 - 1) as it:
                for s in range(2):
                    sp.wait_ge(gated, it * 16 + s * 8 + 8 + 4)
                    load(bass.ds(it * 2 + s + 2, 1), s)
                    store(it * 2 + s, s)
            for s in range(2):
                store(KC - 2 + s, s)
                sp.wait_ge(stored[s], 16 + 16 * KC // 2)

        @block.scalar
        def _(act):
            act.sem_inc(copied, 2)
            with act.Fori(0, NT // 2) as it:
                for s in range(2):
                    act.wait_ge(turned, it * 2 + s + 1 + 2)
                    act.wait_ge(copied, it * 2 + s + 1 + 1)
                    act.activation(oT[:, :, bass.ds((it * 2 + s) * P, P)], pt[s][:, :, :], ACT.Copy).then_inc(copied, 1)

        @block.vector
        def _(dve):
            dve.sem_inc(gated, 4)
            dve.sem_inc(stored[0], 16)
            dve.sem_inc(stored[1], 16)
            with dve.Fori(0, KC // 2) as it:
                for s in range(2):
                    dve.wait_ge(wg_loaded[s], it * 32 + 32)
                    dve.wait_ge(stored[s], it * 16 + 16)
                    for b in range(4):
                        for h in range(2):
                            n = b * 2 + h
                            na = (b - 1) * 2 + h
                            cols = slice(h * HALF, (h + 1) * HALF)
                            dve.wait_ge(multiplied, it * 16 + s * 8 + n + 1)
                            if b == 0:
                                dve.tensor_tensor(mt[s][:, cols], ps[n % 4][:, :], gt[s][:, b, cols],
                                                  ALU.mult).then_inc(gated, 1)
                                continue
                            dve.tensor_tensor(tmp[h][:, :], ps[n % 4][:, :], gt[s][:, b, cols], ALU.mult).then_inc(gated, 1)
                            dve.wait_ge(gated, it * 16 + s * 8 + n + 1 + 4)
                            if b > 1:
                                dve.wait_ge(added, it * 12 + s * 6 + na - 1)
                            dve.tensor_tensor(mt[s][:, cols], mt[s][:, cols], tmp[h][:, :], ALU.add).then_inc(added, 1)

        @block.tensor
        def _(pe):
            pe.sem_inc(turned, 2)
            with pe.Fori(0, NT // 2) as it:
                for s in range(2):
                    pe.wait_ge(o_loaded[s], it * 16 + 16)
                    pe.wait_ge(copied, it * 2 + s + 1)
                    for k in range(KC):
                        last = pe.transpose(pt[s][:, k, :], ot[s][:, k * P:(k + 1) * P], ident[:, :])
                    last.then_inc(turned, 1)
            pe.wait_ge(copied, NT + 2)
            with pe.Fori(0, KC // 2) as it:
                for s in range(2):
                    pe.wait_ge(wg_loaded[s], it * 32 + 32)
                    for b in range(4):
                        for h in range(2):
                            n = b * 2 + h
                            pe.wait_ge(gated, it * 16 + s * 8 + n + 1)
                            for k in range(2):
                                last = pe.matmul(ps[n % 4][:, :], wt[s][:, b, k, :],
                                                 oT[:, 2 * b + k, h * HALF:(h + 1) * HALF], start=(k == 0), stop=(k == 1))
                            last.then_inc(multiplied, 1)


def output_and_router(nc, a, ident, lg, mergedT, x2d, h2d):
    x = a["x"]
    with ExitStack() as c:
        sb = lambda n, s, d=F32: c.enter_context(nc.sbuf_tensor(n, s, d))
        sem = c.enter_context(semaphores(nc))
        wo = sb("or_wo", [P, KC, D])
        wr = sb("or_wr", [P, KC, 36])
        br = sb("or_br", [P, 36])
        g = sb("or_g", [P, D])
        mt = [sb(f"or_mt{s}", [P, KC, P]) for s in range(2)]
        xt = [sb(f"or_x{s}", [P, D]) for s in range(2)]
        x2 = [sb(f"or_x2{s}", [P, D]) for s in range(2)]
        h2 = [sb(f"or_h2{s}", [P, D]) for s in range(2)]
        hT = [sb(f"or_hT{s}", [P, KC, P]) for s in range(2)]
        junk = sb("or_junk", [P, D])
        ss = [sb(f"or_ss{s}", [P, 1]) for s in range(2)]
        sd = [sb(f"or_sd{s}", [P, 1]) for s in range(2)]
        rs = [sb(f"or_rs{s}", [P, 1]) for s in range(2)]
        yp = [c.enter_context(nc.psum_tensor(f"or_yp{s}", [P, D], F32)) for s in range(2)]
        tp = c.enter_context(nc.psum_tensor("or_tp", [P, KC, P], F32))
        lp = [c.enter_context(nc.psum_tensor(f"or_lp{s}", [P, HALF], F32)) for s in range(2)]
        w_loaded = sem("or_w_loaded")
        loaded = [sem(f"or_loaded{s}") for s in range(2)]
        multiplied = sem("or_multiplied")
        summed = sem("or_summed")
        squared = sem("or_squared")
        rooted = sem("or_rooted")
        inverted = sem("or_inverted")
        normed = sem("or_normed")
        turned = sem("or_turned")
        copied = sem("or_copied")
        routed = sem("or_routed")
        logged = sem("or_logged")
        x2_stored = [sem(f"or_x2_stored{s}") for s in range(2)]
        h2_stored = [sem(f"or_h2_stored{s}") for s in range(2)]
        block = c.enter_context(nc.Block())
        tiles = lambda t: t.rearrange("(t p) d -> t p d", p=P)
        n_it = NT // 2

        @block.sync
        def _(sp):
            sp.dma_start(wo[:, :, :], a["w_out"]).then_inc(w_loaded, 16)
            sp.dma_start(wr[:, :, :], a["w_router"]).then_inc(w_loaded, 16)
            sp.dma_start(br[:, :], a["b_router"].to_broadcast([P, 36])).then_inc(w_loaded, 16)
            sp.dma_start(g[:, :], a["norm_ffn_g"].to_broadcast([P, D])).then_inc(w_loaded, 16)

            def load(it):
                for s in range(2):
                    sp.wait_ge(summed, it * 2 + s + 1)
                    sp.dma_start(mt[s][:, :, :], mergedT[:, :, bass.ds((it * 2 + s) * P, P)].rearrange(
                        "k p t -> p k t")).then_inc(loaded[s], 16)
                    sp.dma_start(xt[s][:, :], x[bass.ds(it * 2 + s, 1)].rearrange("a p d -> p (a d)")).then_inc(loaded[s], 16)

            def store(it):
                for s in range(2):
                    sp.wait_ge(summed, it * 2 + s + 1 + 2)
                    sp.dma_start(tiles(x2d)[bass.ds(it * 2 + s, 1)].rearrange("a p d -> p (a d)"), x2[s][:, :]).then_inc(x2_stored[s], 16)
                for s in range(2):
                    sp.wait_ge(normed, it * 2 + s + 1 + 2)
                    sp.dma_start(tiles(h2d)[bass.ds(it * 2 + s, 1)].rearrange("a p d -> p (a d)"), h2[s][:, :]).then_inc(h2_stored[s], 16)

            load(0)
            with sp.Fori(0, n_it - 1) as it:
                load(it + 1)
                store(it)
            store(n_it - 1)
            for s in range(2):
                sp.wait_ge(x2_stored[s], 16 + 16 * n_it)
                sp.wait_ge(h2_stored[s], 16 + 16 * n_it)

        @block.scalar
        def _(act):
            with act.Fori(0, n_it) as it:
                for s in range(2):
                    act.wait_ge(summed, it * 2 + s + 1 + 2)
                    act.activation(junk[:, :], x2[s][:, :], ACT.Square, accum_out=ss[s][:, :]).then_inc(squared, 1)
                    act.wait_ge(squared, it * 2 + s + 1)
                    act.activation(sd[s][:, :], ss[s][:, :], ACT.Sqrt, scale=1.0 / D, bias=EPS).then_inc(rooted, 1)
                for s in range(2):
                    act.wait_ge(turned, it * 2 + s + 1 + 2)
                    act.wait_ge(routed, it * 2 + s + 1)
                    act.activation(hT[s][:, :, :], tp[:, :, :], ACT.Copy).then_inc(copied, 1)

        @block.vector
        def _(dve):
            dve.sem_inc(summed, 2)
            dve.sem_inc(normed, 2)
            dve.sem_inc(logged, 2)
            for s in range(2):
                dve.sem_inc(x2_stored[s], 16)
                dve.sem_inc(h2_stored[s], 16)
            dve.wait_ge(w_loaded, 64)
            with dve.Fori(0, n_it) as it:
                for s in range(2):
                    dve.wait_ge(multiplied, it * 2 + s + 1)
                    dve.wait_ge(x2_stored[s], it * 16 + 16)
                    dve.tensor_tensor(x2[s][:, :], yp[s][:, :], xt[s][:, :], ALU.add).then_inc(summed, 1)
                for s in range(2):
                    dve.wait_ge(rooted, it * 2 + s + 1)
                    dve.reciprocal(rs[s][:, :], sd[s][:, :]).then_inc(inverted, 1)
                    dve.wait_ge(inverted, it * 2 + s + 1)
                    dve.wait_ge(h2_stored[s], it * 16 + 16)
                    dve.wait_ge(turned, it * 2 + s + 1)
                    dve.scalar_tensor_tensor(h2[s][:, :], x2[s][:, :], rs[s][:, 0:1], g[:, :], ALU.mult,
                                             ALU.mult).then_inc(normed, 1)
                for s in range(2):
                    dve.wait_ge(routed, it * 2 + s + 1 + 2)
                    dve.tensor_tensor(lg[:, bass.ds(it * 2 + s, 1), :].rearrange("p a n -> p (a n)"), lp[s][:, 0:36],
                                      br[:, :], ALU.add).then_inc(logged, 1)

        @block.tensor
        def _(pe):
            pe.sem_inc(copied, 1)
            pe.sem_inc(turned, 2)
            pe.sem_inc(routed, 2)
            pe.wait_ge(w_loaded, 64)
            with pe.Fori(0, n_it) as it:
                for s in range(2):
                    pe.wait_ge(loaded[s], it * 32 + 32)
                    pe.wait_ge(summed, it * 2 + s + 1)
                    for h in range(2):
                        for k in range(KC):
                            last = pe.matmul(yp[s][:, h * HALF:(h + 1) * HALF], mt[s][:, k, :],
                                             wo[:, k, h * HALF:(h + 1) * HALF], start=(k == 0), stop=(k == KC - 1))
                    last.then_inc(multiplied, 1)
                for s in range(2):
                    pe.wait_ge(normed, it * 2 + s + 1 + 2)
                    pe.wait_ge(copied, it * 2 + s + 1)
                    for k in range(KC):
                        last = pe.transpose(tp[:, k, :], h2[s][:, k * P:(k + 1) * P], ident[:, :])
                    last.then_inc(turned, 1)
                for s in range(2):
                    pe.wait_ge(copied, it * 2 + s + 1 + 1)
                    pe.wait_ge(logged, it * 2 + s + 1)
                    for k in range(KC):
                        last = pe.matmul(lp[s][:, 0:36], hT[s][:, k, :], wr[:, k, :], start=(k == 0), stop=(k == KC - 1))
                    last.then_inc(routed, 1)


def route(nc, a, lg, pos, gate, eblk, pairs, slot_tok):
    with ExitStack() as c:
        sb = lambda n, s, d=F32: c.enter_context(nc.sbuf_tensor(n, s, d))
        sem = c.enter_context(semaphores(nc))
        E8 = [P, NT, PER_GROUP]
        rank4 = sb("rt_rank4", [P, GROUPS])
        rank8 = sb("rt_rank8", [P, PER_GROUP])
        gs = sb("rt_gs", [P, NT, GROUPS])
        gsc = sb("rt_gsc", [P, NT, GROUPS])
        goh = sb("rt_goh", [P, NT, GROUPS])
        m1 = sb("rt_m1", [P, NT, 1])
        m2 = sb("rt_m2", [P, NT, 1])
        gsum = sb("rt_gsum", [P, NT, 1])
        pg = sb("rt_pg", [P, NT, 1])
        ein = sb("rt_ein", E8)
        etmp = sb("rt_etmp", E8)
        esc = sb("rt_esc", E8)
        eoh = [sb(f"rt_eoh{k}", E8) for k in range(2)]
        ratio = sb("rt_ratio", [P, NT, 1])
        rsum = sb("rt_rsum", [P, NT, 1])
        rinv = sb("rt_rinv", [P, NT, 1])
        full = [sb(f"rt_full{k}", [P, NT, EXPERTS]) for k in range(2)]
        both = sb("rt_both", [P, NT, EXPERTS], BF16)
        ones = sb("rt_ones", [P, P], BF16)
        before = sb("rt_before", [P, P], BF16)
        prefix = sb("rt_prefix", [P, NT + 1, EXPERTS])
        steps = sb("rt_steps", [P, NT])
        cmp = sb("rt_cmp", [P, EXPERTS, NT])
        nblk = sb("rt_nblk", [P, EXPERTS])
        bend = sb("rt_bend", [P, EXPERTS])
        base = sb("rt_base", [P, EXPERTS])
        slot = sb("rt_slot", [P, NT, EXPERTS])
        prod = sb("rt_prod", [P, NT, EXPERTS])
        posf = sb("rt_posf", [P, NT, 1])
        bidx = sb("rt_bidx", [1, MAX_BLOCKS + 2])
        bcmp = sb("rt_bcmp", [1, MAX_BLOCKS + 2, EXPERTS])
        ebf = sb("rt_ebf", [1, MAX_BLOCKS + 2, 1])
        half = sb("rt_half", [1, 1])
        halfc = sb("rt_halfc", [1, MAX_BLOCKS // 2])
        evens = sb("rt_evens", [1, MAX_BLOCKS // 2])
        tok = sb("rt_tok", [P, NT], I32)
        zero = sb("rt_zero", [P, SLOTS // P], I32)
        ranks = c.enter_context(nc.psum_tensor("rt_ranks", [P, NT, EXPERTS], F32))
        sums = c.enter_context(nc.psum_tensor("rt_sums", [P, NT, EXPERTS], F32))
        consts = sem("rt_consts")
        d = sem("rt_d")
        e_done = sem("rt_e_done")
        ranked = sem("rt_ranked")
        zeroed = sem("rt_zeroed")
        scattered = sem("rt_scattered")
        block = c.enter_context(nc.Block())
        marks = {}

        @block.vector
        def _(dve):
            n = [0]

            def step(ins):
                n[0] += 1
                ins.then_inc(d, 1)
                dve.wait_ge(d, n[0])

            bc = lambda ap, shape: ap.to_broadcast(shape)
            row = lambda ap, k: ap.unsqueeze(1).to_broadcast([P, NT, k])
            G4 = [P, NT, GROUPS]
            dve.wait_ge(consts, 7)
            g = lg[:, :, 0:GROUPS]
            step(dve.tensor_reduce(m1[:, :, :], g, AX, ALU.max))
            step(dve.tensor_tensor(gs[:, :, :], g, bc(m1[:, :, :], G4), ALU.subtract))
            marks["group"] = n[0]
            dve.wait_ge(e_done, 1)
            step(dve.tensor_reduce(gsum[:, :, :], gsc[:, :, :], AX, ALU.add))
            step(dve.reciprocal(pg[:, :, :], gsum[:, :, :]))

            def first_max(oh, scores, peak, rank, work, k):
                step(dve.tensor_tensor(work, scores, bc(peak, [P, NT, k]), ALU.is_equal))
                step(dve.tensor_tensor(work, work, row(rank, k), ALU.mult))
                step(dve.tensor_reduce(peak, work, AX, ALU.max))
                step(dve.tensor_tensor(oh, work, bc(peak, [P, NT, k]), ALU.is_equal))

            first_max(goh[:, :, :], g, m1[:, :, :], rank4[:, :], gsc[:, :, :], GROUPS)
            for q in range(GROUPS):
                e = lg[:, :, GROUPS + q * PER_GROUP:GROUPS + (q + 1) * PER_GROUP]
                dst = ein if q == 0 else etmp
                step(dve.tensor_tensor(dst[:, :, :], e, bc(goh[:, :, q:q + 1], E8), ALU.mult))
                if q:
                    step(dve.tensor_tensor(ein[:, :, :], ein[:, :, :], etmp[:, :, :], ALU.add))
            step(dve.tensor_reduce(m1[:, :, :], ein[:, :, :], AX, ALU.max))
            step(dve.tensor_copy(ratio[:, :, :], m1[:, :, :]))
            first_max(eoh[0][:, :, :], ein[:, :, :], m1[:, :, :], rank8[:, :], esc[:, :, :], PER_GROUP)
            step(dve.scalar_tensor_tensor(ein[:, :, :], eoh[0][:, :, :], PICKED, ein[:, :, :], ALU.mult, ALU.add))
            step(dve.tensor_reduce(m2[:, :, :], ein[:, :, :], AX, ALU.max))
            step(dve.tensor_tensor(ratio[:, :, :], m2[:, :, :], ratio[:, :, :], ALU.subtract))
            marks["ratio"] = n[0]
            first_max(eoh[1][:, :, :], ein[:, :, :], m2[:, :, :], rank8[:, :], esc[:, :, :], PER_GROUP)
            dve.wait_ge(e_done, 2)
            step(dve.tensor_scalar(rsum[:, :, :], rinv[:, :, :], 1.0, None, ALU.add))
            step(dve.reciprocal(rsum[:, :, :], rsum[:, :, :]))
            step(dve.tensor_tensor(gate[0][:, :].unsqueeze(2), pg[:, :, :], rsum[:, :, :], ALU.mult))
            step(dve.tensor_tensor(gate[1][:, :].unsqueeze(2), gate[0][:, :].unsqueeze(2), rinv[:, :, :], ALU.mult))
            for k in range(2):
                for q in range(GROUPS):
                    step(dve.tensor_tensor(full[k][:, :, q * PER_GROUP:(q + 1) * PER_GROUP], eoh[k][:, :, :],
                                           bc(goh[:, :, q:q + 1], E8), ALU.mult))
            step(dve.tensor_tensor(both[:, :, :], full[0][:, :, :], full[1][:, :, :], ALU.add))
            marks["both"] = n[0]
            dve.wait_ge(ranked, 2)
            step(dve.memset(prefix[:, 0, :], 0.0))
            for t in range(NT):
                step(dve.tensor_tensor(prefix[:, t + 1, :], sums[:, t, :], prefix[:, t, :], ALU.add))
            S = [P, EXPERTS, NT]
            step(dve.tensor_tensor(cmp[:, :, :], prefix[:, NT, :].unsqueeze(2).to_broadcast(S),
                                   steps[:, :].unsqueeze(1).to_broadcast(S), ALU.is_gt))
            step(dve.tensor_reduce(nblk[:, :].unsqueeze(2), cmp[:, :, :], AX, ALU.add))
            step(dve.tensor_tensor_scan(bend[:, :], nblk[:, :], nblk[:, :], 0.0, ALU.add, ALU.max))
            step(dve.tensor_tensor(base[:, :], bend[:, :], nblk[:, :], ALU.subtract))
            step(dve.tensor_scalar(base[:, :], base[:, :], float(P), None, ALU.mult))
            step(dve.tensor_tensor(slot[:, :, :], ranks[:, :, :], prefix[:, 0:NT, :], ALU.add))
            step(dve.tensor_tensor(slot[:, :, :], slot[:, :, :], base[:, :].unsqueeze(1).to_broadcast([P, NT, EXPERTS]), ALU.add))
            for k in range(2):
                step(dve.tensor_tensor(prod[:, :, :], full[k][:, :, :], slot[:, :, :], ALU.mult))
                step(dve.tensor_reduce(posf[:, :, :], prod[:, :, :], AX, ALU.add))
                step(dve.tensor_copy(pos[k][:, :].unsqueeze(2), posf[:, :, :]))
            marks["pos"] = n[0]
            B = [1, MAX_BLOCKS + 2, EXPERTS]
            step(dve.tensor_tensor(bcmp[:, :, :], bend[0:1, :].unsqueeze(1).to_broadcast(B),
                                   bidx[:, :].unsqueeze(2).to_broadcast(B), ALU.is_le))
            step(dve.tensor_reduce(ebf[:, :, :], bcmp[:, :, :], AX, ALU.add))
            step(dve.tensor_scalar(eblk[:, :].unsqueeze(2), ebf[:, :, :], float(EXPERTS - 1), None, ALU.min))
            step(dve.tensor_tensor(halfc[:, :], bend[0:1, EXPERTS - 1:EXPERTS].to_broadcast([1, MAX_BLOCKS // 2]),
                                   evens[:, :], ALU.is_gt))
            step(dve.tensor_reduce(half[:, :], halfc[:, :], AX, ALU.add))
            step(dve.tensor_copy(pairs[:, :], half[:, :]))

        @block.scalar
        def _(act):
            act.wait_ge(d, marks["group"])
            act.activation(gsc[:, :, :], gs[:, :, :], ACT.Exp).then_inc(e_done, 1)
            act.wait_ge(d, marks["ratio"])
            act.activation(rinv[:, :, :], ratio[:, :, :], ACT.Exp).then_inc(e_done, 1)

        @block.tensor
        def _(pe):
            pe.wait_ge(consts, 7)
            pe.wait_ge(d, marks["both"])
            m = both[:, :, :].rearrange("p t e -> p (t e)")
            pe.matmul(ranks[:, :, :].rearrange("p t e -> p (t e)"), before[:, :], m, start=True, stop=True).then_inc(ranked, 1)
            pe.matmul(sums[:, :, :].rearrange("p t e -> p (t e)"), ones[:, :], m, start=True, stop=True).then_inc(ranked, 1)

        @block.gpsimd
        def _(pool):
            k = [0]

            def const(ins):
                k[0] += 1
                ins.then_inc(consts, 1)

            F = dict(allow_small_or_imprecise_dtypes=True)
            pool.memset(before[:, :], 1.0).then_inc(zeroed, 1)
            pool.memset(zero[:, :], 0).then_inc(zeroed, 1)
            pool.wait_ge(zeroed, 2)
            const(pool.affine_select(out=before[:, :], in_=before[:, :], compare_op=ALU.is_gt, fill=0.0, base=0,
                                     pattern=[[1, P]], channel_multiplier=-1))
            const(pool.memset(ones[:, :], 1.0))
            const(pool.iota(rank4[:, :], pattern=[[-1, GROUPS]], base=GROUPS, channel_multiplier=0, **F))
            const(pool.iota(rank8[:, :], pattern=[[-1, PER_GROUP]], base=PER_GROUP, channel_multiplier=0, **F))
            const(pool.iota(steps[:, :], pattern=[[P, NT]], base=0, channel_multiplier=0, **F))
            const(pool.iota(bidx[:, :], pattern=[[1, MAX_BLOCKS + 2]], base=0, channel_multiplier=0, **F))
            const(pool.iota(evens[:, :], pattern=[[2, MAX_BLOCKS // 2]], base=0, channel_multiplier=0, **F))
            const(pool.iota(tok[:, :], pattern=[[P, NT]], base=0, channel_multiplier=1))
            pool.dma_start(slot_tok.rearrange("(p n) a -> p (n a)", p=P), zero[:, :]).then_inc(scattered, 16)
            pool.wait_ge(scattered, 16)
            pool.wait_ge(consts, 8)
            pool.wait_ge(d, marks["pos"])
            for q in range(2):
                for t in range(NT):
                    pool.indirect_dma_start(slot_tok[:, :], bass.IndirectOffsetOnAxis(ap=pos[q][:, t:t + 1], axis=0),
                                            tok[:, t:t + 1], None).then_inc(scattered, 16)
            pool.wait_ge(scattered, 16 + 16 * 2 * NT)


def experts(nc, a, ident, eblk, pairs, slot_tok, h2d, ybd):
    with ExitStack() as c:
        sb = lambda n, s, d=F32: c.enter_context(nc.sbuf_tensor(n, s, d))
        sem = c.enter_context(semaphores(nc))
        FC = FF // P
        up = [sb(f"ex_up{s}", [P, KC, 2 * FF]) for s in range(2)]
        down = [sb(f"ex_down{s}", [P, FC, D]) for s in range(2)]
        ids = [sb(f"ex_ids{s}", [P, 1], I32) for s in range(2)]
        xg = [sb(f"ex_xg{s}", [P, D]) for s in range(2)]
        xT = [sb(f"ex_xT{s}", [P, KC, P]) for s in range(2)]
        gl = [sb(f"ex_gl{s}", [P, FF]) for s in range(2)]
        act_ = [sb(f"ex_act{s}", [P, FF]) for s in range(2)]
        aT = [sb(f"ex_aT{s}", [P, FC, P]) for s in range(2)]
        yo = [sb(f"ex_yo{s}", [P, D]) for s in range(2)]
        xp = c.enter_context(nc.psum_tensor("ex_xp", [P, KC, P], F32))
        gp = c.enter_context(nc.psum_tensor("ex_gp", [P, FF], F32))
        upp = c.enter_context(nc.psum_tensor("ex_upp", [P, FF], F32))
        ap_ = c.enter_context(nc.psum_tensor("ex_ap", [P, FC, P], F32))
        yp = c.enter_context(nc.psum_tensor("ex_yp", [P, D], F32))
        up_loaded = [sem(f"ex_up_loaded{s}") for s in range(2)]
        down_loaded = [sem(f"ex_down_loaded{s}") for s in range(2)]
        ids_loaded = [sem(f"ex_ids_loaded{s}") for s in range(2)]
        gathered = [sem(f"ex_gathered{s}") for s in range(2)]
        wait_carrier = sem("ex_wait_carrier")
        x_turned = sem("ex_x_turned")
        x_copied = sem("ex_x_copied")
        g_made = sem("ex_g_made")
        u_made = sem("ex_u_made")
        silu_done = sem("ex_silu_done")
        act_made = sem("ex_act_made")
        a_turned = sem("ex_a_turned")
        a_copied = sem("ex_a_copied")
        y_made = sem("ex_y_made")
        y_copied = sem("ex_y_copied")
        stored = [sem(f"ex_stored{s}") for s in range(2)]
        block = c.enter_context(nc.Block())
        upv = a["w_expert_up"].rearrange("e (k p) f -> e p k f", p=P)
        downv = a["w_expert_down"].rearrange("e (k p) f -> e p k f", p=P)
        yv = ybd.rearrange("(b p) d -> b p d", p=P)
        sv = slot_tok.rearrange("(b p) a -> b p a", p=P)
        trips = lambda eng: eng.value_load(pairs[0:1, 0:1], min_val=1, max_val=MAX_BLOCKS // 2)

        @block.sync
        def _(sp):
            n = trips(sp)
            with sp.Fori(0, n) as it:
                for s in range(2):
                    e = sp.value_load(eblk[0:1, bass.ds(it * 2 + s, 1)], min_val=0, max_val=EXPERTS - 1)
                    sp.wait_ge(u_made, it * 2 + s + 1)
                    sp.dma_start(up[s][:, :, :], upv[bass.ds(e, 1)].rearrange("a p k f -> p (a k) f")).then_inc(up_loaded[s], 16)
                    sp.wait_ge(y_made, it * 2 + s + 1)
                    sp.dma_start(down[s][:, :, :], downv[bass.ds(e, 1)].rearrange("a p k f -> p (a k) f")).then_inc(down_loaded[s], 16)

        @block.gpsimd
        def _(pool):
            n = trips(pool)

            def gather(b, s, turned, loads):
                pool.wait_ge(x_turned, turned)
                pool.sem_inc(wait_carrier, 1)
                pool.dma_start(ids[s][:, :], sv[bass.ds(b, 1)].rearrange("a p n -> p (a n)")).then_inc(ids_loaded[s], 16)
                pool.wait_ge(ids_loaded[s], loads)
                pool.sem_inc(wait_carrier, 1)
                pool.indirect_dma_start(xg[s][:, :], None, h2d[:, :],
                                        bass.IndirectOffsetOnAxis(ap=ids[s][:, 0:1], axis=0)).then_inc(gathered[s], 16)

            with pool.Fori(0, n) as it:
                for s in range(2):
                    gather(it * 2 + s, s, it * 2 + s + 1, it * 16 + 16)
            gather(n * 2, 0, n * 2 + 1, n * 16 + 16)

        @block.scalar
        def _(act):
            n = trips(act)

            def x_copy(b, s):
                act.wait_ge(x_turned, b + 1 + 2)
                act.wait_ge(u_made, b + 1)
                act.activation(xT[s][:, :, :], xp[:, :, :], ACT.Copy).then_inc(x_copied, 1)

            x_copy(0, 0)
            with act.Fori(0, n) as it:
                for s in range(2):
                    act.wait_ge(g_made, it * 2 + s + 1)
                    act.wait_ge(act_made, it * 2 + s + 1)
                    act.activation(gl[s][:, :], gp[:, :], ACT.Silu).then_inc(silu_done, 1)
                    x_copy(it * 2 + s + 1, 1 - s)
                    act.wait_ge(y_made, it * 2 + s + 1 + 2)
                    act.wait_ge(stored[s], it * 16 + 16)
                    act.activation(yo[s][:, 0:HALF], yp[:, 0:HALF], ACT.Copy).then_inc(y_copied, 1)
                    act.wait_ge(y_copied, it * 4 + s * 2 + 2 + 2)
                    act.dma_start(yv[bass.ds(it * 2 + s, 1)].rearrange("a p d -> p (a d)"), yo[s][:, :]).then_inc(stored[s], 16)
            for s in range(2):
                act.wait_ge(stored[s], n * 16 + 16)
                act.sem_inc(wait_carrier, 1)

        @block.vector
        def _(dve):
            n = trips(dve)
            dve.sem_inc(act_made, 1)
            dve.sem_inc(y_copied, 2)
            for s in range(2):
                dve.sem_inc(stored[s], 16)
            with dve.Fori(0, n) as it:
                for s in range(2):
                    dve.wait_ge(silu_done, it * 2 + s + 1)
                    dve.wait_ge(u_made, it * 2 + s + 1 + 2)
                    dve.wait_ge(a_turned, it * 2 + s + 1)
                    dve.tensor_tensor(act_[s][:, :], upp[:, :], gl[s][:, :], ALU.mult).then_inc(act_made, 1)
                    dve.wait_ge(a_turned, it * 2 + s + 1 + 2)
                    dve.wait_ge(y_made, it * 2 + s + 1)
                    dve.tensor_copy(aT[s][:, :, :], ap_[:, :, :]).then_inc(a_copied, 1)
                    dve.wait_ge(y_made, it * 2 + s + 1 + 2)
                    dve.wait_ge(stored[s], it * 16 + 16)
                    dve.tensor_copy(yo[s][:, HALF:D], yp[:, HALF:D]).then_inc(y_copied, 1)

        @block.tensor
        def _(pe):
            n = trips(pe)
            pe.sem_inc(x_turned, 2)
            pe.sem_inc(u_made, 2)
            pe.sem_inc(y_made, 2)
            pe.sem_inc(a_turned, 2)

            def turn_x(b, s, loads):
                pe.wait_ge(gathered[s], loads)
                pe.wait_ge(x_copied, b)
                for k in range(KC):
                    last = pe.transpose(xp[:, k, :], xg[s][:, k * P:(k + 1) * P], ident[:, :])
                last.then_inc(x_turned, 1)

            pe.wait_ge(gathered[0], 16)
            for k in range(KC):
                last = pe.transpose(xp[:, k, :], xg[0][:, k * P:(k + 1) * P], ident[:, :])
            last.then_inc(x_turned, 1)
            with pe.Fori(0, n) as it:
                for s in range(2):
                    b = it * 2 + s
                    pe.wait_ge(up_loaded[s], it * 16 + 16)
                    pe.wait_ge(x_copied, b + 1)
                    pe.wait_ge(act_made, b + 1)
                    for bank, f, made in ((gp, 0, g_made), (upp, FF, u_made)):
                        for k in range(KC):
                            last = pe.matmul(bank[:, :], xT[s][:, k, :], up[s][:, k, f:f + FF],
                                             start=(k == 0), stop=(k == KC - 1))
                        last.then_inc(made, 1)
                    turn_x(b + 1, 1 - s, it * 16 + 16 + 16 * s)
                    pe.wait_ge(act_made, b + 1 + 1)
                    for k in range(FC):
                        last = pe.transpose(ap_[:, k, :], act_[s][:, k * P:(k + 1) * P], ident[:, :])
                    last.then_inc(a_turned, 1)
                    pe.wait_ge(a_copied, b + 1)
                    pe.wait_ge(down_loaded[s], it * 16 + 16)
                    pe.wait_ge(y_copied, it * 4 + s * 2 + 2)
                    for h in range(2):
                        for k in range(FC):
                            last = pe.matmul(yp[:, h * HALF:(h + 1) * HALF], aT[s][:, k, :],
                                             down[s][:, k, h * HALF:(h + 1) * HALF], start=(k == 0), stop=(k == FC - 1))
                    last.then_inc(y_made, 1)


def combine(nc, pos, gate, x2d, ybd, out):
    with ExitStack() as c:
        sb = lambda n, s, d=F32: c.enter_context(nc.sbuf_tensor(n, s, d))
        sem = c.enter_context(semaphores(nc))
        xt = [sb(f"cb_x{t}", [P, D]) for t in range(NT)]
        y = [[sb(f"cb_y{t}{k}", [P, D]) for k in range(2)] for t in range(NT)]
        x_loaded = [sem(f"cb_x_loaded{t}") for t in range(NT)]
        y_loaded = [sem(f"cb_y_loaded{t}") for t in range(NT)]
        added = sem("cb_added")
        stored = sem("cb_stored")
        block = c.enter_context(nc.Block())
        rows = lambda d, t: d[t * P:(t + 1) * P, :]

        @block.sync
        def _(sp):
            for t in range(NT):
                sp.dma_start(xt[t][:, :], rows(x2d, t)).then_inc(x_loaded[t], 16)
            for t in range(NT):
                sp.wait_ge(added, 2 * t + 2)
                sp.dma_start(rows(out, t), xt[t][:, :]).then_inc(stored, 16)
            sp.wait_ge(stored, 16 * NT)

        @block.gpsimd
        def _(pool):
            for t in range(NT):
                for k in range(2):
                    pool.indirect_dma_start(y[t][k][:, :], None, ybd[:, :],
                                            bass.IndirectOffsetOnAxis(ap=pos[k][:, t:t + 1], axis=0)).then_inc(y_loaded[t], 16)

        @block.vector
        def _(dve):
            for t in range(NT):
                dve.wait_ge(x_loaded[t], 16)
                dve.wait_ge(y_loaded[t], 32)
                for k in range(2):
                    dve.scalar_tensor_tensor(xt[t][:, :], y[t][k][:, :], gate[k][:, t:t + 1], xt[t][:, :],
                                             ALU.mult, ALU.add).then_inc(added, 1)
                    dve.wait_ge(added, 2 * t + k + 1)


def lay_out(inputs):
    offs = np.cumsum([0, 256, 128, 128, 256, 256, 256, 4, 256, 256, 256, 256, 64, 64, 256, 64, 4, 4096])
    (a_q, a_k, a_v, f_q, f_k, f_v, f_g, s_q, s_k, s_v, d_q, d_k, d_v, i_q, i_k, i_w, gates) = offs[:-1]
    w = np.asarray(inputs["w_in"])[0]
    rows = lambda m: np.ascontiguousarray(m.reshape(-1, P, m.shape[-1]).transpose(1, 0, 2))
    zeros = lambda n: np.zeros((D, n), w.dtype)
    cols = [w[:, a_q:a_q + 384], w[:, f_q:f_q + 512], w[:, d_q:d_q + 320], zeros(64), w[:, i_q:i_q + 320],
            w[:, f_g:f_g + 4], zeros(60), w[:, s_q:s_q + 512]]
    w_qk = np.concatenate(cols, 1).reshape(KC, P, QK_CHUNKS, P).transpose(2, 1, 0, 3)
    w_v = rows(np.concatenate([w[:, f_v:f_v + 256], w[:, s_v:s_v + 256], w[:, a_v:a_v + 128], w[:, d_v:d_v + 64],
                               w[:, i_w:i_w + 4]], 1))
    w_gate = w[:, gates:].reshape(KC, P, 4, KC, P).transpose(3, 2, 1, 0, 4).reshape(4 * KC, P, KC, P)
    w_br = np.asarray(inputs["w_branch"])[0].reshape(4, 2, P, KC, P).transpose(3, 2, 0, 1, 4)
    g = np.asarray(inputs["qk_gain"])[0]
    gain_cols = np.ones((P, QK_CHUNKS), g.dtype)
    for m, (q, k) in enumerate(((SWA_Q, SWA_K), (FOX_Q, FOX_K), (DSA_Q, DSA_K))):
        gain_cols[:, q:q + 2] = np.tile(g[m, 0], 2)[:, None]
        gain_cols[:, k:k + 2 if m == 1 else k + 1] = np.tile(g[m, 1], 2)[:, None]
    gain_cols[:, IDX_Q:IDX_Q + 2] = SCALE
    gain_cols[:, SB_Q:SB_Q + 2] = SCALE
    onehot = np.zeros((N_BUCKETS + 1, 2, T5_LINE), g.dtype)
    for m in range(BAND + P - 1):
        dist = BAND - 1 - m
        n = max(dist, 1)
        large = 16 + int(np.log(np.float32(n) / 16) / np.log(8.0) * 16) if n >= 16 else 0
        bucket = max(dist, 0) if dist < 16 else min(large, N_BUCKETS - 1)
        onehot[N_BUCKETS if dist < 0 or dist >= P else bucket, 0, m] = 1
        onehot[N_BUCKETS if dist < 0 else bucket, 1, m] = 1
    per_chunk = lambda v: np.asarray(v).reshape(KC, P).T
    w_r = np.concatenate([np.asarray(inputs["w_router_group"])[0], np.asarray(inputs["w_router_expert"])[0]], 1)
    b_r = np.concatenate([np.asarray(inputs["b_router_group"])[0], np.asarray(inputs["b_router_expert"])[0]])
    arrays = {
        "x": np.asarray(inputs["x"]).reshape(NT, P, D),
        "norm_mix_g": per_chunk(inputs["norm_mix_g"][0]),
        "w_qk": w_qk, "w_v": w_v, "w_gate": w_gate, "w_br": w_br, "gain_cols": gain_cols,
        "w_out": rows(np.asarray(inputs["w_out"])[0]),
        "forget_bias": np.asarray(inputs["forget_bias"]).reshape(NH, 1),
        "attn_sinks": np.asarray(inputs["attn_sinks"]).reshape(1, NH),
        "t5_table": inputs["t5_table"], "t5_onehot": onehot, "ones": np.ones((1, T), g.dtype),
        "norm_ffn_g": np.asarray(inputs["norm_ffn_g"]).reshape(1, D),
        "w_router": rows(w_r), "b_router": b_r.reshape(1, 36),
        "w_expert_up": np.asarray(inputs["w_expert_up"])[0],
        "w_expert_down": np.asarray(inputs["w_expert_down"])[0],
    }
    return {n: np.ascontiguousarray(v) for n, v in arrays.items()}


def kernel(**inputs):
    import concourse.bacc as bacc
    from concourse.bass_utils import run_bass_kernel_spmd

    nc = bacc.Bacc("TRN2", target_bir_lowering=False, num_devices=1)
    arrays = lay_out(inputs)
    a = {n: nc.dram_tensor(f"in_{n}", v.shape, mybir.dt.from_np(v.dtype), kind="ExternalInput").ap()
         for n, v in arrays.items()}
    out = nc.dram_tensor("out_x", (T, D), F32, kind="ExternalOutput").ap()
    build(nc, a, out)
    r = run_bass_kernel_spmd(nc, [{f"in_{n}": v for n, v in arrays.items()}], core_ids=[0])
    return r.results[0]["out_x"].reshape(1, T, D)
```

```python
from contextlib import ExitStack, contextmanager

import numpy as np

import concourse.bass as bass
from concourse import mybir

ALU = mybir.AluOpType
ACT = mybir.ActivationFunctionType
AX = mybir.AxisListType.X
F32 = mybir.dt.float32
FR = mybir.dt.float32r
BF16 = mybir.dt.bfloat16
I32 = mybir.dt.int32
U32 = mybir.dt.uint32

P = 128
D = 1024
T = 1024
KC = D // P
NT = T // P
HALF = 512
HD = 64
NH = 4
EPS = 1e-6
NEG = -1e30
SCALE = HD ** -0.5

SWA_Q, SWA_K, FOX_Q, FOX_K, DSA_Q, DSA_K = 0, 2, 3, 5, 7, 9
IDX_Q, IDX_K, SB_Q, SB_K = 10, 12, 13, 15
NORMED = 10
QK_CHUNKS = 17
FG_ROW = IDX_K * P + HD
V_FOX, V_SB, V_SWA, V_DSA, V_IW, V_COLS = 0, 256, 512, 640, 704, 708
V_PAD = 768

TOPK = 256
BAND = 2 * P
T5_LINE = 384
N_BUCKETS = 32
PICKED = -3e38
UNSEEN = -2e38

GROUPS, PER_GROUP, EXPERTS, FF = 4, 8, 32, 512
MAX_BLOCKS = 48
SLOTS = (MAX_BLOCKS + 2) * P
ZERO_BLOCKS = 10


@contextmanager
def semaphores(nc):
    made = []

    def sem(name):
        made.append(nc.alloc_semaphore(name))
        return made[-1]

    yield sem
    nc.clear_and_free_semaphores(made)
    nc.all_engine_barrier()




def multiply(pe, out, lhs, rhs):
    for k, ((a_hi, a_lo), (b_hi, b_lo)) in enumerate(zip(lhs, rhs)):
        pe.matmul(out, a_hi, b_hi, start=(k == 0), stop=False)
        pe.matmul(out, a_hi, b_lo, start=False, stop=False)
        last = pe.matmul(out, a_lo, b_hi, start=False, stop=(k == len(lhs) - 1))
    return last


def near_blocks(i):
    return list(range(max(0, i - 1), i + 1))


def all_blocks(i):
    return list(range(i + 1))


def build(nc, a, out):
    def dram(name, shape, dt=F32):
        return nc.dram_tensor(name, shape, dt, kind="Internal").ap()

    qkh = dram("qkh", (QK_CHUNKS * P, T))
    qkl = dram("qkl", (QK_CHUNKS * P, T))
    vtok = dram("vtok", (T, V_COLS))
    gatesT = dram("gatesT", (4 * KC, P, T))
    crow = dram("crow", (2, NH, 4, T))
    t5line = dram("t5line", (2, NH, T5_LINE))
    t5tile = dram("t5tile", (2 * NH, P, BAND))
    otok = dram("otok", (T, D))
    mergedT = dram("mergedT", (KC, P, T))
    x2d = dram("x2d", (T, D))
    h2d = dram("h2d", (T, D))
    slot_tok = dram("slot_tok", (SLOTS, 1), I32)
    ybd = dram("ybd", (SLOTS, D))

    with ExitStack() as top:
        ident = top.enter_context(nc.sbuf_tensor("ident", [P, P], F32))
        lg = top.enter_context(nc.sbuf_tensor("lg", [P, NT, 36], F32))
        with ExitStack() as mem:
            selm = mem.enter_context(nc.sbuf_tensor("selm", [P, sum(range(3, NT + 1)), P], F32))
            sel_at = {i: sum(range(3, i + 1)) for i in range(2, NT)}
            with ExitStack() as early:
                hT = [early.enter_context(nc.sbuf_tensor(f"hT{n}", [P, KC, T], FR)) for n in ("_hi", "_lo")]
                iw = early.enter_context(nc.sbuf_tensor("iw", [P, NT, NH], F32))
                norm_input(nc, a, ident, hT)
                project(nc, a, hT, iw, qkh, qkl, vtok)
                select_and_gate(nc, a, hT, iw, selm, sel_at, qkh, qkl, gatesT, crow, t5line, t5tile, ybd)
            attention(nc, a, ident, selm, sel_at, qkh, qkl, vtok, crow, t5tile, otok)
        merge(nc, a, ident, otok, gatesT, mergedT)
        output_and_router(nc, a, ident, lg, mergedT, x2d, h2d)
        pos = [top.enter_context(nc.sbuf_tensor(f"pos{k}", [P, NT], I32)) for k in range(2)]
        gate = [top.enter_context(nc.sbuf_tensor(f"gate{k}", [P, NT], F32)) for k in range(2)]
        eblk = top.enter_context(nc.sbuf_tensor("eblk", [1, MAX_BLOCKS + 2], I32))
        pairs = top.enter_context(nc.sbuf_tensor("pairs", [1, 1], I32))
        route(nc, a, lg, pos, gate, eblk, pairs, slot_tok)
        experts(nc, a, ident, eblk, pairs, slot_tok, h2d, ybd)
        combine(nc, pos, gate, x2d, ybd, out)


def norm_input(nc, a, ident, hT):
    x = a["x"]
    with ExitStack() as c:
        sb = lambda n, s, d=F32: c.enter_context(nc.sbuf_tensor(n, s, d))
        sem = c.enter_context(semaphores(nc))
        xt = [sb(f"ni_x{s}", [P, D]) for s in range(2)]
        xn = [sb(f"ni_xn{s}", [P, D]) for s in range(2)]
        junk = [sb(f"ni_junk{s}", [P, D]) for s in range(2)]
        ss = [sb(f"ni_ss{s}", [P, 1]) for s in range(2)]
        sd = [sb(f"ni_sd{s}", [P, 1]) for s in range(2)]
        rs = [sb(f"ni_rs{s}", [P, 1]) for s in range(2)]
        g = sb("ni_g", [P, KC])
        hf = [sb(f"ni_hf{s}", [P, KC, P]) for s in range(2)]
        pt = [c.enter_context(nc.psum_tensor(f"ni_pt{s}", [P, KC, P], F32)) for s in range(2)]
        x_loaded = [sem(f"ni_x_loaded{s}") for s in range(2)]
        g_loaded = sem("ni_g_loaded")
        ident_done = sem("ni_ident_done")
        squared = sem("ni_squared")
        rooted = sem("ni_rooted")
        inverted = sem("ni_inverted")
        scaled = sem("ni_scaled")
        turned = sem("ni_turned")
        stored = sem("ni_stored")
        parted = sem("ni_parted")
        block = c.enter_context(nc.Block())

        @block.sync
        def _(sp):
            sp.dma_start(g[:, :], a["norm_mix_g"]).then_inc(g_loaded, 16)
            with sp.Fori(0, NT // 2) as it:
                for s in range(2):
                    sp.wait_ge(scaled, it * 2 + s + 1)
                    sp.dma_start(xt[s][:, :], x[bass.ds(it * 2 + s, 1)].rearrange("a p f -> p (a f)")).then_inc(x_loaded[s], 16)

        @block.gpsimd
        def _(pool):
            pool.memset(ident[:, :], 0.0).then_inc(ident_done, 1)
            pool.wait_ge(ident_done, 1)
            pool.affine_select(out=ident[:, :], in_=ident[:, :], compare_op=ALU.not_equal, fill=1.0, base=0,
                               pattern=[[-1, P]], channel_multiplier=1).then_inc(ident_done, 1)

        @block.scalar
        def _(act):
            with act.Fori(0, NT // 2) as it:
                for s in range(2):
                    act.wait_ge(x_loaded[s], it * 16 + 16)
                    act.activation(junk[s][:, :], xt[s][:, :], ACT.Square, accum_out=ss[s][:, :]).then_inc(squared, 1)
                    act.wait_ge(squared, it * 2 + s + 1)
                    act.activation(sd[s][:, :], ss[s][:, :], ACT.Sqrt, scale=1.0 / D, bias=EPS).then_inc(rooted, 1)

        @block.vector
        def _(dve):
            dve.sem_inc(scaled, 2)
            dve.sem_inc(stored, 2)
            dve.sem_inc(parted, 4)
            dve.wait_ge(g_loaded, 16)
            with dve.Fori(0, NT // 2) as it:
                for s in range(2):
                    dve.wait_ge(rooted, it * 2 + s + 1)
                    dve.reciprocal(rs[s][:, :], sd[s][:, :]).then_inc(inverted, 1)
                    dve.wait_ge(inverted, it * 2 + s + 1)
                    dve.wait_ge(turned, it * 2 + s + 1)
                    dve.tensor_scalar(xn[s][:, :], xt[s][:, :], rs[s][:, 0:1], None, ALU.mult).then_inc(scaled, 1)
                for s in range(2):
                    dve.wait_ge(turned, it * 2 + s + 1 + 2)
                    dve.wait_ge(parted, it * 4 + s * 2 + 2)
                    hi = hT[0][:, :, bass.ds((it * 2 + s) * P, P)]
                    lo = hT[1][:, :, bass.ds((it * 2 + s) * P, P)]
                    dve.tensor_tensor(hf[s][:, :, :], pt[s][:, :, :], g[:, :].unsqueeze(2).to_broadcast([P, KC, P]),
                                      ALU.mult).then_inc(stored, 1)
                    dve.wait_ge(stored, it * 2 + s + 1 + 2)
                    dve.tensor_scalar(hi, hf[s][:, :, :], 1.0, None, ALU.mult).then_inc(parted, 1)
                    dve.wait_ge(parted, it * 4 + s * 2 + 1 + 4)
                    dve.tensor_tensor(lo, hf[s][:, :, :], hi.bitcast(F32), ALU.subtract).then_inc(parted, 1)

        @block.tensor
        def _(pe):
            pe.sem_inc(turned, 2)
            pe.wait_ge(ident_done, 2)
            with pe.Fori(0, NT // 2) as it:
                for s in range(2):
                    pe.wait_ge(scaled, it * 2 + s + 1 + 2)
                    pe.wait_ge(stored, it * 2 + s + 1)
                    for k in range(KC):
                        last = pe.transpose(pt[s][:, k, :], xn[s][:, k * P:(k + 1) * P], ident[:, :])
                    last.then_inc(turned, 1)


def project(nc, a, hT, iw, qkh, qkl, vtok):
    outs = [t.rearrange("(c p) t -> c p t", p=P) for t in (qkh, qkl)]
    pieces = QK_CHUNKS + KC
    with ExitStack() as c:
        sb = lambda n, s, d=F32: c.enter_context(nc.sbuf_tensor(n, s, d))
        sem = c.enter_context(semaphores(nc))
        raw = [sb(f"pj_raw{s}", [P, KC * P]) for s in range(2)]
        wh = [sb(f"pj_wh{s}", [P, KC, P], FR) for s in range(2)]
        wl = [sb(f"pj_wl{s}", [P, KC, P], FR) for s in range(2)]
        vh = sb("pj_vh", [P, KC, V_PAD], FR)
        vl = sb("pj_vl", [P, KC, V_PAD], FR)
        gc = sb("pj_gain", [P, QK_CHUNKS])
        heads_mean = sb("pj_heads_mean", [P, P])
        sq = [sb(f"pj_sq{h}", [P, HALF]) for h in range(2)]
        sd = [sb(f"pj_sd{h}", [P, HALF]) for h in range(2)]
        rc = [sb(f"pj_rc{h}", [P, HALF]) for h in range(2)]
        ob = [sb(f"pj_out{s}", [P, T]) for s in range(2)]
        oh = [sb(f"pj_oh{s}", [P, T], FR) for s in range(2)]
        ol = [sb(f"pj_ol{s}", [P, T], FR) for s in range(2)]
        ps = [[c.enter_context(nc.psum_tensor(f"pj_ps{s}{h}", [P, HALF], F32)) for h in range(2)] for s in range(2)]
        nps = [c.enter_context(nc.psum_tensor(f"pj_nps{h}", [P, HALF], F32)) for h in range(2)]
        w_loaded = [sem(f"pj_w_loaded{s}") for s in range(2)]
        w_high = sem("pj_w_high")
        w_low = sem("pj_w_low")
        gain_loaded = sem("pj_gain_loaded")
        gain_done = sem("pj_gain_done")
        mean_done = sem("pj_mean_done")
        multiplied = sem("pj_multiplied")
        squared = sem("pj_squared")
        averaged = sem("pj_averaged")
        rooted = sem("pj_rooted")
        inverted = sem("pj_inverted")
        evacuated = sem("pj_evacuated")
        o_high = sem("pj_o_high")
        o_low = sem("pj_o_low")
        iw_done = sem("pj_iw_done")
        stored = [sem(f"pj_stored{s}") for s in range(2)]
        v_stored = [sem(f"pj_v_stored{s}") for s in range(2)]
        block = c.enter_context(nc.Block())
        SPLIT_LOOPS = ((0, NORMED // 2), (NORMED // 2, 7))

        @block.sync
        def _(sp):
            def load(k, s):
                sp.wait_ge(w_low, k + 1)
                sp.dma_start(raw[s][:, :], a["w_qk"][bass.ds(k, 1)].rearrange("a p n -> p (a n)")).then_inc(w_loaded[s], 16)

            def load_v(k):
                sp.wait_ge(w_low, QK_CHUNKS + k + 1)
                sp.dma_start(raw[(k + 1) % 2][:, 0:V_PAD], a["w_v"][k]).then_inc(w_loaded[(k + 1) % 2], 16)

            def store(k, s):
                sp.wait_ge(o_low, k + 1 + 2)
                for o, t in zip(outs, (oh, ol)):
                    sp.dma_start(o[bass.ds(k, 1)].rearrange("a p t -> p (a t)"), t[s][:, :].bitcast(F32)).then_inc(stored[s], 16)

            sp.dma_start(gc[:, :], a["gain_cols"]).then_inc(gain_loaded, 16)
            for s in range(2):
                load(s, s)
            with sp.Fori(0, 7) as it:
                for s in range(2):
                    load(it * 2 + s + 2, s)
                    store(it * 2 + s, s)
            load(16, 0)
            for k in (14, 15, 16):
                load_v(k - 14)
                store(k, k % 2)
            for k in range(3, KC):
                load_v(k)
            for t in range(NT):
                sp.wait_ge(evacuated, (QK_CHUNKS + t) * 2 + 2 + 4)
                sp.dma_start(vtok[t * P:(t + 1) * P, :], ob[(QK_CHUNKS + t) % 2][:, 0:V_COLS]).then_inc(v_stored[t % 2], 16)
            for s in range(2):
                sp.wait_ge(stored[s], 32 + 32 * (9 - s))
                sp.wait_ge(v_stored[s], 16 * NT // 2)

        @block.gpsimd
        def _(pool):
            pool.sem_inc(w_low, 2)
            pool.sem_inc(o_low, 2)
            pool.memset(heads_mean[:, :], 0.0).then_inc(mean_done, 1)
            pool.wait_ge(mean_done, 1)
            for q in range(2):
                pool.memset(heads_mean[q * HD:(q + 1) * HD, q * HD:(q + 1) * HD], 1.0 / HD).then_inc(mean_done, 1)

            def low(k, s):
                pool.wait_ge(w_high, k + 1)
                w3 = wh[s][:, :, :].rearrange("p k n -> p (k n)")
                pool.tensor_tensor(wl[s][:, :, :].rearrange("p k n -> p (k n)"), raw[s][:, :], w3.bitcast(F32),
                                   ALU.subtract).then_inc(w_low, 1)

            def low_v(k):
                pool.wait_ge(w_high, QK_CHUNKS + k + 1)
                pool.tensor_tensor(vl[:, k, :], raw[(k + 1) % 2][:, 0:V_PAD], vh[:, k, :].bitcast(F32),
                                   ALU.subtract).then_inc(w_low, 1)

            def out_low(k, s):
                pool.wait_ge(o_high, k + 1)
                pool.tensor_tensor(ol[s][:, :], ob[s][:, :], oh[s][:, :].bitcast(F32), ALU.subtract).then_inc(o_low, 1)

            pool.wait_ge(mean_done, 3)
            low(0, 0)
            low(1, 1)
            with pool.Fori(0, 7) as it:
                for s in range(2):
                    low(it * 2 + s + 2, s)
                    out_low(it * 2 + s, s)
            low(16, 0)
            for k in range(3):
                low_v(k)
                out_low(14 + k, k % 2)
            for k in range(3, KC):
                low_v(k)

        @block.scalar
        def _(act):
            def high(k, s):
                act.wait_ge(w_loaded[s], loads(k, s))
                act.wait_ge(multiplied, k * 2 + 2)
                act.activation(wh[s][:, :, :], raw[s][:, :].rearrange("p (k n) -> p k n", k=KC), ACT.Copy).then_inc(w_high, 1)

            def high_v(k):
                act.wait_ge(w_loaded[(k + 1) % 2], 16 * ((QK_CHUNKS + k) // 2 + 1))
                act.activation(vh[:, k, :], raw[(k + 1) % 2][:, 0:V_PAD], ACT.Copy).then_inc(w_high, 1)

            def loads(k, s):
                return (k - s) * 8 + 16

            def out_high(k, s):
                act.wait_ge(evacuated, k * 2 + 2 + 4)
                act.wait_ge(stored[s], (k - s) * 16 + 32)
                act.activation(oh[s][:, :], ob[s][:, :], ACT.Copy).then_inc(o_high, 1)

            high(0, 0)
            high(1, 1)
            for lo_it, hi_it in SPLIT_LOOPS:
                with act.Fori(lo_it, hi_it) as it:
                    for s in range(2):
                        k = it * 2 + s
                        if hi_it <= NORMED // 2:
                            for h in range(2):
                                act.wait_ge(multiplied, k * 2 + h + 1 + 4)
                                act.wait_ge(averaged, k * 2 + h + 1)
                                act.activation(sq[h][:, :], ps[s][h][:, :], ACT.Square).then_inc(squared, 1)
                            for h in range(2):
                                act.wait_ge(averaged, k * 2 + h + 1 + 2)
                                act.wait_ge(inverted, k * 2 + h + 1)
                                act.activation(sd[h][:, :], nps[h][:, :], ACT.Sqrt, bias=EPS).then_inc(rooted, 1)
                        act.wait_ge(w_loaded[s], it * 16 + 32)
                        act.wait_ge(multiplied, k * 2 + 2 + 4)
                        act.activation(wh[s][:, :, :], raw[s][:, :].rearrange("p (k n) -> p k n", k=KC),
                                       ACT.Copy).then_inc(w_high, 1)
                        act.wait_ge(evacuated, k * 2 + 2 + 4)
                        act.wait_ge(stored[s], it * 32 + 32)
                        act.activation(oh[s][:, :], ob[s][:, :], ACT.Copy).then_inc(o_high, 1)
            high(16, 0)
            for k in range(3):
                high_v(k)
                out_high(14 + k, k % 2)
            for k in range(3, KC):
                high_v(k)

        @block.vector
        def _(dve):
            dve.sem_inc(evacuated, 4)
            dve.sem_inc(inverted, 2)
            dve.sem_inc(stored[0], 32)
            dve.sem_inc(stored[1], 32)
            dve.wait_ge(gain_loaded, 16)
            for n, q in enumerate((SWA_Q, FOX_Q, DSA_Q)):
                dve.tensor_scalar(gc[:, q:q + 2], gc[:, q:q + 2], SCALE, None, ALU.mult).then_inc(gain_done, 1)
            dve.wait_ge(gain_done, 3)
            with dve.Fori(0, NORMED // 2) as it:
                for s in range(2):
                    for h in range(2):
                        dve.wait_ge(rooted, it * 4 + s * 2 + h + 1 + 2)
                        dve.reciprocal(rc[h][:, :], sd[h][:, :]).then_inc(inverted, 1)
                        dve.wait_ge(inverted, it * 4 + s * 2 + h + 1 + 2)
                        if h == 0:
                            dve.wait_ge(o_low, it * 2 + s + 1)
                        dve.scalar_tensor_tensor(ob[s][:, h * HALF:(h + 1) * HALF], ps[s][h][:, :],
                                                 gc[:, bass.ds(it * 2 + s, 1)], rc[h][:, :],
                                                 ALU.mult, ALU.mult).then_inc(evacuated, 1)

            def plain(k, s):
                for h in range(2):
                    dve.wait_ge(multiplied, k * 2 + h + 1 + 4)
                    if h == 0:
                        dve.wait_ge(o_low, k + 1)
                    dve.tensor_scalar(ob[s][:, h * HALF:(h + 1) * HALF], ps[s][h][:, :], gc[:, bass.ds(k, 1)], None,
                                      ALU.mult).then_inc(evacuated, 1)

            with dve.Fori(NORMED // 2, 8) as it:
                for s in range(2):
                    plain(it * 2 + s, s)
            plain(16, 0)
            for t in range(NT):
                k = QK_CHUNKS + t
                s = k % 2
                dve.wait_ge(multiplied, k * 2 + 1 + 4)
                if t < 2:
                    dve.wait_ge(o_low, k + 1)
                else:
                    dve.wait_ge(v_stored[t % 2], 16 * (t // 2))
                    dve.wait_ge(iw_done, t - 1)
                dve.tensor_copy(ob[s][:, 0:HALF], ps[s][0][:, :]).then_inc(evacuated, 1)
                dve.wait_ge(multiplied, k * 2 + 2 + 4)
                dve.tensor_copy(ob[s][:, HALF:V_COLS], ps[s][1][:, 0:V_COLS - HALF]).then_inc(evacuated, 1)
                dve.wait_ge(evacuated, k * 2 + 2 + 4)
                dve.tensor_scalar(iw[:, t, :], ob[s][:, V_IW:V_COLS], NH ** -0.5, None, ALU.mult).then_inc(iw_done, 1)

        @block.tensor
        def _(pe):
            pe.sem_inc(averaged, 2)
            pe.sem_inc(rooted, 2)
            pe.sem_inc(multiplied, 4)
            pe.wait_ge(mean_done, 3)

            def chunk(k, s):
                pe.wait_ge(w_low, k + 1 + 2)
                for h in range(2):
                    pe.wait_ge(evacuated, k * 2 + h + 1)
                    cols = slice(h * HALF, (h + 1) * HALF)
                    multiply(pe, ps[s][h][:, :], [(wh[s][:, q, :], wl[s][:, q, :]) for q in range(KC)],
                             [(hT[0][:, q, cols], hT[1][:, q, cols]) for q in range(KC)]).then_inc(multiplied, 1)

            with pe.Fori(0, NORMED // 2) as it:
                for s in range(2):
                    chunk(it * 2 + s, s)
                    for h in range(2):
                        pe.wait_ge(squared, it * 4 + s * 2 + h + 1)
                        pe.wait_ge(rooted, it * 4 + s * 2 + h + 1)
                        pe.matmul(nps[h][:, :], heads_mean[:, :], sq[h][:, :], start=True, stop=True).then_inc(averaged, 1)
            with pe.Fori(NORMED // 2, 8) as it:
                for s in range(2):
                    chunk(it * 2 + s, s)
            chunk(16, 0)
            pe.wait_ge(w_low, pieces + 2)
            for t in range(NT):
                k = QK_CHUNKS + t
                rows = slice(t * P, (t + 1) * P)
                for h, (f, n) in enumerate(((0, HALF), (HALF, V_PAD - HALF))):
                    pe.wait_ge(evacuated, k * 2 + h + 1)
                    multiply(pe, ps[k % 2][h][:, 0:n], [(hT[0][:, q, rows], hT[1][:, q, rows]) for q in range(KC)],
                             [(vh[:, q, f:f + n], vl[:, q, f:f + n]) for q in range(KC)]).then_inc(multiplied, 1)


def select_and_gate(nc, a, hT, iw, selm, sel_at, qkh, qkl, gatesT, crow, t5line, t5tile, ybd):
    with ExitStack() as c:
        sb = lambda n, s, d=F32: c.enter_context(nc.sbuf_tensor(n, s, d))
        sem = c.enter_context(semaphores(nc))
        iq = sb("sg_iq", [P, NH, T], FR)
        ik = sb("sg_ik", [P, 2, T], FR)
        fg = sb("sg_fg", [NH, T])
        fa = sb("sg_fa", [NH, T])
        fb = sb("sg_fb", [NH, T])
        fhl = sb("sg_fhl", [NH, 2, T], FR)
        neg = sb("sg_neg", [NH, 2, T], FR)
        one = sb("sg_one", [NH, T], FR)
        fbias = sb("sg_fbias", [NH, 1])
        onehot = sb("sg_onehot", [N_BUCKETS + 1, 2, T5_LINE])
        table = sb("sg_table", [N_BUCKETS + 1, 2 * NH])
        lines = sb("sg_lines", [NH, 2, T5_LINE])
        flip = sb("sg_flip", [P, P])
        reversed_ = sb("sg_reversed", [P, 2 * NH, BAND])
        t5 = sb("sg_t5", [P, 2 * NH, BAND])
        later = sb("sg_later", [P, P])
        r = [sb(f"sg_r{s}", [P, T]) for s in range(2)]
        top8 = [sb(f"sg_top8{s}", [P, 8]) for s in range(2)]
        zeros = sb("sg_zeros", [P, D])
        raw = [sb(f"sg_raw{s}", [P, KC * P]) for s in range(2)]
        wh = [sb(f"sg_wh{s}", [P, KC, P], FR) for s in range(2)]
        wl = [sb(f"sg_wl{s}", [P, KC, P], FR) for s in range(2)]
        go = [sb(f"sg_go{s}", [P, T]) for s in range(2)]
        si = [c.enter_context(nc.psum_tensor(f"sg_si{s}", [P, T], F32)) for s in range(2)]
        gp = [[c.enter_context(nc.psum_tensor(f"sg_gp{s}{h}", [P, HALF], F32)) for h in range(2)] for s in range(2)]
        zeros_made = sem("sg_zeros_made")
        zeros_stored = sem("sg_zeros_stored")
        small_loaded = sem("sg_small_loaded")
        idx_loaded = sem("sg_idx_loaded")
        table_set = sem("sg_table_set")
        lines_made = sem("sg_lines_made")
        lines_out = sem("sg_lines_out")
        lines_stored = sem("sg_lines_stored")
        reversed_loaded = sem("sg_reversed_loaded")
        tiles_flipped = sem("sg_tiles_flipped")
        tiles_made = sem("sg_tiles_made")
        tiles_stored = sem("sg_tiles_stored")
        f_act = sem("sg_f_act")
        f_dve = sem("sg_f_dve")
        c_stored = sem("sg_c_stored")
        later_done = sem("sg_later_done")
        scored = sem("sg_scored")
        rectified = sem("sg_rectified")
        added = sem("sg_added")
        picked = sem("sg_picked")
        wait_carrier = sem("sg_wait_carrier")
        w_loaded = [sem(f"sg_w_loaded{s}") for s in range(2)]
        w_high = sem("sg_w_high")
        w_low = sem("sg_w_low")
        gated = sem("sg_gated")
        sigmoided = sem("sg_sigmoided")
        g_stored = [sem(f"sg_g_stored{s}") for s in range(2)]
        units = [(i, h) for i in range(2, NT) for h in range(NH)]
        block = c.enter_context(nc.Block())

        @block.sync
        def _(sp):
            for part, qk in enumerate((qkh, qkl)):
                rows = slice(part * HD, (part + 1) * HD)
                sp.dma_start(iq[rows, :, :].bitcast(F32), qk[IDX_Q * P:(IDX_Q + 2) * P, :].rearrange("(h d) t -> d h t", d=HD)).then_inc(idx_loaded, 16)
                for half in range(2):
                    sp.dma_start(ik[half * HD:(half + 1) * HD, part, :].bitcast(F32), qk[IDX_K * P:IDX_K * P + HD, :]).then_inc(idx_loaded, 16)
                sp.dma_start(fhl[:, part, :].bitcast(F32), qk[FG_ROW:FG_ROW + NH, :]).then_inc(small_loaded, 16)
            sp.dma_start(fbias[:, :], a["forget_bias"]).then_inc(small_loaded, 16)
            sp.dma_start(onehot[:, :, :], a["t5_onehot"]).then_inc(small_loaded, 16)
            sp.dma_start(table[0:N_BUCKETS, :], a["t5_table"]).then_inc(small_loaded, 16)

            def load(k, s):
                sp.dma_start(raw[s][:, :], a["w_gate"][k].rearrange("a p n -> p (a n)")).then_inc(w_loaded[s], 16)

            def store(k, s):
                sp.wait_ge(sigmoided, k * 2 + 2 + 4)
                sp.dma_start(gatesT[bass.ds(k, 1)].rearrange("a p t -> p (a t)"), go[s][:, :]).then_inc(g_stored[s], 16)

            load(bass.ds(0, 1), 0)
            load(bass.ds(1, 1), 1)
            n = 4 * KC
            with sp.Fori(0, n // 2 - 1) as it:
                for s in range(2):
                    sp.wait_ge(w_low, it * 2 + s + 1)
                    load(bass.ds(it * 2 + s + 2, 1), s)
                    store(it * 2 + s, s)
            for s in range(2):
                store(n - 2 + s, s)
                sp.wait_ge(g_stored[s], 16 + 16 * n // 2)

        @block.gpsimd
        def _(pool):
            pool.memset(later[:, :], 0.0).then_inc(later_done, 1)
            pool.memset(flip[:, :], 0.0).then_inc(later_done, 1)
            pool.wait_ge(later_done, 2)
            pool.affine_select(out=flip[:, :], in_=flip[:, :], compare_op=ALU.not_equal, fill=1.0, base=1 - P,
                               pattern=[[1, P]], channel_multiplier=1).then_inc(later_done, 1)
            pool.affine_select(out=later[:, :], in_=later[:, :], compare_op=ALU.is_ge, fill=UNSEEN, base=0,
                               pattern=[[-1, P]], channel_multiplier=1).then_inc(later_done, 1)
            pool.memset(zeros[:, :], 0.0).then_inc(zeros_made, 1)
            pool.wait_ge(zeros_made, 1)
            for b in range(0, SLOTS // P, ZERO_BLOCKS):
                pool.dma_start(ybd.rearrange("(b p) d -> p b d", p=P)[:, b:b + ZERO_BLOCKS, :],
                               zeros[:, :].unsqueeze(1).to_broadcast([P, ZERO_BLOCKS, D])).then_inc(zeros_stored, 16)
            pool.wait_ge(lines_out, 2)
            pool.dma_start(t5line.rearrange("v h n -> h v n"), lines[:, :, :]).then_inc(lines_stored, 16)
            pool.wait_ge(lines_stored, 16)
            for v in range(2):
                for h in range(NH):
                    src = bass.AP(t5line.tensor, (v * NH + h) * T5_LINE, [[1, P], [1, BAND]])
                    pool.dma_start(reversed_[:, v * NH + h, :], src).then_inc(reversed_loaded, 16)
            pool.wait_ge(tiles_made, 4)
            pool.dma_start(t5tile.rearrange("h p k -> p h k"), t5[:, :, :]).then_inc(tiles_stored, 16)
            pool.wait_ge(f_dve, 8)
            pool.dma_start(crow[0][:, 0:2, :], fhl[:, :, :].bitcast(F32)).then_inc(c_stored, 16)
            pool.dma_start(crow[1][:, 2:4, :], neg[:, :, :].bitcast(F32)).then_inc(c_stored, 16)
            for side, first in ((0, 2), (1, 0)):
                for row in (first, first + 1):
                    pool.dma_start(crow[side][:, row, :], one[:, :].bitcast(F32)).then_inc(c_stored, 16)

            with pool.Fori(0, 2 * KC) as it:
                for s in range(2):
                    pool.wait_ge(w_high, it * 2 + s + 1)
                    w2 = wh[s][:, :, :].rearrange("p k n -> p (k n)")
                    pool.tensor_tensor(wl[s][:, :, :].rearrange("p k n -> p (k n)"), raw[s][:, :], w2.bitcast(F32),
                                       ALU.subtract).then_inc(w_low, 1)
            pool.wait_ge(c_stored, 96)
            pool.wait_ge(tiles_stored, 16)
            pool.wait_ge(zeros_stored, 16 * (SLOTS // P // ZERO_BLOCKS))

        @block.scalar
        def _(act):
            act.preload_act_table_set("natural_log_exp_and_others")
            act.wait_ge(f_dve, 1)
            act.activation(fa[:, :], fg[:, :], ACT.Abs, bias=fbias[:, 0:1]).then_inc(f_act, 1)
            act.wait_ge(f_act, 1)
            act.activation(fa[:, :], fa[:, :], ACT.Exp, scale=-1.0).then_inc(f_act, 1)
            act.wait_ge(f_act, 2)
            act.activation(fa[:, :], fa[:, :], ACT.Ln, bias=1.0).then_inc(f_act, 1)
            for u, (i, h) in enumerate(units):
                W = (i + 1) * P
                act.wait_ge(scored, u + 1)
                if u >= 2:
                    act.wait_ge(added, u - 1)
                act.activation(r[u % 2][:, 0:W], si[u % 2][:, 0:W], ACT.Relu).then_inc(rectified, 1)

            def high(s, loads, used):
                act.wait_ge(w_loaded[s], loads)
                act.wait_ge(gated, used)
                act.activation(wh[s][:, :, :], raw[s][:, :].rearrange("p (k n) -> p k n", k=KC), ACT.Copy).then_inc(w_high, 1)

            def sigmoid(k, s, stores):
                for h in range(2):
                    act.wait_ge(gated, k * 2 + h + 1 + 4)
                    if h == 0:
                        act.wait_ge(g_stored[s], stores)
                    act.activation(go[s][:, h * HALF:(h + 1) * HALF], gp[s][h][:, :], ACT.Sigmoid).then_inc(sigmoided, 1)

            high(0, 16, 2)
            high(1, 16, 4)
            with act.Fori(0, 2 * KC - 1) as it:
                for s in range(2):
                    high(s, it * 16 + 32, it * 4 + s * 2 + 2 + 4)
                    sigmoid(it * 2 + s, s, it * 16 + 16)
            for s in range(2):
                sigmoid(4 * KC - 2 + s, s, 16 * 2 * KC)

        @block.vector
        def _(dve):
            dve.memset(table[N_BUCKETS:N_BUCKETS + 1, :], NEG).then_inc(table_set, 1)
            dve.sem_inc(g_stored[0], 16)
            dve.sem_inc(g_stored[1], 16)
            dve.sem_inc(sigmoided, 4)
            dve.memset(one[:, :].bitcast(F32), 1.0).then_inc(table_set, 1)
            dve.wait_ge(small_loaded, 80)
            f32 = lambda t: t.bitcast(F32)
            dve.tensor_tensor(fg[:, :], f32(fhl[:, 0, :]), f32(fhl[:, 1, :]), ALU.add).then_inc(f_dve, 1)
            dve.wait_ge(f_dve, 1)
            dve.tensor_scalar(fb[:, :], fg[:, :], fbias[:, 0:1], 0.0, ALU.add, ALU.min).then_inc(f_dve, 1)
            dve.wait_ge(f_act, 3)
            dve.wait_ge(f_dve, 2)
            dve.tensor_tensor(fb[:, :], fb[:, :], fa[:, :], ALU.subtract).then_inc(f_dve, 1)
            dve.wait_ge(f_dve, 3)
            dve.tensor_tensor_scan(fg[:, :], fb[:, :], fb[:, :], 0.0, ALU.add, ALU.min).then_inc(f_dve, 1)
            dve.wait_ge(f_dve, 4)
            dve.tensor_scalar(fhl[:, 0, :], fg[:, :], 1.0, None, ALU.mult).then_inc(f_dve, 1)
            dve.wait_ge(f_dve, 5)
            dve.tensor_tensor(fhl[:, 1, :], fg[:, :], f32(fhl[:, 0, :]), ALU.subtract).then_inc(f_dve, 1)
            dve.wait_ge(f_dve, 6)
            for part in range(2):
                dve.tensor_scalar(neg[:, part, :], f32(fhl[:, part, :]), -1.0, None, ALU.mult).then_inc(f_dve, 1)
            dve.wait_ge(table_set, 2)
            for v in range(2):
                dve.wait_ge(lines_made, v + 1)
                dve.tensor_copy(lines[:, v, :], gp[0][v][0:NH, 0:T5_LINE]).then_inc(lines_out, 1)
            dve.wait_ge(later_done, 4)
            for u, (i, h) in enumerate(units):
                W = (i + 1) * P
                acc = selm[:, sel_at[i]:sel_at[i] + i + 1, :].rearrange("p b k -> p (b k)")
                dve.wait_ge(rectified, u + 1)
                if h == 0:
                    dve.tensor_scalar(acc, r[u % 2][:, 0:W], iw[:, i, h:h + 1], None, ALU.mult).then_inc(added, 1)
                else:
                    dve.wait_ge(added, u)
                    dve.scalar_tensor_tensor(acc, r[u % 2][:, 0:W], iw[:, i, h:h + 1], acc, ALU.mult,
                                             ALU.add).then_inc(added, 1)
            for j in range(4):
                dve.wait_ge(tiles_flipped, j + 1)
                dve.tensor_copy(t5[:, 2 * j:2 * j + 2, :].rearrange("p h k -> p (h k)"),
                                gp[j // 2][j % 2][:, :]).then_inc(tiles_made, 1)
            n = 0
            for pair in ((2, 7), (3, 6), (4, 5)):
                accs = [selm[:, sel_at[i]:sel_at[i] + i + 1, :].rearrange("p b k -> p (b k)") for i in pair]
                dve.wait_ge(added, len(units))
                for i in pair:
                    diagonal = selm[:, sel_at[i] + i, :]
                    dve.tensor_tensor(diagonal, diagonal, later[:, :], ALU.add).then_inc(picked, 1)
                n += 2
                with dve.Fori(0, TOPK // 8) as rnd:
                    for j, acc in enumerate(accs):
                        dve.wait_ge(picked, rnd * 4 + n - 1 + j)
                        dve.sem_inc(wait_carrier, 1)
                        dve.max(top8[j][:, :], acc).then_inc(picked, 1)
                    for j, acc in enumerate(accs):
                        dve.wait_ge(picked, rnd * 4 + n + 1 + j)
                        dve.sem_inc(wait_carrier, 1)
                        dve.match_replace(acc, top8[j][:, :], acc, PICKED).then_inc(picked, 1)
                n += 4 * (TOPK // 8)
                dve.wait_ge(picked, n)
                for acc in accs:
                    dve.tensor_scalar(acc, acc, (PICKED + UNSEEN) / 2, NEG, ALU.is_gt, ALU.mult).then_inc(picked, 1)
                n += 2
            dve.wait_ge(picked, n)

        @block.tensor
        def _(pe):
            pe.sem_inc(gated, 4)
            pe.wait_ge(small_loaded, 80)
            pe.wait_ge(table_set, 2)
            for v in range(2):
                pe.matmul(gp[0][v][0:NH, 0:T5_LINE], table[:, v * NH:(v + 1) * NH], onehot[:, v, :],
                          start=True, stop=True).then_inc(lines_made, 1)
            pe.wait_ge(idx_loaded, 96)
            for u, (i, h) in enumerate(units):
                if u >= 2:
                    pe.wait_ge(rectified, u - 1)
                for f in range(0, (i + 1) * P, HALF):
                    n = min(HALF, (i + 1) * P - f)
                    for part in range(2):
                        last = pe.matmul(si[u % 2][:, f:f + n], iq[:, h, i * P:(i + 1) * P], ik[:, part, f:f + n],
                                         start=(part == 0), stop=(part == 1))
                last.then_inc(scored, 1)
            pe.wait_ge(later_done, 4)
            pe.wait_ge(reversed_loaded, 16 * 2 * NH)
            for j in range(4):
                pe.matmul(gp[j // 2][j % 2][:, :], flip[:, :], reversed_[:, 2 * j:2 * j + 2, :].rearrange("p h k -> p (h k)"),
                          start=True, stop=True).then_inc(tiles_flipped, 1)
            pe.wait_ge(tiles_made, 4)
            with pe.Fori(0, 2 * KC) as it:
                for s in range(2):
                    pe.wait_ge(w_low, it * 2 + s + 1)
                    for h in range(2):
                        pe.wait_ge(sigmoided, it * 4 + s * 2 + h + 1)
                        cols = slice(h * HALF, (h + 1) * HALF)
                        multiply(pe, gp[s][h][:, :], [(wh[s][:, q, :], wl[s][:, q, :]) for q in range(KC)],
                                 [(hT[0][:, q, cols], hT[1][:, q, cols]) for q in range(KC)]).then_inc(gated, 1)


class Chain:

    def __init__(self, sem, per_iteration):
        self.sem, self.per, self.n = sem, per_iteration, 0

    def did(self, instruction):
        instruction.then_inc(self.sem, 1)
        self.n += 1

    def wait(self, engine, it):
        engine.wait_ge(self.sem, it * self.per + self.n)


def attention(nc, a, ident, selm, sel_at, qkh, qkl, vtok, crow, t5tile, otok):
    with ExitStack() as c:
        sb = lambda n, s, d=F32: c.enter_context(nc.sbuf_tensor(n, s, d))
        sem = c.enter_context(semaphores(nc))
        m = dict(
            q=[sb(f"at_q{s}", [P, T], FR) for s in range(2)],
            kh=[sb(f"at_kh{s}", [P, T], FR) for s in range(2)],
            kl=[sb(f"at_kl{s}", [P, T], FR) for s in range(2)],
            qc=[sb(f"at_qc{s}", [P, T], FR) for s in range(2)],
            v=[sb(f"at_v{s}", [P, NT, P]) for s in range(2)],
            t5=[sb(f"at_t5{s}", [P, BAND]) for s in range(2)],
            hc=[sb(f"at_hc{s}", [P, 1]) for s in range(2)],
            hcn=[sb(f"at_hcn{s}", [P, 1]) for s in range(2)],
            x=[sb(f"at_x{s}", [P, T]) for s in range(2)],
            t=[sb(f"at_t{s}", [P, T]) for s in range(2)],
            sp=sb("at_sp", [P, T]),
            pT=[sb(f"at_pT{s}", [P, NT, P]) for s in range(2)],
            o=[sb(f"at_o{s}", [P, NT, HD]) for s in range(2)],
            negmax=[sb(f"at_negmax{s}", [P, 1]) for s in range(4)],
            rawmax=[sb(f"at_rawmax{s}", [P, 1]) for s in range(2)],
            den=[sb(f"at_den{s}", [P, 1]) for s in range(4)],
            sinkp=[sb(f"at_sinkp{s}", [P, 1]) for s in range(4)],
            rden=[sb(f"at_rden{s}", [P, 1]) for s in range(2)],
            identb=sb("at_identb", [P, P], BF16),
            causal=sb("at_causal", [P, P], BF16),
            strict=sb("at_strict", [P, P], BF16),
            s_ps=[c.enter_context(nc.psum_tensor(f"at_sps{s}", [P, T], F32)) for s in range(2)],
            t_ps=[c.enter_context(nc.psum_tensor(f"at_tps{s}", [P, 4, P], F32)) for s in range(2)],
            o_ps=[c.enter_context(nc.psum_tensor(f"at_ops{s}", [P, HALF], F32)) for s in range(2)],
        )
        masks_done = sem("at_masks_done")
        zeroed = sem("at_zeroed")
        with nc.Block() as block:
            @block.gpsimd
            def _(pool):
                pool.memset(m["identb"][:, :], 0.0).then_inc(masks_done, 1)
                pool.memset(m["causal"][:, :], 0.0).then_inc(masks_done, 1)
                pool.memset(m["strict"][:, :], 0.0).then_inc(masks_done, 1)
                pool.wait_ge(masks_done, 3)
                pool.affine_select(out=m["identb"][:, :], in_=m["identb"][:, :], compare_op=ALU.not_equal, fill=1.0,
                                   base=0, pattern=[[-1, P]], channel_multiplier=1).then_inc(masks_done, 1)
                pool.affine_select(out=m["causal"][:, :], in_=m["causal"][:, :], compare_op=ALU.is_ge, fill=NEG,
                                   base=0, pattern=[[-1, P]], channel_multiplier=1).then_inc(masks_done, 1)
                pool.affine_select(out=m["strict"][:, :], in_=m["strict"][:, :], compare_op=ALU.is_gt, fill=NEG,
                                   base=0, pattern=[[-1, P]], channel_multiplier=1).then_inc(masks_done, 1)
                pool.wait_ge(masks_done, 6)

            @block.vector
            def _(dve):
                for s in range(2):
                    dve.memset(m["v"][s][:, :, HD:P], 0.0).then_inc(zeroed, 1)
                    for k in ("qc", "kl"):
                        dve.memset(m[k][s][HD:P, :].bitcast(F32), 0.0).then_inc(zeroed, 1)
                dve.wait_ge(zeroed, 6)

        for kind in ("fox", "sb", "dsa", "swa"):
            mixer(nc, a, kind, m, ident, selm, sel_at, qkh, qkl, vtok, crow, t5tile, otok)


def mixer(nc, a, kind, m, ident, selm, sel_at, qkh, qkl, vtok, crow, t5tile, otok):
    units = [(i, s) for i in range(NT) for s in range(2)]
    N = len(units)
    keys = near_blocks if kind == "swa" else all_blocks
    groups, first_group = [], []
    for u, (i, s) in enumerate(units):
        first_group.append(len(groups))
        ks = keys(i)
        groups += [(u, g, min(4, len(ks) - g)) for g in range(0, len(ks), 4)]
    first_group.append(len(groups))
    NG = len(groups)
    act_turns = kind in ("dsa", "swa")
    q_row = {"fox": FOX_Q, "sb": SB_Q, "dsa": DSA_Q, "swa": SWA_Q}[kind] * P
    k_row = {"fox": FOX_K, "sb": SB_K, "dsa": DSA_K, "swa": SWA_K}[kind] * P
    v_col = {"fox": V_FOX, "sb": V_SB, "dsa": V_DSA, "swa": V_SWA}[kind]
    branch = {"swa": 0, "fox": 1, "sb": 2, "dsa": 3}[kind]
    kv_of = lambda h: {"dsa": 0, "swa": h // 2}.get(kind, h)
    n_loads = {"fox": 8, "sb": 6, "dsa": 8, "swa": 8}[kind]
    x, t = m["x"], m["t"]

    with ExitStack() as c:
        new = c.enter_context(semaphores(nc))
        sem = lambda n: new(f"{kind}_{n}")
        qk_loaded = [sem(f"qk_loaded{s}") for s in range(2)]
        v_loaded = [sem(f"v_loaded{s}") for s in range(2)]
        logits = sem("logits")
        soft = sem("soft")
        shaped = sem("shaped")
        weighed = sem("weighed")
        turned = sem("turned")
        copied = sem("copied")
        summed = sem("summed")
        finished = sem("finished")
        stored = [sem(f"stored{s}") for s in range(2)]
        dve_chain = sem("dve_chain")
        act_chain = sem("act_chain")
        block = c.enter_context(nc.Block())

        def group_end(u):
            return first_group[u + 1]

        def copy_turned(engine, it, u):
            for g in range(first_group[u], first_group[u + 1]):
                _, b, n = groups[g]
                engine.wait_ge(turned, it * NG + g + 1 + lead)
                if b == 0:
                    engine.wait_ge(summed, it * N + u + 1)
                src, dst = m["t_ps"][g % 2][:, 0:n, :], m["pT"][u % 2][:, b:b + n, :]
                if act_turns:
                    ins = engine.activation(dst, src, ACT.Copy)
                else:
                    ins = engine.tensor_copy(dst, src)
                ins.then_inc(copied, 1)

        lead = NG - first_group[N - 2]

        def free_weights(engine, it, u):
            if u >= 2:
                engine.wait_ge(turned, it * NG + first_group[u - 1] + lead)
            else:
                engine.wait_ge(turned, it * NG + (0 if u == 1 else first_group[N - 1] - NG) + lead)

        @block.sync
        def _(sp):
            def load(h, s):
                hh = kv_of(h)
                q = [d[q_row + h * HD:q_row + (h + 1) * HD, :] for d in (qkh, qkl)]
                k = [d[k_row + hh * HD:k_row + (hh + 1) * HD, :] for d in (qkh, qkl)]
                for half in range(2):
                    rows = slice(half * HD, (half + 1) * HD)
                    sp.dma_start(m["q"][s][rows, :].bitcast(F32), q[half]).then_inc(qk_loaded[s], 16)
                    sp.dma_start(m["kh"][s][rows, :].bitcast(F32), k[0]).then_inc(qk_loaded[s], 16)
                    if kind != "fox":
                        sp.dma_start(m["kl"][s][rows, :].bitcast(F32), k[1]).then_inc(qk_loaded[s], 16)
                if kind == "fox":
                    sp.dma_start(m["qc"][s][0:HD, :].bitcast(F32), q[0]).then_inc(qk_loaded[s], 16)
                    sp.dma_start(m["kl"][s][0:HD, :].bitcast(F32), k[1]).then_inc(qk_loaded[s], 16)
                    for side, n in enumerate(("qc", "kl")):
                        sp.dma_start(m[n][s][HD:HD + 4, :].bitcast(F32), crow[side, h]).then_inc(qk_loaded[s], 16)
                if kind in ("dsa", "swa"):
                    sp.dma_start(m["t5"][s][:, :], t5tile[(NH if kind == "dsa" else 0) + h]).then_inc(qk_loaded[s], 16)
                    col = a["t5_table"][N_BUCKETS - 1:N_BUCKETS, NH + h:NH + h + 1] if kind == "dsa" else a["attn_sinks"][0:1, h:h + 1]
                    sp.dma_start(m["hc"][s][:, :], col.to_broadcast([P, 1])).then_inc(qk_loaded[s], 16)
                sp.dma_start(m["v"][s][:, :, 0:HD], vtok[:, v_col + hh * HD:v_col + (hh + 1) * HD].rearrange(
                    "(b p) d -> p b d", p=P)).then_inc(v_loaded[s], 16)

            for s in range(2):
                load(s, s)
            for it in range(2):
                for s in range(2):
                    h = it * 2 + s
                    sp.wait_ge(finished, it * N + N - 1 + s + 2)
                    sp.dma_start(otok[:, branch * 256 + h * HD:branch * 256 + (h + 1) * HD].rearrange(
                        "(b p) d -> p b d", p=P), m["o"][s][:, :, :]).then_inc(stored[s], 16)
                    if it == 0:
                        load(h + 2, s)
            for s in range(2):
                sp.wait_ge(stored[s], 16 + 32)

        @block.scalar
        def _(act):
            act.preload_act_table_set("natural_log_exp_and_others")
            if kind == "sb":
                chain = Chain(act_chain, 2 * N)
            if kind == "swa":
                chain = Chain(act_chain, N)

            def soften(it, u):
                W = (units[u][0] + 1) * P
                z, y = m["s_ps"][u % 2], t[u % 2]
                act.wait_ge(logits, it * N + u + 1)
                act.wait_ge(shaped, it * N + u + 1)
                chain.did(act.activation(y[:, 0:W], z[:, 0:W], ACT.Abs))
                chain.wait(act, it)
                chain.did(act.activation(y[:, 0:W], y[:, 0:W], ACT.Exp, scale=-1.0))
                chain.wait(act, it)
                act.activation(y[:, 0:W], y[:, 0:W], ACT.Ln, bias=1.0).then_inc(soft, 1)

            def weigh(it, u):
                W = len(keys(units[u][0])) * P
                act.wait_ge(shaped, it * N + u + 1 + 2)
                if kind == "sb":
                    act.activation(x[u % 2][:, 0:W], x[u % 2][:, 0:W], ACT.Exp).then_inc(weighed, 1)
                    return
                nm = m["negmax"][u % 4][:, 0:1]
                if kind == "swa":
                    chain.did(act.activation(m["sinkp"][u % 4][:, :], m["hc"][units[u][1]][:, :], ACT.Exp, bias=nm))
                if kind == "fox":
                    free_weights(act, it, u)
                src = m["s_ps"][u % 2] if kind == "fox" else x[u % 2]
                act.activation(x[u % 2][:, 0:W], src[:, 0:W], ACT.Exp, bias=nm,
                               accum_out=m["den"][u % 4][:, :]).then_inc(weighed, 1)

            with act.Fori(0, 2) as it:
                if kind in ("sb", "swa"):
                    chain.n = 0
                for u in range(N + 2):
                    if kind == "sb" and u < N:
                        soften(it, u)
                    if 1 <= u <= N:
                        weigh(it, u - 1)
                    if act_turns and u >= 2:
                        copy_turned(act, it, u - 2)

        @block.vector
        def _(dve):
            dve.sem_inc(shaped, 2)
            dve.sem_inc(finished, 2)
            dve.sem_inc(stored[0], 16)
            dve.sem_inc(stored[1], 16)
            if not act_turns:
                dve.sem_inc(copied, 2)

            def ops_of(u):
                i = units[u][0]
                return {"fox": 1, "sb": 3, "swa": 4,
                        "dsa": 2 if i < 2 else 4}[kind] - (1 if kind == "sb" else 0)

            per = sum(ops_of(u) for u in range(N)) + (2 if kind == "swa" else 0)
            chain = Chain(dve_chain, per)

            def shape(it, u):
                i, s = units[u]
                W = len(keys(i)) * P
                S, X = m["s_ps"][u % 2], x[u % 2]
                T5 = m["t5"][s]
                dve.wait_ge(logits, it * N + u + 1)
                if kind == "fox":
                    dve.tensor_reduce(m["negmax"][u % 4][:, :], S[:, 0:W], AX, ALU.max, negate=True).then_inc(shaped, 1)
                    return
                free_weights(dve, it, u)
                if kind == "sb":
                    dve.wait_ge(soft, it * N + u + 1)
                    chain.did(dve.scalar_tensor_tensor(m["sp"][:, 0:W], S[:, 0:W], 0.0, t[u % 2][:, 0:W],
                                                       ALU.max, ALU.add))
                    chain.wait(dve, it)
                    sp = m["sp"][:, 0:W][:, ::-1]
                    chain.did(dve.tensor_tensor_scan(X[:, 0:W][:, ::-1],
                                                     sp, sp, 0.0,
                                                     ALU.add, ALU.max))
                    chain.wait(dve, it)
                    dve.tensor_tensor(X[:, 0:W], S[:, 0:W], X[:, 0:W], ALU.subtract).then_inc(shaped, 1)
                    return
                n0 = 0 if i == 0 else W - BAND
                band = T5[:, P:] if i == 0 else T5[:, :]
                if kind == "dsa" and i >= 2:
                    sel = selm[:, sel_at[i]:sel_at[i] + i + 1, :].rearrange("p b k -> p (b k)")
                    chain.did(dve.scalar_tensor_tensor(X[:, 0:n0], S[:, 0:n0], m["hc"][s][:, 0:1], sel[:, 0:n0],
                                                       ALU.add, ALU.add))
                chain.did(dve.tensor_tensor(X[:, n0:W], S[:, n0:W], band, ALU.add))
                if kind == "dsa" and i >= 2:
                    chain.wait(dve, it)
                    chain.did(dve.tensor_tensor(X[:, n0:W], X[:, n0:W], sel[:, n0:W], ALU.add))
                chain.wait(dve, it)
                if kind == "dsa":
                    dve.tensor_reduce(m["negmax"][u % 4][:, :], X[:, 0:W], AX, ALU.max, negate=True).then_inc(shaped, 1)
                else:
                    chain.did(dve.tensor_reduce(m["rawmax"][u % 2][:, :], X[:, 0:W], AX, ALU.max, negate=True))
                    chain.wait(dve, it)
                    dve.tensor_tensor(m["negmax"][u % 4][:, :], m["rawmax"][u % 2][:, :], m["hcn"][s][:, :],
                                      ALU.min).then_inc(shaped, 1)

            def finish(it, u):
                i, s = units[u]
                O = m["o_ps"][u % 2][:, 0:HD]
                if kind != "sb":
                    dve.wait_ge(weighed, it * N + u + 1 + 2)
                    if kind == "swa":
                        chain.did(dve.tensor_tensor(m["den"][u % 4][:, :], m["den"][u % 4][:, :],
                                                    m["sinkp"][u % 4][:, :], ALU.add))
                        chain.wait(dve, it)
                    chain.did(dve.reciprocal(m["rden"][u % 2][:, :], m["den"][u % 4][:, :]))
                    chain.wait(dve, it)
                dve.wait_ge(summed, it * N + u + 1 + 2)
                if i == 0:
                    dve.wait_ge(stored[s], it * 16 + 16)
                if kind == "sb":
                    dve.tensor_copy(m["o"][s][:, i, :], O).then_inc(finished, 1)
                else:
                    dve.tensor_scalar(m["o"][s][:, i, :], O, m["rden"][u % 2][:, 0:1], None,
                                      ALU.mult).then_inc(finished, 1)

            with dve.Fori(0, 2) as it:
                if kind == "swa":
                    for s in range(2):
                        dve.wait_ge(qk_loaded[s], it * 16 * n_loads + 16 * n_loads)
                        chain.did(dve.tensor_scalar(m["hcn"][s][:, :], m["hc"][s][:, :], -1.0, None, ALU.mult))
                    chain.wait(dve, it)
                if kind == "dsa":
                    for s in range(2):
                        dve.wait_ge(qk_loaded[s], it * 16 * n_loads + 16 * n_loads)
                for u in range(N + 3):
                    if u < N:
                        shape(it, u)
                    if not act_turns and 2 <= u < N + 2:
                        copy_turned(dve, it, u - 2)
                    if u >= 3:
                        finish(it, u - 3)
                assert chain.n == per, (kind, chain.n, per)

        @block.tensor
        def _(pe):
            pe.sem_inc(turned, lead)
            pe.sem_inc(summed, 2)
            if act_turns:
                pe.sem_inc(copied, 2)
            pe.sem_inc(weighed, 2)

            def score(it, u):
                i, s = units[u]
                if i == 0:
                    pe.wait_ge(qk_loaded[s], it * 16 * n_loads + 16 * n_loads)
                pe.wait_ge(weighed if kind == "fox" else shaped, it * N + u + 1)
                k0 = keys(i)[0] * P
                W = len(keys(i)) * P
                products = ((m["q"][s], m["kh"][s]), (m["qc" if kind == "fox" else "q"][s], m["kl"][s]))
                for f in range(0, W, HALF):
                    n = min(HALF, W - f)
                    masked = kind in ("fox", "sb") and f + n == W
                    if masked:
                        mask = m["causal"] if kind == "fox" else m["strict"]
                        pe.matmul(m["s_ps"][u % 2][:, W - P:W], m["identb"][:, :], mask[:, :],
                                  start=True, stop=False, skip_group_check=True)
                    for j, (q, k) in enumerate(products):
                        last = pe.matmul(m["s_ps"][u % 2][:, f:f + n], q[:, i * P:(i + 1) * P], k[:, k0 + f:k0 + f + n],
                                         start=(j == 0 and not masked), stop=(j == 1), skip_group_check=masked)
                last.then_inc(logits, 1)

            def turn(it, u):
                pe.wait_ge(weighed, it * N + u + 1 + 2)
                for g in range(first_group[u], first_group[u + 1]):
                    _, b, n = groups[g]
                    pe.wait_ge(copied, it * NG + g + 1)
                    for j in range(n):
                        last = pe.transpose(m["t_ps"][g % 2][:, j, :], x[u % 2][:, (b + j) * P:(b + j + 1) * P],
                                            ident[:, :])
                    last.then_inc(turned, 1)

            def apply(it, u):
                i, s = units[u]
                if i == 0:
                    pe.wait_ge(v_loaded[s], it * 16 + 16)
                pe.wait_ge(copied, it * NG + group_end(u) + 2)
                pe.wait_ge(finished, it * N + u + 1)
                ks = keys(i)
                for j, kb in enumerate(ks):
                    last = pe.matmul(m["o_ps"][u % 2][:, 0:P], m["pT"][u % 2][:, j, :], m["v"][s][:, kb, :],
                                     start=(j == 0), stop=(j == len(ks) - 1))
                last.then_inc(summed, 1)

            with pe.Fori(0, 2) as it:
                score(it, 0)
                for u in range(N + 2):
                    if u + 1 < N:
                        score(it, u + 1)
                    if 1 <= u <= N:
                        turn(it, u - 1)
                    if u >= 2:
                        apply(it, u - 2)


def merge(nc, a, ident, otok, gatesT, mergedT):
    with ExitStack() as c:
        sb = lambda n, s, d=F32: c.enter_context(nc.sbuf_tensor(n, s, d))
        sem = c.enter_context(semaphores(nc))
        ot = [sb(f"mg_ot{s}", [P, D]) for s in range(2)]
        oT = sb("mg_oT", [P, KC, T])
        wt = [sb(f"mg_w{s}", [P, 4, 2, P]) for s in range(2)]
        gt = [sb(f"mg_g{s}", [P, 4, T]) for s in range(2)]
        mt = [sb(f"mg_m{s}", [P, T]) for s in range(2)]
        tmp = [sb(f"mg_tmp{s}", [P, HALF]) for s in range(2)]
        pt = [c.enter_context(nc.psum_tensor(f"mg_pt{s}", [P, KC, P], F32)) for s in range(2)]
        ps = [c.enter_context(nc.psum_tensor(f"mg_ps{s}", [P, HALF], F32)) for s in range(4)]
        o_loaded = [sem(f"mg_o_loaded{s}") for s in range(2)]
        turned = sem("mg_turned")
        copied = sem("mg_copied")
        wg_loaded = [sem(f"mg_wg_loaded{s}") for s in range(2)]
        multiplied = sem("mg_multiplied")
        gated = sem("mg_gated")
        added = sem("mg_added")
        stored = [sem(f"mg_stored{s}") for s in range(2)]
        block = c.enter_context(nc.Block())
        oview = otok.rearrange("(t p) d -> t p d", p=P)

        @block.sync
        def _(sp):
            def load(k, s):
                sp.dma_start(wt[s][:, :, :, :], a["w_br"][k].rearrange("a p b k n -> p (a b) k n")).then_inc(wg_loaded[s], 16)
                sp.dma_start(gt[s][:, :, :], gatesT.rearrange("(c b) p t -> c p b t", b=4)[k].rearrange(
                    "a p b t -> p (a b) t")).then_inc(wg_loaded[s], 16)

            def store(k, s):
                sp.wait_ge(added, k * 6 + 6)
                sp.dma_start(mergedT[bass.ds(k, 1)].rearrange("a p t -> p (a t)"), mt[s][:, :]).then_inc(stored[s], 16)

            with sp.Fori(0, NT // 2) as it:
                for s in range(2):
                    sp.wait_ge(turned, it * 2 + s + 1)
                    sp.dma_start(ot[s][:, :], oview[bass.ds(it * 2 + s, 1)].rearrange("a p d -> p (a d)")).then_inc(o_loaded[s], 16)
            load(bass.ds(0, 1), 0)
            load(bass.ds(1, 1), 1)
            with sp.Fori(0, KC // 2 - 1) as it:
                for s in range(2):
                    sp.wait_ge(gated, it * 16 + s * 8 + 8 + 4)
                    load(bass.ds(it * 2 + s + 2, 1), s)
                    store(it * 2 + s, s)
            for s in range(2):
                store(KC - 2 + s, s)
                sp.wait_ge(stored[s], 16 + 16 * KC // 2)

        @block.scalar
        def _(act):
            act.sem_inc(copied, 2)
            with act.Fori(0, NT // 2) as it:
                for s in range(2):
                    act.wait_ge(turned, it * 2 + s + 1 + 2)
                    act.wait_ge(copied, it * 2 + s + 1 + 1)
                    act.activation(oT[:, :, bass.ds((it * 2 + s) * P, P)], pt[s][:, :, :], ACT.Copy).then_inc(copied, 1)

        @block.vector
        def _(dve):
            dve.sem_inc(gated, 4)
            dve.sem_inc(stored[0], 16)
            dve.sem_inc(stored[1], 16)
            with dve.Fori(0, KC // 2) as it:
                for s in range(2):
                    dve.wait_ge(wg_loaded[s], it * 32 + 32)
                    dve.wait_ge(stored[s], it * 16 + 16)
                    for b in range(4):
                        for h in range(2):
                            n = b * 2 + h
                            na = (b - 1) * 2 + h
                            cols = slice(h * HALF, (h + 1) * HALF)
                            dve.wait_ge(multiplied, it * 16 + s * 8 + n + 1)
                            if b == 0:
                                dve.tensor_tensor(mt[s][:, cols], ps[n % 4][:, :], gt[s][:, b, cols],
                                                  ALU.mult).then_inc(gated, 1)
                                continue
                            dve.tensor_tensor(tmp[h][:, :], ps[n % 4][:, :], gt[s][:, b, cols], ALU.mult).then_inc(gated, 1)
                            dve.wait_ge(gated, it * 16 + s * 8 + n + 1 + 4)
                            if b > 1:
                                dve.wait_ge(added, it * 12 + s * 6 + na - 1)
                            dve.tensor_tensor(mt[s][:, cols], mt[s][:, cols], tmp[h][:, :], ALU.add).then_inc(added, 1)

        @block.tensor
        def _(pe):
            pe.sem_inc(turned, 2)
            with pe.Fori(0, NT // 2) as it:
                for s in range(2):
                    pe.wait_ge(o_loaded[s], it * 16 + 16)
                    pe.wait_ge(copied, it * 2 + s + 1)
                    for k in range(KC):
                        last = pe.transpose(pt[s][:, k, :], ot[s][:, k * P:(k + 1) * P], ident[:, :])
                    last.then_inc(turned, 1)
            pe.wait_ge(copied, NT + 2)
            with pe.Fori(0, KC // 2) as it:
                for s in range(2):
                    pe.wait_ge(wg_loaded[s], it * 32 + 32)
                    for b in range(4):
                        for h in range(2):
                            n = b * 2 + h
                            pe.wait_ge(gated, it * 16 + s * 8 + n + 1)
                            for k in range(2):
                                last = pe.matmul(ps[n % 4][:, :], wt[s][:, b, k, :],
                                                 oT[:, 2 * b + k, h * HALF:(h + 1) * HALF], start=(k == 0), stop=(k == 1))
                            last.then_inc(multiplied, 1)


def output_and_router(nc, a, ident, lg, mergedT, x2d, h2d):
    x = a["x"]
    with ExitStack() as c:
        sb = lambda n, s, d=F32: c.enter_context(nc.sbuf_tensor(n, s, d))
        sem = c.enter_context(semaphores(nc))
        wo = sb("or_wo", [P, KC, D])
        wr = sb("or_wr", [P, KC, P])
        br = sb("or_br", [P, 36])
        g = sb("or_g", [P, D])
        mt = [sb(f"or_mt{s}", [P, KC, P]) for s in range(2)]
        xt = [sb(f"or_x{s}", [P, D]) for s in range(2)]
        x2 = [sb(f"or_x2{s}", [P, D]) for s in range(2)]
        h2 = [sb(f"or_h2{s}", [P, D]) for s in range(2)]
        hT = [sb(f"or_hT{s}", [P, KC, P]) for s in range(2)]
        junk = sb("or_junk", [P, D])
        ss = [sb(f"or_ss{s}", [P, 1]) for s in range(2)]
        sd = [sb(f"or_sd{s}", [P, 1]) for s in range(2)]
        rs = [sb(f"or_rs{s}", [P, 1]) for s in range(2)]
        yp = [c.enter_context(nc.psum_tensor(f"or_yp{s}", [P, D], F32)) for s in range(2)]
        tp = c.enter_context(nc.psum_tensor("or_tp", [P, KC, P], F32))
        lp = [c.enter_context(nc.psum_tensor(f"or_lp{s}", [P, HALF], F32)) for s in range(2)]
        w_loaded = sem("or_w_loaded")
        loaded = [sem(f"or_loaded{s}") for s in range(2)]
        multiplied = sem("or_multiplied")
        summed = sem("or_summed")
        squared = sem("or_squared")
        rooted = sem("or_rooted")
        inverted = sem("or_inverted")
        normed = sem("or_normed")
        turned = sem("or_turned")
        copied = sem("or_copied")
        routed = sem("or_routed")
        logged = sem("or_logged")
        x2_stored = [sem(f"or_x2_stored{s}") for s in range(2)]
        h2_stored = [sem(f"or_h2_stored{s}") for s in range(2)]
        block = c.enter_context(nc.Block())
        tiles = lambda t: t.rearrange("(t p) d -> t p d", p=P)
        n_it = NT // 2

        @block.sync
        def _(sp):
            sp.dma_start(wo[:, :, :], a["w_out"]).then_inc(w_loaded, 16)
            sp.dma_start(wr[:, :, :], a["w_router"]).then_inc(w_loaded, 16)
            sp.dma_start(br[:, :], a["b_router"].to_broadcast([P, 36])).then_inc(w_loaded, 16)
            sp.dma_start(g[:, :], a["norm_ffn_g"].to_broadcast([P, D])).then_inc(w_loaded, 16)

            def load(it):
                for s in range(2):
                    sp.wait_ge(summed, it * 2 + s + 1)
                    sp.dma_start(mt[s][:, :, :], mergedT[:, :, bass.ds((it * 2 + s) * P, P)].rearrange(
                        "k p t -> p k t")).then_inc(loaded[s], 16)
                    sp.dma_start(xt[s][:, :], x[bass.ds(it * 2 + s, 1)].rearrange("a p d -> p (a d)")).then_inc(loaded[s], 16)

            def store(it):
                for s in range(2):
                    sp.wait_ge(summed, it * 2 + s + 1 + 2)
                    sp.dma_start(tiles(x2d)[bass.ds(it * 2 + s, 1)].rearrange("a p d -> p (a d)"), x2[s][:, :]).then_inc(x2_stored[s], 16)
                for s in range(2):
                    sp.wait_ge(normed, it * 2 + s + 1 + 2)
                    sp.dma_start(tiles(h2d)[bass.ds(it * 2 + s, 1)].rearrange("a p d -> p (a d)"), h2[s][:, :]).then_inc(h2_stored[s], 16)

            load(0)
            with sp.Fori(0, n_it - 1) as it:
                load(it + 1)
                store(it)
            store(n_it - 1)
            for s in range(2):
                sp.wait_ge(x2_stored[s], 16 + 16 * n_it)
                sp.wait_ge(h2_stored[s], 16 + 16 * n_it)

        @block.scalar
        def _(act):
            with act.Fori(0, n_it) as it:
                for s in range(2):
                    act.wait_ge(summed, it * 2 + s + 1 + 2)
                    act.activation(junk[:, :], x2[s][:, :], ACT.Square, accum_out=ss[s][:, :]).then_inc(squared, 1)
                    act.wait_ge(squared, it * 2 + s + 1)
                    act.activation(sd[s][:, :], ss[s][:, :], ACT.Sqrt, scale=1.0 / D, bias=EPS).then_inc(rooted, 1)
                for s in range(2):
                    act.wait_ge(turned, it * 2 + s + 1 + 2)
                    act.wait_ge(routed, it * 2 + s + 1)
                    act.activation(hT[s][:, :, :], tp[:, :, :], ACT.Copy).then_inc(copied, 1)

        @block.vector
        def _(dve):
            dve.sem_inc(summed, 2)
            dve.sem_inc(normed, 2)
            dve.sem_inc(logged, 2)
            for s in range(2):
                dve.sem_inc(x2_stored[s], 16)
                dve.sem_inc(h2_stored[s], 16)
            dve.wait_ge(w_loaded, 64)
            with dve.Fori(0, n_it) as it:
                for s in range(2):
                    dve.wait_ge(multiplied, it * 2 + s + 1)
                    dve.wait_ge(x2_stored[s], it * 16 + 16)
                    dve.tensor_tensor(x2[s][:, :], yp[s][:, :], xt[s][:, :], ALU.add).then_inc(summed, 1)
                for s in range(2):
                    dve.wait_ge(rooted, it * 2 + s + 1)
                    dve.reciprocal(rs[s][:, :], sd[s][:, :]).then_inc(inverted, 1)
                    dve.wait_ge(inverted, it * 2 + s + 1)
                    dve.wait_ge(h2_stored[s], it * 16 + 16)
                    dve.wait_ge(turned, it * 2 + s + 1)
                    dve.scalar_tensor_tensor(h2[s][:, :], x2[s][:, :], rs[s][:, 0:1], g[:, :], ALU.mult,
                                             ALU.mult).then_inc(normed, 1)
                for s in range(2):
                    dve.wait_ge(routed, it * 2 + s + 1 + 2)
                    dve.tensor_tensor(lg[:, bass.ds(it * 2 + s, 1), :].rearrange("p a n -> p (a n)"), lp[s][:, 0:36],
                                      br[:, :], ALU.add).then_inc(logged, 1)

        @block.tensor
        def _(pe):
            pe.sem_inc(copied, 1)
            pe.sem_inc(turned, 2)
            pe.sem_inc(routed, 2)
            pe.wait_ge(w_loaded, 64)
            with pe.Fori(0, n_it) as it:
                for s in range(2):
                    pe.wait_ge(loaded[s], it * 32 + 32)
                    pe.wait_ge(summed, it * 2 + s + 1)
                    for h in range(2):
                        for k in range(KC):
                            last = pe.matmul(yp[s][:, h * HALF:(h + 1) * HALF], mt[s][:, k, :],
                                             wo[:, k, h * HALF:(h + 1) * HALF], start=(k == 0), stop=(k == KC - 1))
                    last.then_inc(multiplied, 1)
                for s in range(2):
                    pe.wait_ge(normed, it * 2 + s + 1 + 2)
                    pe.wait_ge(copied, it * 2 + s + 1)
                    for k in range(KC):
                        last = pe.transpose(tp[:, k, :], h2[s][:, k * P:(k + 1) * P], ident[:, :])
                    last.then_inc(turned, 1)
                for s in range(2):
                    pe.wait_ge(copied, it * 2 + s + 1 + 1)
                    pe.wait_ge(logged, it * 2 + s + 1)
                    for k in range(KC):
                        last = pe.matmul(lp[s][:, 0:P], hT[s][:, k, :], wr[:, k, :], start=(k == 0), stop=(k == KC - 1))
                    last.then_inc(routed, 1)


def route(nc, a, lg, pos, gate, eblk, pairs, slot_tok):
    with ExitStack() as c:
        sb = lambda n, s, d=F32: c.enter_context(nc.sbuf_tensor(n, s, d))
        sem = c.enter_context(semaphores(nc))
        E8 = [P, NT, PER_GROUP]
        rank4 = sb("rt_rank4", [P, GROUPS])
        rank8 = sb("rt_rank8", [P, PER_GROUP])
        gs = sb("rt_gs", [P, NT, GROUPS])
        gsc = sb("rt_gsc", [P, NT, GROUPS])
        goh = sb("rt_goh", [P, NT, GROUPS])
        m1 = sb("rt_m1", [P, NT, 1])
        m2 = sb("rt_m2", [P, NT, 1])
        gsum = sb("rt_gsum", [P, NT, 1])
        pg = sb("rt_pg", [P, NT, 1])
        ein = sb("rt_ein", E8)
        etmp = sb("rt_etmp", E8)
        esc = sb("rt_esc", E8)
        eoh = [sb(f"rt_eoh{k}", E8) for k in range(2)]
        ratio = sb("rt_ratio", [P, NT, 1])
        rsum = sb("rt_rsum", [P, NT, 1])
        rinv = sb("rt_rinv", [P, NT, 1])
        full = [sb(f"rt_full{k}", [P, NT, EXPERTS]) for k in range(2)]
        both = sb("rt_both", [P, NT, EXPERTS], BF16)
        ones = sb("rt_ones", [P, P], BF16)
        before = sb("rt_before", [P, P], BF16)
        prefix = sb("rt_prefix", [P, NT + 1, EXPERTS])
        steps = sb("rt_steps", [P, NT])
        cmp = sb("rt_cmp", [P, EXPERTS, NT])
        nblk = sb("rt_nblk", [P, EXPERTS])
        bend = sb("rt_bend", [P, EXPERTS])
        base = sb("rt_base", [P, EXPERTS])
        slot = sb("rt_slot", [P, NT, EXPERTS])
        prod = sb("rt_prod", [P, NT, EXPERTS])
        posf = sb("rt_posf", [P, NT, 1])
        bidx = sb("rt_bidx", [1, MAX_BLOCKS + 2])
        bcmp = sb("rt_bcmp", [1, MAX_BLOCKS + 2, EXPERTS])
        ebf = sb("rt_ebf", [1, MAX_BLOCKS + 2, 1])
        half = sb("rt_half", [1, 1])
        halfc = sb("rt_halfc", [1, MAX_BLOCKS // 2])
        evens = sb("rt_evens", [1, MAX_BLOCKS // 2])
        tok = sb("rt_tok", [P, NT], I32)
        zero = sb("rt_zero", [P, SLOTS // P], I32)
        ranks = c.enter_context(nc.psum_tensor("rt_ranks", [P, NT, EXPERTS], F32))
        sums = c.enter_context(nc.psum_tensor("rt_sums", [P, NT, EXPERTS], F32))
        consts = sem("rt_consts")
        d = sem("rt_d")
        e_done = sem("rt_e_done")
        ranked = sem("rt_ranked")
        zeroed = sem("rt_zeroed")
        scattered = sem("rt_scattered")
        block = c.enter_context(nc.Block())
        marks = {}

        @block.vector
        def _(dve):
            n = [0]

            def step(ins):
                n[0] += 1
                ins.then_inc(d, 1)
                dve.wait_ge(d, n[0])

            bc = lambda ap, shape: ap.to_broadcast(shape)
            row = lambda ap, k: ap.unsqueeze(1).to_broadcast([P, NT, k])
            G4 = [P, NT, GROUPS]
            dve.wait_ge(consts, 7)
            g = lg[:, :, 0:GROUPS]
            step(dve.tensor_reduce(m1[:, :, :], g, AX, ALU.max))
            step(dve.tensor_tensor(gs[:, :, :], g, bc(m1[:, :, :], G4), ALU.subtract))
            marks["group"] = n[0]
            dve.wait_ge(e_done, 1)
            step(dve.tensor_reduce(gsum[:, :, :], gsc[:, :, :], AX, ALU.add))
            step(dve.reciprocal(pg[:, :, :], gsum[:, :, :]))

            def first_max(oh, scores, peak, rank, work, k):
                step(dve.tensor_tensor(work, scores, bc(peak, [P, NT, k]), ALU.is_equal))
                step(dve.tensor_tensor(work, work, row(rank, k), ALU.mult))
                step(dve.tensor_reduce(peak, work, AX, ALU.max))
                step(dve.tensor_tensor(oh, work, bc(peak, [P, NT, k]), ALU.is_equal))

            first_max(goh[:, :, :], g, m1[:, :, :], rank4[:, :], gsc[:, :, :], GROUPS)
            for q in range(GROUPS):
                e = lg[:, :, GROUPS + q * PER_GROUP:GROUPS + (q + 1) * PER_GROUP]
                dst = ein if q == 0 else etmp
                step(dve.tensor_tensor(dst[:, :, :], e, bc(goh[:, :, q:q + 1], E8), ALU.mult))
                if q:
                    step(dve.tensor_tensor(ein[:, :, :], ein[:, :, :], etmp[:, :, :], ALU.add))
            step(dve.tensor_reduce(m1[:, :, :], ein[:, :, :], AX, ALU.max))
            step(dve.tensor_copy(ratio[:, :, :], m1[:, :, :]))
            first_max(eoh[0][:, :, :], ein[:, :, :], m1[:, :, :], rank8[:, :], esc[:, :, :], PER_GROUP)
            step(dve.scalar_tensor_tensor(ein[:, :, :], eoh[0][:, :, :], PICKED, ein[:, :, :], ALU.mult, ALU.add))
            step(dve.tensor_reduce(m2[:, :, :], ein[:, :, :], AX, ALU.max))
            step(dve.tensor_tensor(ratio[:, :, :], m2[:, :, :], ratio[:, :, :], ALU.subtract))
            marks["ratio"] = n[0]
            first_max(eoh[1][:, :, :], ein[:, :, :], m2[:, :, :], rank8[:, :], esc[:, :, :], PER_GROUP)
            dve.wait_ge(e_done, 2)
            step(dve.tensor_scalar(rsum[:, :, :], rinv[:, :, :], 1.0, None, ALU.add))
            step(dve.reciprocal(rsum[:, :, :], rsum[:, :, :]))
            step(dve.tensor_tensor(gate[0][:, :].unsqueeze(2), pg[:, :, :], rsum[:, :, :], ALU.mult))
            step(dve.tensor_tensor(gate[1][:, :].unsqueeze(2), gate[0][:, :].unsqueeze(2), rinv[:, :, :], ALU.mult))
            for k in range(2):
                for q in range(GROUPS):
                    step(dve.tensor_tensor(full[k][:, :, q * PER_GROUP:(q + 1) * PER_GROUP], eoh[k][:, :, :],
                                           bc(goh[:, :, q:q + 1], E8), ALU.mult))
            step(dve.tensor_tensor(both[:, :, :], full[0][:, :, :], full[1][:, :, :], ALU.add))
            marks["both"] = n[0]
            dve.wait_ge(ranked, 2)
            step(dve.memset(prefix[:, 0, :], 0.0))
            for t in range(NT):
                step(dve.tensor_tensor(prefix[:, t + 1, :], sums[:, t, :], prefix[:, t, :], ALU.add))
            S = [P, EXPERTS, NT]
            step(dve.tensor_tensor(cmp[:, :, :], prefix[:, NT, :].unsqueeze(2).to_broadcast(S),
                                   steps[:, :].unsqueeze(1).to_broadcast(S), ALU.is_gt))
            step(dve.tensor_reduce(nblk[:, :].unsqueeze(2), cmp[:, :, :], AX, ALU.add))
            step(dve.tensor_tensor_scan(bend[:, :], nblk[:, :], nblk[:, :], 0.0, ALU.add, ALU.max))
            step(dve.tensor_tensor(base[:, :], bend[:, :], nblk[:, :], ALU.subtract))
            step(dve.tensor_scalar(base[:, :], base[:, :], float(P), None, ALU.mult))
            step(dve.tensor_tensor(slot[:, :, :], ranks[:, :, :], prefix[:, 0:NT, :], ALU.add))
            step(dve.tensor_tensor(slot[:, :, :], slot[:, :, :], base[:, :].unsqueeze(1).to_broadcast([P, NT, EXPERTS]), ALU.add))
            for k in range(2):
                step(dve.tensor_tensor(prod[:, :, :], full[k][:, :, :], slot[:, :, :], ALU.mult))
                step(dve.tensor_reduce(posf[:, :, :], prod[:, :, :], AX, ALU.add))
                step(dve.tensor_copy(pos[k][:, :].unsqueeze(2), posf[:, :, :]))
            marks["pos"] = n[0]
            B = [1, MAX_BLOCKS + 2, EXPERTS]
            step(dve.tensor_tensor(bcmp[:, :, :], bend[0:1, :].unsqueeze(1).to_broadcast(B),
                                   bidx[:, :].unsqueeze(2).to_broadcast(B), ALU.is_le))
            step(dve.tensor_reduce(ebf[:, :, :], bcmp[:, :, :], AX, ALU.add))
            step(dve.tensor_scalar(eblk[:, :].unsqueeze(2), ebf[:, :, :], float(EXPERTS - 1), None, ALU.min))
            step(dve.tensor_tensor(halfc[:, :], bend[0:1, EXPERTS - 1:EXPERTS].to_broadcast([1, MAX_BLOCKS // 2]),
                                   evens[:, :], ALU.is_gt))
            step(dve.tensor_reduce(half[:, :], halfc[:, :], AX, ALU.add))
            step(dve.tensor_scalar(pairs[:, :], half[:, :], -1.0, None, ALU.add))

        @block.scalar
        def _(act):
            act.wait_ge(d, marks["group"])
            act.activation(gsc[:, :, :], gs[:, :, :], ACT.Exp).then_inc(e_done, 1)
            act.wait_ge(d, marks["ratio"])
            act.activation(rinv[:, :, :], ratio[:, :, :], ACT.Exp).then_inc(e_done, 1)

        @block.tensor
        def _(pe):
            pe.wait_ge(consts, 7)
            pe.wait_ge(d, marks["both"])
            m = both[:, :, :].rearrange("p t e -> p (t e)")
            pe.matmul(ranks[:, :, :].rearrange("p t e -> p (t e)"), before[:, :], m, start=True, stop=True).then_inc(ranked, 1)
            pe.matmul(sums[:, :, :].rearrange("p t e -> p (t e)"), ones[:, :], m, start=True, stop=True).then_inc(ranked, 1)

        @block.gpsimd
        def _(pool):
            k = [0]

            def const(ins):
                k[0] += 1
                ins.then_inc(consts, 1)

            F = dict(allow_small_or_imprecise_dtypes=True)
            pool.memset(before[:, :], 1.0).then_inc(zeroed, 1)
            pool.memset(zero[:, :], 0).then_inc(zeroed, 1)
            pool.wait_ge(zeroed, 2)
            const(pool.affine_select(out=before[:, :], in_=before[:, :], compare_op=ALU.is_gt, fill=0.0, base=0,
                                     pattern=[[1, P]], channel_multiplier=-1))
            const(pool.memset(ones[:, :], 1.0))
            const(pool.iota(rank4[:, :], pattern=[[-1, GROUPS]], base=GROUPS, channel_multiplier=0, **F))
            const(pool.iota(rank8[:, :], pattern=[[-1, PER_GROUP]], base=PER_GROUP, channel_multiplier=0, **F))
            const(pool.iota(steps[:, :], pattern=[[P, NT]], base=0, channel_multiplier=0, **F))
            const(pool.iota(bidx[:, :], pattern=[[1, MAX_BLOCKS + 2]], base=0, channel_multiplier=0, **F))
            const(pool.iota(evens[:, :], pattern=[[2, MAX_BLOCKS // 2]], base=0, channel_multiplier=0, **F))
            const(pool.iota(tok[:, :], pattern=[[P, NT]], base=0, channel_multiplier=1))
            pool.dma_start(slot_tok.rearrange("(p n) a -> p (n a)", p=P), zero[:, :]).then_inc(scattered, 16)
            pool.wait_ge(scattered, 16)
            pool.wait_ge(consts, 8)
            pool.wait_ge(d, marks["pos"])
            for q in range(2):
                for t in range(NT):
                    pool.indirect_dma_start(slot_tok[:, :], bass.IndirectOffsetOnAxis(ap=pos[q][:, t:t + 1], axis=0),
                                            tok[:, t:t + 1], None).then_inc(scattered, 16)
            pool.wait_ge(scattered, 16 + 16 * 2 * NT)


def experts(nc, a, ident, eblk, pairs, slot_tok, h2d, ybd):
    with ExitStack() as c:
        sb = lambda n, s, d=F32: c.enter_context(nc.sbuf_tensor(n, s, d))
        sem = c.enter_context(semaphores(nc))
        FC = FF // P
        PIECES, RING, GROUP = KC + FC, 6, 4
        raw = [sb(f"ex_raw{g}", [P, GROUP, D]) for g in range(6)]
        wh = [sb(f"ex_wh{r}", [P, D], FR) for r in range(RING)]
        wl = [sb(f"ex_wl{r}", [P, D], FR) for r in range(RING)]
        ids = [sb(f"ex_ids{s}", [P, 1], I32) for s in range(2)]
        xg = [sb(f"ex_xg{s}", [P, D]) for s in range(2)]
        xh = [sb(f"ex_xh{s}", [P, KC, P], FR) for s in range(2)]
        xl = [sb(f"ex_xl{s}", [P, KC, P], FR) for s in range(2)]
        gl = [sb(f"ex_gl{s}", [P, FF]) for s in range(2)]
        act_ = [sb(f"ex_act{s}", [P, FF]) for s in range(2)]
        ah = [sb(f"ex_ah{s}", [P, FC, P], FR) for s in range(2)]
        al = [sb(f"ex_al{s}", [P, FC, P], FR) for s in range(2)]
        yo = [sb(f"ex_yo{s}", [P, D]) for s in range(2)]
        xp = c.enter_context(nc.psum_tensor("ex_xp", [P, KC, P], F32))
        gp = c.enter_context(nc.psum_tensor("ex_gp", [P, FF], F32))
        upp = c.enter_context(nc.psum_tensor("ex_upp", [P, FF], F32))
        ap_ = c.enter_context(nc.psum_tensor("ex_ap", [P, FC, P], F32))
        yp = c.enter_context(nc.psum_tensor("ex_yp", [P, D], F32))
        w_loaded = [sem(f"ex_w_loaded{g}") for g in range(6)]
        ids_loaded = [sem(f"ex_ids_loaded{s}") for s in range(2)]
        gathered = [sem(f"ex_gathered{s}") for s in range(2)]
        wait_carrier = sem("ex_wait_carrier")
        w_high = sem("ex_w_high")
        low_dve = sem("ex_low_dve")
        low_pool = sem("ex_low_pool")
        used = sem("ex_used")
        x_turned = sem("ex_x_turned")
        x_high = sem("ex_x_high")
        x_low = sem("ex_x_low")
        g_made = sem("ex_g_made")
        silu_done = sem("ex_silu_done")
        act_made = sem("ex_act_made")
        a_turned = sem("ex_a_turned")
        a_high = sem("ex_a_high")
        a_low = sem("ex_a_low")
        y_copied = sem("ex_y_copied")
        stored = [sem(f"ex_stored{s}") for s in range(2)]
        block = c.enter_context(nc.Block())
        upv = a["w_expert_up"].rearrange("e (k p) f -> e p k f", p=P)
        downv = a["w_expert_down"].rearrange("e (k p) f -> e p k f", p=P)
        yv = ybd.rearrange("(b p) d -> b p d", p=P)
        sv = slot_tok.rearrange("(b p) a -> b p a", p=P)
        trips = lambda eng: eng.value_load(pairs[0:1, 0:1], min_val=7, max_val=MAX_BLOCKS // 2 - 1)

        POOL_PIECES = (1, 4, 7, 10)
        DVE_PIECES = tuple(q for q in range(PIECES) if q not in POOL_PIECES)
        upto = lambda pieces, q: sum(1 for p in pieces if p <= q)
        FIRST = 4
        DVE_CREDITS = 2 * len(DVE_PIECES) - (len(DVE_PIECES) - upto(DVE_PIECES, FIRST - 1))
        POOL_CREDITS = 2 * len(POOL_PIECES) - (len(POOL_PIECES) - upto(POOL_PIECES, FIRST - 1))

        def piece_number(b, q):
            return b * PIECES + q + 1 + PIECES - FIRST

        def lows(b, q):
            if q in POOL_PIECES:
                return low_pool, b * len(POOL_PIECES) + upto(POOL_PIECES, q) + 2 * len(POOL_PIECES)
            return low_dve, b * len(DVE_PIECES) + upto(DVE_PIECES, q) + 2 * len(DVE_PIECES)

        SKIPPED = KC
        SKIPPED_DVE, SKIPPED_POOL = upto(DVE_PIECES, KC - 1), upto(POOL_PIECES, KC - 1)

        @block.sync
        def _(sp):
            n = trips(sp)
            expert = lambda b: sp.value_load(eblk[0:1, bass.ds(b, 1)], min_val=0, max_val=EXPERTS - 1)

            def load(g, view, e, k):
                sp.dma_start(raw[g][:, :, :], view[bass.ds(e, 1), :, k:k + GROUP, :].rearrange(
                    "a p k f -> p (a k) f")).then_inc(w_loaded[g], 16)

            def wait_free(b, j):
                q = j * GROUP + GROUP - 1
                sp.wait_ge(low_dve, b * len(DVE_PIECES) + upto(DVE_PIECES, q))
                sp.sem_inc(wait_carrier, 1)
                sp.wait_ge(low_pool, b * len(POOL_PIECES) + upto(POOL_PIECES, q))

            e = expert(0)
            load(4, upv, e, 0)
            load(5, upv, e, GROUP)

            def step(b, s):
                e = expert(b + 1)
                for j in range(2):
                    wait_free(b, j)
                    load(s * 3 + j, upv, e, j * GROUP)
                e = expert(b)
                wait_free(b, 2)
                load(s * 3 + 2, downv, e, 0)

            with sp.Fori(0, n) as it:
                for s in range(2):
                    step(it * 2 + s, s)
            step(n * 2, 0)
            e = expert(n * 2 + 1)
            wait_free(n * 2 + 1, 2)
            load(5, downv, e, 0)

        @block.gpsimd
        def _(pool):
            n = trips(pool)
            pool.sem_inc(low_pool, POOL_CREDITS)

            def gather(s, loads):
                pool.wait_ge(ids_loaded[s], loads)
                pool.sem_inc(wait_carrier, 1)
                pool.indirect_dma_start(xg[s][:, :], None, h2d[:, :],
                                        bass.IndirectOffsetOnAxis(ap=ids[s][:, 0:1], axis=0)).then_inc(gathered[s], 16)

            def low(b, s, q, skipped=0):
                if q not in POOL_PIECES:
                    return
                pool.wait_ge(w_high, piece_number(b, q) - skipped)
                r = q % RING
                pool.tensor_tensor(wl[r][:, :], raw[s * 3 + q // GROUP][:, q % GROUP, :], wh[r][:, :].bitcast(F32),
                                   ALU.subtract).then_inc(low_pool, 1)

            gather(0, 16)
            gather(1, 16)
            pool.wait_ge(x_turned, 1)
            gather(0, 32)
            for q in range(FIRST, PIECES):
                low(-1, 1, q)
            for q in range(RING):
                low(0, 0, q)
            with pool.Fori(0, n) as it:
                for s in range(2):
                    b = it * 2 + s
                    for q in range(RING, PIECES):
                        low(b, s, q)
                    for q in range(RING):
                        low(b + 1, 1 - s, q)
                    pool.wait_ge(x_turned, b + 2)
                    pool.sem_inc(wait_carrier, 1)
                    gather(1 - s, it * 16 + 32 + 16 * s)
            for q in range(RING, PIECES):
                low(n * 2, 0, q)
            for q in range(KC, PIECES):
                low(n * 2 + 1, 1, q, SKIPPED)
            for s in range(2):
                pool.wait_ge(gathered[s], n * 16 + 16 + 16 * (1 - s))
                pool.sem_inc(wait_carrier, 1)

        @block.scalar
        def _(act):
            n = trips(act)

            def high(b, s, q, loads):
                if q % GROUP == 0:
                    act.wait_ge(w_loaded[s * 3 + q // GROUP], loads)
                act.wait_ge(used, piece_number(b, q))
                act.activation(wh[q % RING][:, :], raw[s * 3 + q // GROUP][:, q % GROUP, :], ACT.Copy).then_inc(w_high, 1)

            def loads(it, s, q):
                return it * 16 + (32 if s * 3 + q // GROUP >= 4 else 16)

            def x_hi(b, s):
                act.wait_ge(x_turned, b + 1)
                act.activation(xh[s][:, :, :], xp[:, :, :], ACT.Copy).then_inc(x_high, 1)

            def silu(b, s):
                act.wait_ge(g_made, b + 1)
                act.activation(gl[s][:, :], gp[:, :], ACT.Silu).then_inc(silu_done, 1)

            def output(b, s, products, it):
                act.wait_ge(used, products + RING)
                act.wait_ge(stored[s], it * 16 + 16)
                act.activation(yo[s][:, :], yp[:, :], ACT.Copy).then_inc(y_copied, 1)
                act.wait_ge(y_copied, b + 1 + 1)
                act.dma_start(yv[bass.ds(b, 1)].rearrange("a p d -> p (a d)"), yo[s][:, :]).then_inc(stored[s], 16)

            def load_ids(b, s):
                act.dma_start(ids[s][:, :], sv[bass.ds(b, 1)].rearrange("a p n -> p (a n)")).then_inc(ids_loaded[s], 16)

            load_ids(0, 0)
            load_ids(1, 1)
            x_hi(0, 0)
            act.wait_ge(gathered[0], 16)
            load_ids(2, 0)
            for q in range(FIRST, PIECES):
                high(-1, 1, q, 16)
            silu(0, 0)
            x_hi(1, 1)
            for q in range(RING):
                high(0, 0, q, 16)
            with act.Fori(0, n) as it:
                for s in range(2):
                    b = it * 2 + s
                    for q in range(RING, PIECES):
                        high(b, s, q, loads(it, s, q))
                    silu(b + 1, 1 - s)
                    x_hi(b + 2, s)
                    act.wait_ge(gathered[1 - s], it * 16 + 16 + 16 * s)
                    load_ids(b + 3, 1 - s)
                    for q in range(RING):
                        high(b + 1, 1 - s, q, loads(it + s, 1 - s, q))
                    output(b, s, piece_number(b, PIECES - 1), it)
            for q in range(RING, PIECES):
                high(n * 2, 0, q, loads(n, 0, q))
            silu(n * 2 + 1, 1)
            act.wait_ge(w_loaded[5], n * 16 + 32)
            for q in range(KC, PIECES):
                act.wait_ge(used, piece_number(n * 2, q) + RING)
                act.activation(wh[q % RING][:, :], raw[5][:, q % GROUP, :], ACT.Copy).then_inc(w_high, 1)
            output(n * 2, 0, piece_number(n * 2, PIECES - 1), n)
            output(n * 2 + 1, 1, piece_number(n * 2 + 1, PIECES - 1) - SKIPPED, n)
            for s in range(2):
                act.wait_ge(stored[s], n * 16 + 32)
                act.sem_inc(wait_carrier, 1)

        @block.vector
        def _(dve):
            n = trips(dve)
            dve.sem_inc(low_dve, DVE_CREDITS)
            for s in range(2):
                dve.sem_inc(stored[s], 16)

            def low(b, s, q, skipped=0):
                if q not in DVE_PIECES:
                    return
                dve.wait_ge(w_high, piece_number(b, q) - skipped)
                r = q % RING
                dve.tensor_tensor(wl[r][:, :], raw[s * 3 + q // GROUP][:, q % GROUP, :], wh[r][:, :].bitcast(F32),
                                  ALU.subtract).then_inc(low_dve, 1)

            def x_lo(b, s):
                dve.wait_ge(x_high, b + 1)
                dve.tensor_tensor(xl[s][:, :, :], xp[:, :, :], xh[s][:, :, :].bitcast(F32), ALU.subtract).then_inc(x_low, 1)

            def gate_up(b, s, products):
                dve.wait_ge(silu_done, b + 1)
                dve.wait_ge(used, products + RING)
                dve.tensor_tensor(act_[s][:, :], upp[:, :], gl[s][:, :], ALU.mult).then_inc(act_made, 1)

            def a_parts(b, s):
                dve.wait_ge(a_turned, b + 1)
                dve.tensor_copy(ah[s][:, :, :], ap_[:, :, :]).then_inc(a_high, 1)
                dve.wait_ge(a_high, b + 1)
                dve.tensor_tensor(al[s][:, :, :], ap_[:, :, :], ah[s][:, :, :].bitcast(F32), ALU.subtract).then_inc(a_low, 1)

            x_lo(0, 0)
            for q in range(FIRST, PIECES):
                low(-1, 1, q)
            gate_up(0, 0, KC)
            x_lo(1, 1)
            for q in range(RING):
                low(0, 0, q)
            a_parts(0, 0)
            with dve.Fori(0, n) as it:
                for s in range(2):
                    b = it * 2 + s
                    for q in range(RING, PIECES):
                        low(b, s, q)
                    gate_up(b + 1, 1 - s, piece_number(b, KC - 1))
                    x_lo(b + 2, s)
                    for q in range(RING):
                        low(b + 1, 1 - s, q)
                    a_parts(b + 1, 1 - s)
            for q in range(RING, PIECES):
                low(n * 2, 0, q)
            gate_up(n * 2 + 1, 1, piece_number(n * 2, KC - 1))
            for q in range(KC, PIECES):
                low(n * 2 + 1, 1, q, SKIPPED)
            a_parts(n * 2 + 1, 1)

        @block.tensor
        def _(pe):
            n = trips(pe)
            pe.sem_inc(used, RING)
            pe.sem_inc(y_copied, 1)

            def turn_x(b, s, loads):
                pe.wait_ge(gathered[s], loads)
                if not isinstance(b, int) or b > 0:
                    pe.wait_ge(x_low, b)
                for k in range(KC):
                    last = pe.transpose(xp[:, k, :], xg[s][:, k * P:(k + 1) * P], ident[:, :])
                last.then_inc(x_turned, 1)

            def piece(b, q, banks, left, k, last_k, made=None, skipped=(0, 0)):
                sem_, value = lows(b, q)
                pe.wait_ge(sem_, value - skipped[0 if sem_ is low_dve else 1])
                hi, lo = left
                r = q % RING
                for j, bank in enumerate(banks):
                    cols = slice(j * HALF, (j + 1) * HALF)
                    pe.matmul(bank, hi[:, k, :], wh[r][:, cols], start=(k == 0), stop=False)
                    pe.matmul(bank, hi[:, k, :], wl[r][:, cols], start=False, stop=False)
                    last = pe.matmul(bank, lo[:, k, :], wh[r][:, cols], start=False, stop=(k == last_k))
                    if made is not None and j == 0:
                        last.then_inc(made, 1)
                last.then_inc(used, 1)

            def up(b, s, step, first):
                for k in range(KC):
                    if k == 0:
                        pe.wait_ge(x_low, b + 1)
                        if first == 0:
                            pe.wait_ge(act_made, b)
                    piece(step, first + k, (gp[:, :], upp[:, :]), (xh[s], xl[s]), k, KC - 1,
                          made=g_made if k == KC - 1 else None)

            def down(b, s, skipped=(0, 0)):
                pe.wait_ge(a_low, b + 1)
                pe.wait_ge(y_copied, b + 1)
                for k in range(FC):
                    piece(b, KC + k, (yp[:, 0:HALF], yp[:, HALF:D]), (ah[s], al[s]), k, FC - 1, skipped=skipped)

            def turn_a(b, s):
                pe.wait_ge(act_made, b + 1)
                for k in range(FC):
                    last = pe.transpose(ap_[:, k, :], act_[s][:, k * P:(k + 1) * P], ident[:, :])
                last.then_inc(a_turned, 1)

            turn_x(0, 0, 16)
            up(0, 0, -1, FIRST)
            turn_x(1, 1, 16)
            turn_a(0, 0)
            with pe.Fori(0, n) as it:
                for s in range(2):
                    b = it * 2 + s
                    up(b + 1, 1 - s, b, 0)
                    turn_x(b + 2, s, it * 16 + 32)
                    down(b, s)
                    turn_a(b + 1, 1 - s)
            up(n * 2 + 1, 1, n * 2, 0)
            down(n * 2, 0)
            turn_a(n * 2 + 1, 1)
            down(n * 2 + 1, 1, (SKIPPED_DVE, SKIPPED_POOL))


def combine(nc, pos, gate, x2d, ybd, out):
    with ExitStack() as c:
        sb = lambda n, s, d=F32: c.enter_context(nc.sbuf_tensor(n, s, d))
        sem = c.enter_context(semaphores(nc))
        xt = [sb(f"cb_x{t}", [P, D]) for t in range(NT)]
        y = [[sb(f"cb_y{t}{k}", [P, D]) for k in range(2)] for t in range(NT)]
        x_loaded = [sem(f"cb_x_loaded{t}") for t in range(NT)]
        y_loaded = [sem(f"cb_y_loaded{t}") for t in range(NT)]
        added = sem("cb_added")
        stored = sem("cb_stored")
        block = c.enter_context(nc.Block())
        rows = lambda d, t: d[t * P:(t + 1) * P, :]

        @block.sync
        def _(sp):
            for t in range(NT):
                sp.dma_start(xt[t][:, :], rows(x2d, t)).then_inc(x_loaded[t], 16)
            for t in range(NT):
                sp.wait_ge(added, 2 * t + 2)
                sp.dma_start(rows(out, t), xt[t][:, :]).then_inc(stored, 16)
            sp.wait_ge(stored, 16 * NT)

        @block.gpsimd
        def _(pool):
            for t in range(NT):
                for k in range(2):
                    pool.indirect_dma_start(y[t][k][:, :], None, ybd[:, :],
                                            bass.IndirectOffsetOnAxis(ap=pos[k][:, t:t + 1], axis=0)).then_inc(y_loaded[t], 16)

        @block.vector
        def _(dve):
            for t in range(NT):
                dve.wait_ge(x_loaded[t], 16)
                dve.wait_ge(y_loaded[t], 32)
                for k in range(2):
                    dve.scalar_tensor_tensor(xt[t][:, :], y[t][k][:, :], gate[k][:, t:t + 1], xt[t][:, :],
                                             ALU.mult, ALU.add).then_inc(added, 1)
                    dve.wait_ge(added, 2 * t + k + 1)


def lay_out(inputs):
    offs = np.cumsum([0, 256, 128, 128, 256, 256, 256, 4, 256, 256, 256, 256, 64, 64, 256, 64, 4, 4096])
    (a_q, a_k, a_v, f_q, f_k, f_v, f_g, s_q, s_k, s_v, d_q, d_k, d_v, i_q, i_k, i_w, gates) = offs[:-1]
    w = np.asarray(inputs["w_in"])[0]
    rows = lambda m: np.ascontiguousarray(m.reshape(-1, P, m.shape[-1]).transpose(1, 0, 2))
    zeros = lambda n: np.zeros((D, n), w.dtype)
    cols = [w[:, a_q:a_q + 384], w[:, f_q:f_q + 512], w[:, d_q:d_q + 320], zeros(64), w[:, i_q:i_q + 320],
            w[:, f_g:f_g + 4], zeros(60), w[:, s_q:s_q + 512]]
    w_qk = np.concatenate(cols, 1).reshape(KC, P, QK_CHUNKS, P).transpose(2, 1, 0, 3).reshape(QK_CHUNKS, P, KC * P)
    w_v = (np.concatenate([w[:, f_v:f_v + 256], w[:, s_v:s_v + 256], w[:, a_v:a_v + 128], w[:, d_v:d_v + 64],
                           w[:, i_w:i_w + 4], zeros(V_PAD - V_COLS)], 1).reshape(KC, P, V_PAD))
    w_gate = w[:, gates:].reshape(KC, P, 4, KC, P).transpose(3, 2, 1, 0, 4).reshape(4 * KC, P, KC * P)
    w_br = np.asarray(inputs["w_branch"])[0].reshape(4, 2, P, KC, P).transpose(3, 2, 0, 1, 4)
    g = np.asarray(inputs["qk_gain"])[0]
    gain_cols = np.ones((P, QK_CHUNKS), g.dtype)
    for m, (q, k) in enumerate(((SWA_Q, SWA_K), (FOX_Q, FOX_K), (DSA_Q, DSA_K))):
        gain_cols[:, q:q + 2] = np.tile(g[m, 0], 2)[:, None]
        gain_cols[:, k:k + 2 if m == 1 else k + 1] = np.tile(g[m, 1], 2)[:, None]
    gain_cols[:, IDX_Q:IDX_Q + 2] = SCALE
    gain_cols[:, SB_Q:SB_Q + 2] = SCALE
    onehot = np.zeros((N_BUCKETS + 1, 2, T5_LINE), g.dtype)
    for m in range(BAND + P - 1):
        dist = BAND - 1 - m
        n = max(dist, 1)
        large = 16 + int(np.log(np.float32(n) / 16) / np.log(8.0) * 16) if n >= 16 else 0
        bucket = max(dist, 0) if dist < 16 else min(large, N_BUCKETS - 1)
        onehot[N_BUCKETS if dist < 0 or dist >= P else bucket, 0, m] = 1
        onehot[N_BUCKETS if dist < 0 else bucket, 1, m] = 1
    per_chunk = lambda v: np.asarray(v).reshape(KC, P).T
    w_r = np.concatenate([np.asarray(inputs["w_router_group"])[0], np.asarray(inputs["w_router_expert"])[0],
                          zeros(P - GROUPS - EXPERTS)], 1)
    b_r = np.concatenate([np.asarray(inputs["b_router_group"])[0], np.asarray(inputs["b_router_expert"])[0]])
    arrays = {
        "x": np.asarray(inputs["x"]).reshape(NT, P, D),
        "norm_mix_g": per_chunk(inputs["norm_mix_g"][0]),
        "w_qk": w_qk, "w_v": w_v, "w_gate": w_gate, "w_br": w_br, "gain_cols": gain_cols,
        "w_out": rows(np.asarray(inputs["w_out"])[0]),
        "forget_bias": np.asarray(inputs["forget_bias"]).reshape(NH, 1),
        "attn_sinks": np.asarray(inputs["attn_sinks"]).reshape(1, NH),
        "t5_table": inputs["t5_table"], "t5_onehot": onehot, "ones": np.ones((1, T), g.dtype),
        "norm_ffn_g": np.asarray(inputs["norm_ffn_g"]).reshape(1, D),
        "w_router": rows(w_r), "b_router": b_r.reshape(1, 36),
        "w_expert_up": np.asarray(inputs["w_expert_up"])[0],
        "w_expert_down": np.asarray(inputs["w_expert_down"])[0],
    }
    return {n: np.ascontiguousarray(v) for n, v in arrays.items()}


def kernel(**inputs):
    import concourse.bacc as bacc
    from concourse.bass_utils import run_bass_kernel_spmd

    nc = bacc.Bacc("TRN2", target_bir_lowering=False, num_devices=1)
    arrays = lay_out(inputs)
    a = {n: nc.dram_tensor(f"in_{n}", v.shape, mybir.dt.from_np(v.dtype), kind="ExternalInput").ap()
         for n, v in arrays.items()}
    out = nc.dram_tensor("out_x", (T, D), F32, kind="ExternalOutput").ap()
    build(nc, a, out)
    r = run_bass_kernel_spmd(nc, [{f"in_{n}": v for n, v in arrays.items()}], core_ids=[0])
    return r.results[0]["out_x"].reshape(1, T, D)
```
